# Optimizing a Trainium2 kernel written in Bass

```python
import jax
import jax.numpy as jnp
from jax import lax
import numpy as np

D_MODEL = 2048
BATCH = 1
SEQ = 256
DEPTH = 1

D_MIX = D_MODEL
D_LRU = D_MIX // 2
D_RWKV = D_MIX - D_LRU
LRU_HEADS = 8
LRU_HEAD_DIM = D_LRU // LRU_HEADS
CONV_WIDTH = 4
LRU_C = 8.0
RWKV_HEAD_DIM = 64
RWKV_HEADS = D_RWKV // RWKV_HEAD_DIM
DECAY_LORA = 64
AAA_LORA = 64
GATE_LORA = 160
RWKV_COLS = 3 * D_RWKV + DECAY_LORA + AAA_LORA + GATE_LORA
IN_COLS = 2 * D_LRU + RWKV_COLS
PEER_HEADS = 8
PEER_NKEYS = 128
PEER_EXPERTS = PEER_NKEYS * PEER_NKEYS
PEER_DQ = 256
PEER_DHALF = PEER_DQ // 2
PEER_TOPK = 16
PEER_BLOCK = 128
NORM_EPS = 1e-6
GN_EPS = 64e-5

kernel_name = "hybrid_rglru_rwkv7_peer"

def rms_norm(x, g):
    xf = x.astype(jnp.float32)
    y = xf * lax.rsqrt(jnp.mean(xf * xf, axis=-1, keepdims=True) + NORM_EPS)
    return (y * g.astype(jnp.float32)).astype(x.dtype)

def rg_lru_group(xb, gate, conv_w, conv_b, wa, ba, wi, bi, lam):
    B, S, C = xb.shape
    xc = lax.conv_general_dilated(
        xb, conv_w.astype(xb.dtype)[:, None, :], window_strides=(1,),
        padding=((CONV_WIDTH - 1, 0),), dimension_numbers=("NWC", "WIO", "NWC"),
        feature_group_count=C) + conv_b
    xh = xc.reshape(B, S, LRU_HEADS, LRU_HEAD_DIM)
    r = jax.nn.sigmoid(jnp.einsum("bshi,hij->bshj", xh, wa).reshape(B, S, C) + ba)
    i = jax.nn.sigmoid(jnp.einsum("bshi,hij->bshj", xh, wi).reshape(B, S, C) + bi)
    log_a = -LRU_C * r.astype(jnp.float32) * jax.nn.softplus(-lam.astype(jnp.float32))
    a = jnp.exp(log_a)
    bx = jnp.sqrt(-jnp.expm1(2.0 * log_a)) * (i * xc).astype(jnp.float32)

    def combine(c1, c2):
        a1, b1 = c1
        a2, b2 = c2
        return a1 * a2, a2 * b1 + b2

    _, h = lax.associative_scan(combine, (a, bx), axis=1)
    return (h * jax.nn.gelu(gate.astype(jnp.float32))).astype(xb.dtype)

def rwkv7_group(p, mu, w0, w2, a0, a2, g2, k_k, k_a, r_k, lnx_w, lnx_b):
    B, S, _ = p.shape
    H, N = RWKV_HEADS, RWKV_HEAD_DIM
    prev = jnp.pad(p, ((0, 0), (1, 0), (0, 0)))[:, :-1]
    ps = (p + (prev - p) * mu).astype(jnp.float32)
    r, k, v, wd, ad, gd = jnp.split(
        ps, [D_RWKV, 2 * D_RWKV, 3 * D_RWKV, 3 * D_RWKV + DECAY_LORA,
             3 * D_RWKV + DECAY_LORA + AAA_LORA], axis=-1)
    w_log = -jax.nn.softplus(-(w0 + jnp.tanh(wd) @ w2)) - 0.5
    decay = jnp.exp(-jnp.exp(w_log))
    a = jax.nn.sigmoid(a0 + ad @ a2)
    g = jax.nn.sigmoid(gd) @ g2
    kk = (k * k_k).reshape(B, S, H, N)
    kk = kk / jnp.maximum(jnp.sqrt(jnp.sum(kk * kk, axis=-1, keepdims=True)), 1e-12)
    k = k * (1.0 + (a - 1.0) * k_a)
    heads = lambda t: t.reshape(B, S, H, N)
    r_h, k_h, v_h, w_h, a_h = heads(r), heads(k), heads(v), heads(decay), heads(a)
    b_h = kk * a_h

    def step(state, inp):
        r_t, w_t, k_t, v_t, na_t, b_t = inp
        sa = jnp.einsum("bhij,bhj->bhi", state, na_t)
        state = (state * w_t[:, :, None, :] + sa[..., None] * b_t[:, :, None, :]
                 + v_t[..., None] * k_t[:, :, None, :])
        return state, jnp.einsum("bhij,bhj->bhi", state, r_t)

    seq_first = lambda t: jnp.moveaxis(t, 1, 0)
    state0 = jnp.zeros((B, H, N, N), jnp.float32)
    _, y = lax.scan(step, state0, (seq_first(r_h), seq_first(w_h), seq_first(k_h),
                                   seq_first(v_h), seq_first(-kk), seq_first(b_h)))
    y = jnp.moveaxis(y, 0, 1)
    mean = jnp.mean(y, axis=-1, keepdims=True)
    var = jnp.mean(jnp.square(y - mean), axis=-1, keepdims=True)
    y = ((y - mean) * lax.rsqrt(var + GN_EPS)).reshape(B, S, D_RWKV) * lnx_w + lnx_b
    bonus = jnp.sum(r_h * k_h * r_k, axis=-1, keepdims=True) * v_h
    y = (y + bonus.reshape(B, S, D_RWKV)) * g
    return y.astype(p.dtype)

def peer_ffn(h, wq, keys, u_tab, v_tab):
    B, S, D = h.shape
    q = (h @ wq).astype(jnp.float32).reshape(B, S, PEER_HEADS, 2, PEER_DHALF)
    sub = jnp.einsum("bshpd,hpnd->bshpn", q, keys.astype(jnp.float32))
    sv, si = lax.top_k(sub, PEER_TOPK)
    cand = (sv[..., 0, :, None] + sv[..., 1, None, :]).reshape(
        B, S, PEER_HEADS, PEER_TOPK * PEER_TOPK)
    cid = (si[..., 0, :, None] * PEER_NKEYS + si[..., 1, None, :]).reshape(
        B, S, PEER_HEADS, PEER_TOPK * PEER_TOPK)
    best, pos = lax.top_k(cand, PEER_TOPK)
    experts = jnp.take_along_axis(cid, pos, axis=-1)
    gates = jax.nn.softmax(best, axis=-1)
    n_blk = (B * S) // PEER_BLOCK
    E = PEER_HEADS * PEER_TOPK
    xs = h.reshape(n_blk, PEER_BLOCK, D)
    es = experts.reshape(n_blk, PEER_BLOCK, E)
    gs = gates.reshape(n_blk, PEER_BLOCK, E).astype(h.dtype)

    def block(args):
        xb, eb, gb = args
        u = jnp.take(u_tab, eb, axis=0)
        act = jax.nn.gelu(jnp.einsum("cd,ced->ce", xb, u))
        vv = jnp.take(v_tab, eb, axis=0)
        return jnp.einsum("ce,ced->cd", gb * act, vv)

    return lax.map(block, (xs, es, gs)).reshape(B, S, D)

def hybrid_layer(x, norm1_g, w_in, conv_w, conv_b, lru_wa, lru_ba, lru_wi, lru_bi,
                 lru_lambda, rwkv_mu, rwkv_w0, rwkv_w2, rwkv_a0, rwkv_a2, rwkv_g2,
                 rwkv_k_k, rwkv_k_a, rwkv_r_k, rwkv_lnx_w, rwkv_lnx_b, w_out,
                 norm2_g, peer_wq, peer_keys, peer_u, peer_v):
    h = rms_norm(x, norm1_g)
    proj = h @ w_in
    y_lru = rg_lru_group(proj[..., :D_LRU], proj[..., D_LRU:2 * D_LRU], conv_w, conv_b,
                         lru_wa, lru_ba, lru_wi, lru_bi, lru_lambda)
    y_rwkv = rwkv7_group(proj[..., 2 * D_LRU:], rwkv_mu, rwkv_w0, rwkv_w2, rwkv_a0,
                         rwkv_a2, rwkv_g2, rwkv_k_k, rwkv_k_a, rwkv_r_k,
                         rwkv_lnx_w, rwkv_lnx_b)
    x = x + jnp.concatenate([y_lru, y_rwkv], axis=-1) @ w_out
    x = x + peer_ffn(rms_norm(x, norm2_g), peer_wq, peer_keys, peer_u, peer_v)
    return x

def setup_inputs(seed: int = 0) -> dict:
    key = jax.random.key(seed)
    ks = jax.random.split(key, 28)
    f32 = jnp.float32
    L = DEPTH

    def nrm(k, shape, std):
        return jax.random.normal(k, shape, f32) * std

    lam_u = jax.random.uniform(ks[10], (L, D_LRU), f32, 0.9, 0.999)
    lam_s = lam_u ** (1.0 / LRU_C)
    lru_lambda = jnp.log(lam_s) - jnp.log1p(-lam_s)
    ramp = jnp.linspace(0.0, 1.0, D_RWKV, dtype=f32)
    rwkv_w0 = -6.5 + 5.0 * ramp ** 0.85 + nrm(ks[12], (L, D_RWKV), 0.1)
    return {
        "x": nrm(ks[0], (BATCH, SEQ, D_MODEL), 1.0),
        "norm1_g": 1.0 + nrm(ks[1], (L, D_MODEL), 0.02),
        "w_in": nrm(ks[2], (L, D_MODEL, IN_COLS), D_MODEL ** -0.5),
        "conv_w": nrm(ks[3], (L, CONV_WIDTH, D_LRU), CONV_WIDTH ** -0.5),
        "conv_b": nrm(ks[4], (L, D_LRU), 0.02),
        "lru_wa": nrm(ks[5], (L, LRU_HEADS, LRU_HEAD_DIM, LRU_HEAD_DIM), LRU_HEAD_DIM ** -0.5),
        "lru_ba": nrm(ks[6], (L, D_LRU), 0.02),
        "lru_wi": nrm(ks[7], (L, LRU_HEADS, LRU_HEAD_DIM, LRU_HEAD_DIM), LRU_HEAD_DIM ** -0.5),
        "lru_bi": nrm(ks[8], (L, D_LRU), 0.02),
        "lru_lambda": lru_lambda,
        "rwkv_mu": jax.random.uniform(ks[11], (L, RWKV_COLS), f32),
        "rwkv_w0": rwkv_w0,
        "rwkv_w2": nrm(ks[13], (L, DECAY_LORA, D_RWKV), 0.1 * DECAY_LORA ** -0.5),
        "rwkv_a0": nrm(ks[14], (L, D_RWKV), 0.1),
        "rwkv_a2": nrm(ks[15], (L, AAA_LORA, D_RWKV), AAA_LORA ** -0.5),
        "rwkv_g2": nrm(ks[16], (L, GATE_LORA, D_RWKV), GATE_LORA ** -0.5),
        "rwkv_k_k": 0.85 + nrm(ks[17], (L, D_RWKV), 0.02),
        "rwkv_k_a": 1.0 + nrm(ks[18], (L, D_RWKV), 0.02),
        "rwkv_r_k": nrm(ks[19], (L, RWKV_HEADS, RWKV_HEAD_DIM), 0.1),
        "rwkv_lnx_w": 1.0 + nrm(ks[20], (L, D_RWKV), 0.02),
        "rwkv_lnx_b": nrm(ks[21], (L, D_RWKV), 0.02),
        "w_out": nrm(ks[22], (L, D_MIX, D_MODEL), D_MIX ** -0.5),
        "norm2_g": 1.0 + nrm(ks[23], (L, D_MODEL), 0.02),
        "peer_wq": nrm(ks[24], (L, D_MODEL, PEER_HEADS * PEER_DQ), D_MODEL ** -0.5),
        "peer_keys": nrm(ks[25], (L, PEER_HEADS, 2, PEER_NKEYS, PEER_DHALF), PEER_DHALF ** -0.5),
        "peer_u": nrm(ks[26], (L, PEER_EXPERTS, D_MODEL), D_MODEL ** -0.5),
        "peer_v": nrm(ks[27], (L, PEER_EXPERTS, D_MODEL), 0.5),
        "normf_g": 1.0 + nrm(ks[9], (D_MODEL,), 0.02),
    }

def reference(x, norm1_g, w_in, conv_w, conv_b, lru_wa, lru_ba, lru_wi, lru_bi,
              lru_lambda, rwkv_mu, rwkv_w0, rwkv_w2, rwkv_a0, rwkv_a2, rwkv_g2,
              rwkv_k_k, rwkv_k_a, rwkv_r_k, rwkv_lnx_w, rwkv_lnx_b, w_out, norm2_g,
              peer_wq, peer_keys, peer_u, peer_v, normf_g):
    for l in range(DEPTH):
        x = hybrid_layer(x, norm1_g[l], w_in[l], conv_w[l], conv_b[l], lru_wa[l],
                         lru_ba[l], lru_wi[l], lru_bi[l], lru_lambda[l], rwkv_mu[l],
                         rwkv_w0[l], rwkv_w2[l], rwkv_a0[l], rwkv_a2[l], rwkv_g2[l],
                         rwkv_k_k[l], rwkv_k_a[l], rwkv_r_k[l], rwkv_lnx_w[l],
                         rwkv_lnx_b[l], w_out[l], norm2_g[l], peer_wq[l],
                         peer_keys[l], peer_u[l], peer_v[l])
    return rms_norm(x, normf_g)


_drawn_inputs = setup_inputs


def setup_inputs(seed=0):
    import zlib

    import numpy as np

    out = dict(_drawn_inputs(seed))
    spreads = {}
    factors = {'lru_ba': 29.116,
     'lru_bi': 20.145,
     'rwkv_w2': 5.245,
     'rwkv_k_k': 9.725,
     'rwkv_lnx_w': 2.841,
     'rwkv_lnx_b': 2.955,
     'normf_g': 7.741}
    for name, (base, spread) in spreads.items():
        noise = np.random.default_rng([zlib.crc32(name.encode()), seed]).standard_normal(out[name].shape)
        drawn = base * np.exp(spread * noise) if base else spread * noise
        out[name] = jnp.asarray(drawn.astype(out[name].dtype))
    for name, factor in factors.items():
        out[name] = (out[name] * factor).astype(out[name].dtype)
    return out
```

```python
from contextlib import ExitStack

import numpy as np

import concourse.bass as bass
from concourse import mybir

F32 = mybir.dt.float32
F32R = mybir.dt.float32r
U32 = mybir.dt.uint32
BF16 = mybir.dt.bfloat16
ALU = mybir.AluOpType
ACT = mybir.ActivationFunctionType
AX_X = mybir.AxisListType.X

P = 128
SEQ = 256
NT2 = SEQ // P
D = 2048
KC = D // P
PIECE = 1024
D_LRU = 1024
CT = D_LRU // P
LORA_TILES = 3
GROUPS = 4
CHUNK = 64
NKEY = 128
HEADS = 8
TOPK = 16
EPS = 1e-6
GN_EPS = 64e-5
NEG = -3.0e38
EXPM = float(np.exp(-0.5))

COLS = {}
_at = 0
for _name, _n in (("g1", KC), ("g2", KC), ("conv_w", 4 * CT), ("conv_b", CT), ("ba", CT), ("bi", CT),
                  ("lam", CT), ("mu", 27), ("w0", CT), ("a0", CT), ("k_k", CT), ("k_a", CT),
                  ("r_k", CT), ("lnw", CT), ("lnb", CT)):
    COLS[_name] = (_at, _n)
    _at += _n
NCOL = _at

def w_in_order():
    def group(g):
        return [(kind, 2 * g + c) for kind in "rkv" for c in range(2)]
    lru = [(kind, c) for c in range(CT) for kind in ("xb", "gate")]
    order = [("lora", i) for i in range(LORA_TILES)] + group(0)
    for g in range(1, GROUPS):
        order += group(g) + lru[3 * (g - 1):3 * g]
    return order + lru[9:]


ORDER = w_in_order()
N_IN = len(ORDER)
N_OUT = KC
N_Q = KC
N_U = NKEY
N_V = NKEY
T_OUT = N_IN
T_Q = T_OUT + N_OUT
T_U = T_Q + N_Q
T_V = T_U + N_U
N_MASK = 11
N_G = SEQ // 4
U_FIRST = 96
U_EXP = 72
SHIFTED = [t for t, (kind, _) in enumerate(ORDER) if kind in ("lora", "r", "k", "v")]
MU = {t: {"r": 0, "k": CT, "v": 2 * CT, "lora": 3 * CT}[ORDER[t][0]] + ORDER[t][1] for t in SHIFTED}
MARKS = [range(9, 18), range(18, 27), range(27, 36), range(36, N_IN)]

RWKV_JOBS = ["zw", "za", "gate", "ss", "bsum", "vt", "bt", "kt",
             "m1_0", "m2_0", "m1_2", "m2_2", "m3_0", "m1_1", "m2_1", "m1_3", "m2_3", "m3_1"]
for _lv in range(1, 6):
    RWKV_JOBS += [f"y{_lv}_0", f"y{_lv}_1"]
    for _half in range(2):
        RWKV_JOBS += [f"{_kind}{_lv}_{_half}" for _kind in (("t", "tt") if _lv < 5 else ("tt",))]
for _c in range(4):
    RWKV_JOBS += [f"{_kind}{_c}" for _kind in ("r", "sa", "st", "yc") if (_kind, _c) != ("st", 3)]
RWKV_JOBS += ["yt", "mean", "var"]


def psum_plan():
    names = [("x1", i, i % 8) for i in range(8)]
    ring = 0
    for t in range(9):
        names.append(("tile", t, t % 2))
    for g in range(GROUPS):
        for t in MARKS[g]:
            names.append(("tile", t, t % 2))
        for job in RWKV_JOBS:
            names.append((job, g, 2 + ring % 6))
            ring += 1
    for c in range(CT):
        for kind in ("lr", "li"):
            names.append((kind, c, 2 + ring % 6))
            ring += 1
    names += [("out", i, i) for i in range(8)]
    names += [("x2", i, i) for i in range(8)]
    for t in range(N_Q):
        names.append(("tile", T_Q + t, (T_Q + t) % 2))
        names.append(("sub", t, 2 + t % 4))
    for t in range(N_U):
        names.append(("tile", T_U + t, (T_U + t) % 2))
    for i in range(6):
        names.append(("idx", i, 2 + i))
    for i in range(SEQ // 4):
        names.append(("gm", i, 2 + i % 4))
    names += [("peer", i, i) for i in range(8)]
    uses, plan = [0] * 8, {}
    for name, i, bank in names:
        plan[name, i] = (bank, uses[bank])
        uses[bank] += 1
    return plan


PLAN = psum_plan()


def full_counts():
    counts, out = [0] * 8, {}
    for (name, i), (bank, _) in PLAN.items():
        if name not in ("tile", "out", "peer"):
            counts[bank] += 1
            out[name, i] = counts[bank]
    return out


FULLS = full_counts()


def hybrid_layer_kernel(nc, a, out):
    ctx = ExitStack()
    with ctx:
        sems = {}

        def sem(name):
            if name not in sems:
                sems[name] = ctx.enter_context(nc.semaphore(name))
            return sems[name]

        base = [16512]

        def at(name, shape, dt, offset):
            return nc.alloc_sbuf_tensor_at(name, shape, dt, offset=offset)

        def place(name, shape, dt=F32):
            size = 4 * int(np.prod(shape[1:]))
            t = at(name, shape, dt, base[0])
            base[0] += (size + 31) // 32 * 32
            return t

        raw = [place(f"raw{i}", [P, PIECE]) for i in range(4)]
        hi = [place(f"hi{i}", [P, PIECE], F32R) for i in range(4)]
        lo = [place(f"lo{i}", [P, PIECE], F32R) for i in range(2)]
        hT_at = base[0]
        hT_hi = place("hT_hi", [P, KC, SEQ], F32R)
        hT_lo = place("hT_lo", [P, KC, SEQ], F32R)
        cols = place("cols", [P, NCOL])
        ident = place("ident", [P, P])
        iota = place("iota", [P, P])
        scal = place("scal", [P, 64])
        idx_at = base[0]
        idxT = place("idxT", [P, 3, SEQ])
        xpad = at("xpad", [P, SEQ + 3], F32, idx_at + 1024)
        mshift = [place(f"mshift{i}", [P, 1 + SEQ]) for i in range(2)]
        ARENA = (base[0] + 31) // 32 * 32
        ARENA_F = 32768
        end = ARENA + 4 * ARENA_F
        identb = at("identb", [P, P], BF16, end)
        assert end + 256 <= nc.sbuf_usable_end, (end, nc.sbuf_usable_end)

        def ar(name, first, shape, dt=F32):
            assert first + int(np.prod(shape[1:])) <= ARENA_F, name
            return at(name, shape, dt, ARENA + 4 * first)

        actg = ar("actg", 0, [P, NKEY, SEQ])

        f = [0]

        def nx(name, shape, dt=F32):
            t = ar(name, f[0], shape, dt)
            f[0] += int(np.prod(shape[1:]))
            return t

        masks = nx("masks", [P, N_MASK, P])
        blk, blk64, mU, m0, m0T = masks[:, 0], masks[:, 1], masks[:, 2:4], masks[:, 4], masks[:, 5]
        d1scan = nx("d1scan", [P, 8 * 65])
        wa2 = nx("wa2", [P, D_LRU])
        g2 = nx("g2", [P, 2, D_LRU])
        wai = nx("wai", [P, 2, CT, P])
        xc = nx("xc", [P, CT, SEQ])
        gate = nx("gate", [P, CT, SEQ])
        yR_hi = nx("yR_hi", [P, CT, SEQ], F32R)
        yR_lo = nx("yR_lo", [P, CT, SEQ], F32R)
        rkv = [nx(f"rkv{i}", [P, 3, 2, SEQ]) for i in range(2)]
        lora = nx("lora", [P, 3, SEQ])
        group_at = f[0]
        w65 = nx("w65", [P, 8, 65])
        aT = nx("aT", [P, 2, SEQ])
        inv_at = f[0]
        iP = nx("iP", [P, 2, SEQ])
        kk = nx("kk", [P, 2, SEQ])
        k2 = nx("k2", [P, 2, SEQ])
        bb = nx("bb", [P, 2, SEQ])
        sq = nx("sq", [P, 2, SEQ])
        gT = nx("gT", [P, 2, SEQ])
        P65 = nx("P65", [P, 8, 65])
        ARt = nx("ARt", [P, 2, 2, SEQ])
        ym_at = f[0]
        bt = nx("bt", [P, 2, SEQ])
        kt = nx("kt", [P, 2, SEQ])
        rk = nx("rk", [P, 2, SEQ])
        bon = nx("bon", [P, 2, SEQ])
        Vt = nx("Vt", [P, 2, NT2, P])
        Bt = nx("Bt", [P, 2, NT2, P])
        Kt = nx("Kt", [P, 2, NT2, P])
        L1 = nx("L1", [P, 8, 2, P])
        L2 = nx("L2", [P, 8, 2, P])
        ST1 = nx("ST1", [P, 2, P])
        Tm = ar("Tm", inv_at, [P, 8, P])
        TT = ar("TT", inv_at + 1024, [P, 8, P])
        Ym = ar("Ym", ym_at, [P, 8, P])
        Rm = ar("Rm", group_at, [P, 4, 64])
        SA = ar("SA", group_at + 256, [P, NT2, 4, 64])
        ST = [ar("ST0", group_at + 768, [P, 2, P]), ST1]
        y_tm = ar("y_tm", inv_at, [P, NT2, 2, P])
        yT = ar("yT", inv_at + 512, [P, 2, SEQ])
        gn_d = ar("gn_d", inv_at + 1024, [P, 2, SEQ])
        gn_s = ar("gn_s", inv_at + 1536, [P, 2, SEQ])
        x_sb = ar("x_sb", group_at, [P, NT2, D])
        h0 = ar("h0", group_at + 4096, [P, NT2, D])
        h_tmp = ar("h_tmp", group_at + 8192, [P, 2, 512])
        yL_hi = ar("yL_hi", group_at, [P, CT, SEQ], F32R)
        yL_lo = ar("yL_lo", group_at + 2048, [P, CT, SEQ], F32R)
        lr = ar("lr", group_at + 4096, [P, CT, SEQ])
        li = ar("li", group_at + 6144, [P, CT, SEQ])
        la = ar("la", group_at + 8192, [P, CT, SEQ])
        lt = ar("lt", group_at + 10240, [P, CT, SEQ])
        x2 = ar("x2", 0, [P, NT2, D])
        h2 = ar("h2", 4096, [P, NT2, D])
        h2_tmp = ar("h2_tmp", 8192, [P, 2, 512])
        keysT = ar("keysT", 20480, [P, 2 * HEADS, NKEY])
        TK = U_FIRST * SEQ
        qT = [ar(f"qT{i}", TK + i * SEQ, [P, SEQ]) for i in range(2)]
        tk_s = ar("tk_s", TK + 512, [P, P])
        tk_cand = ar("tk_cand", TK + 640, [P, TOPK, TOPK])
        tk_cand2 = ar("tk_cand2", TK + 896, [P, TOPK * TOPK])
        tk_sv = ar("tk_sv", TK + 1152, [P, 2, TOPK])
        tk_si = ar("tk_si", TK + 1184, [P, 2, TOPK], U32)
        tk_pos = ar("tk_pos", TK + 1216, [P, TOPK], U32)
        tk_ab = ar("tk_ab", TK + 1232, [P, 2, TOPK], U32)
        sif = ar("sif", TK + 1280, [P, NT2, 2, HEADS, TOPK])
        abf = ar("abf", TK + 1792, [P, NT2, 2, HEADS, TOPK])
        best = ar("best", TK + 2304, [P, NT2, HEADS, TOPK])
        sel = ar("sel", TK + 2560, [P, NT2, 3, HEADS * TOPK])
        sm = ar("sm", TK + 3328, [P, NT2, HEADS])
        sub = ar("sub", TK + 4096, [P, NT2, 2 * HEADS, P])
        oneh = ar("oneh", TK + 4096, [P, HEADS * TOPK, TOPK])
        oneB = [at(f"oneB{i}", [P, 4, P], F32, hT_at + 2048 * i) for i in range(2)]
        oneA = [at(f"oneA{i}", [P, 4, P], F32, hT_at + 4096 + 2048 * i) for i in range(2)]
        a_hi = [at(f"a_hi{i}", [P, SEQ], F32R, hT_at + 8192 + 1024 * i) for i in range(2)]
        a_lo = [at(f"a_lo{i}", [P, SEQ], F32R, hT_at + 10240 + 1024 * i) for i in range(2)]
        xr = ar("xr", 0, [P, NT2, D])
        gf = ar("gf", 4096, [P, D])
        junk = ar("junk", 6144, [P, D])

        ps = ctx.enter_context(nc.psum_tensor("ps", [P, 8, 512], F32))
        x2_dram = nc.dram_tensor("x2_spill", (P, NT2 * D), F32, kind="Internal").ap()

        full = [sem(f"bank_full{i}") for i in range(8)]
        free = [sem(f"bank_free{i}") for i in range(8)]
        raw_in = [sem(f"raw_in{i}") for i in range(4)]
        hi_done, lo_done, mm_done = sem("hi_done"), sem("lo_done"), sem("mm_done")
        block = ctx.enter_context(nc.Block())

        def col(name, i=0, n=1):
            first = COLS[name][0] + i
            return cols[:, first:first + n]

        def colr(name):
            return col(name, 0, COLS[name][1])

        rs, ssq, sd = scal[:, 0:2], scal[:, 2:4], scal[:, 4:6]
        hw0, ha0, hba, hbi, nsp = (scal[:, 6 + 8 * i:14 + 8 * i] for i in range(5))
        eps_c, gneps_c, mc2 = scal[:, 46:47], scal[:, 47:48], scal[:, 48:49]
        omu, oka, psp = idxT[:, 0, 0:27], idxT[:, 0, 32:40], idxT[:, 0, 40:48]
        sp = [idxT[:, 0, 48 + 8 * i:56 + 8 * i] for i in range(7)]

        def bank(name, i):
            return ps[:, PLAN[name, i][0]]

        def freed(name, i):
            return free[PLAN[name, i][0]]

        def wait_full(eng, name, i):
            b, n = PLAN[name, i]
            if name == "tile":
                eng.wait_ge(mm_done, 2 * i + 2)
            else:
                eng.wait_ge(full[b], FULLS[name, i])

        def wait_free(eng, name, i):
            b, n = PLAN[name, i]
            if n:
                eng.wait_ge(free[b], n)

        def wait_read(eng, name, i):
            b, n = PLAN[name, i]
            eng.wait_ge(free[b], n + 1)

        def dest(t):
            kind, c = ORDER[t]
            if kind == "lora":
                return lora[:, c]
            return rkv[(c // 2) % 2][:, "rkv".index(kind), c % 2]

        @block.sync
        def _(sync):
            xv = a["x"].rearrange("o (t p) d -> p (o t) d", p=P)
            sync.dma_start(x_sb[:, :, :], xv).then_inc(sem("x_in"), 16)
            sync.dma_start(cols[:, :], a["cols"]).then_inc(sem("cols_in"), 16)
            sync.dma_start(ident[:, :], a["consts"][:, 0:P]).then_inc(sem("ident_in"), 16)
            sync.dma_start(iota[:, :], a["consts"][:, P:2 * P]).then_inc(sem("iota_in"), 16)

            def load(n, src):
                if n >= 4:
                    sync.wait_ge(lo_done, n - 3)
                sync.dma_start(raw[n % 4][:, :], src).then_inc(raw_in[n % 4], 16)

            for n in range(2 * N_IN):
                load(n, a["w_in"][n // 2, n % 2])
                if n == 3:
                    m_end = (2 + N_MASK) * P
                    sync.dma_start(masks[:, :, :], a["consts"][:, 2 * P:m_end].rearrange(
                        "p (m q) -> p m q", q=P)).then_inc(sem("masks_in"), 16)
                    sync.dma_start(d1scan[:, :], a["consts"][:, m_end:m_end + 520]).then_inc(
                        sem("scan_in"), 16)
                    sync.dma_start(wa2[0:64, :], a["w2"]).then_inc(sem("w2_in"), 16)
                    sync.dma_start(wa2[64:128, :], a["a2"]).then_inc(sem("a2_in"), 16)
                    sync.dma_start(g2[:, :, :], a["g2"].rearrange("(k p) c -> p k c", p=P)).then_inc(
                        sem("g2_in"), 16)
                    sync.dma_start(wai[:, 0], a["lru_wa"].rearrange("h i j -> i h j")).then_inc(
                        sem("wa_in"), 16)
                    sync.dma_start(wai[:, 1], a["lru_wi"].rearrange("h i j -> i h j")).then_inc(
                        sem("wi_in"), 16)
            for c in range(N_OUT):
                ch = (c + CT) % KC
                for half in range(2):
                    load(2 * (T_OUT + c) + half,
                         a["w_out"][ch * P:(ch + 1) * P, half * PIECE:(half + 1) * PIECE])
                if c == 0:
                    sync.wait_ge(sem("yR_lo"), GROUPS)
                    sync.dma_start(x2[:, :, :], xv).then_inc(sem("x2_in"), 16)
            for t in range(N_Q):
                for half in range(2):
                    load(2 * (T_Q + t) + half, a["wq"][t, half])
                if t == 0:
                    sync.wait_ge(sem("x2_done"), 8)
                    sync.dma_start(keysT[:, :, :], a["keys"]).then_inc(sem("keys_in"), 16)
                    sync.dma_start(x2_dram, x2[:, :, :].rearrange("p t d -> p (t d)")).then_inc(
                        sem("x2_out"), 16)
            with sync.Fori(0, N_U // 2) as it:
                for q in range(4):
                    n = 2 * T_U + q
                    sync.wait_ge(lo_done, it * 4 + (n - 3))
                    sync.dma_start(raw[n % 4][:, :], a["peer_u"][it * 2 + q // 2, q % 2]).then_inc(
                        raw_in[n % 4], 16)
            with sync.Fori(0, N_V // 2) as it:
                for q in range(4):
                    n = 2 * T_V + q
                    sync.wait_ge(lo_done, it * 4 + (n - 3))
                    sync.dma_start(raw[n % 4][:, :], a["peer_v"][
                        it * 2 + q // 2, :, (q % 2) * PIECE:(q % 2 + 1) * PIECE]).then_inc(
                        raw_in[n % 4], 16)
            sync.wait_ge(sem("alo_done"), N_V)
            sync.wait_ge(sem("x2_out"), 16)
            sync.dma_start(xr[:, :, :].rearrange("p t d -> p (t d)"), x2_dram).then_inc(sem("xr_in"), 16)
            sync.dma_start(gf[:, :], a["normf_g"].partition_broadcast(P)).then_inc(sem("gf_in"), 16)
            outv = out.rearrange("o (t p) d -> p (o t) d", p=P)
            for t in range(NT2):
                sync.wait_ge(sem("y_done"), t + 1)
                sync.dma_start(outv[:, t], xr[:, t]).then_inc(sem("out_sent"), 16)
            sync.wait_ge(sem("out_sent"), 16 * NT2)

        @block.scalar
        def _(act):
            def mark(ins, name, value):
                ins.then_inc(sem(name), 1)
                act.wait_ge(sem(name), value)

            def hi_piece(n):
                act.wait_ge(raw_in[n % 4], 16 * (n // 4 + 1))
                if n >= 4:
                    act.wait_ge(mm_done, n - 3)
                nc.scalar.activation(hi[n % 4][:, :], raw[n % 4][:, :], ACT.Copy).then_inc(hi_done, 1)

            def norm_root(i):
                act.wait_ge(sem("ssq_done"), 2 * i + 2)
                nc.scalar.activation(sd, ssq, ACT.Sqrt, scale=1.0 / D, bias=eps_c).then_inc(
                    sem("sd_done"), 1)

            def turned_hi(name, tmp):
                for j in range(8):
                    act.wait_ge(sem(f"{name}_tmp"), j + 1)
                    nc.scalar.activation(hT_hi[:, 2 * j:2 * j + 2, :].rearrange("p c t -> p (c t)"),
                                         tmp[:, j % 2], ACT.Copy).then_inc(sem(f"{name}_hi"), 1)

            act.wait_ge(sem("consts_done"), 1)
            norm_root(0)
            act.wait_ge(sem("lam_abs"), 1)
            nc.scalar.activation(sp[1], sp[0], ACT.Exp, scale=-1.0).then_inc(sem("lam_exp"), 1)
            act.wait_ge(sem("lam_u"), 1)
            nc.scalar.activation(sp[3], sp[2], ACT.Ln).then_inc(sem("lam_ln"), 1)
            turned_hi("h1", h_tmp)

            def result(t):
                kind, c = ORDER[t]
                wait_full(act, "tile", t)
                pb = bank("tile", t)[:, 0:SEQ]
                if kind == "xb":
                    if c:
                        act.wait_ge(sem("conv_done"), c)
                    nc.scalar.activation(xpad[:, 3:3 + SEQ], pb, ACT.Copy).then_inc(freed("tile", t), 1)
                elif kind == "gate":
                    nc.scalar.activation(gate[:, c], pb, ACT.Copy).then_inc(freed("tile", t), 1)
                else:
                    q = SHIFTED.index(t)
                    if q >= 2:
                        wait_read(act, "tile", SHIFTED[q - 2])
                    nc.scalar.activation(mshift[q % 2][:, 1:1 + SEQ], pb, ACT.Copy,
                                         scale=col("mu", MU[t])).then_inc(sem("mu_done"), 1)

            def tile(t):
                hi_piece(2 * t)
                hi_piece(2 * t + 1)
                if t:
                    result(t - 1)

            for t in range(9):
                tile(t)
                if t == 3:
                    wait_read(act, "tile", 2)
                    nc.scalar.activation(lora[0:64, 0], lora[0:64, 0], ACT.Tanh).then_inc(
                        sem("lora_act"), 1)
                    nc.scalar.activation(lora[:, 1:3], lora[:, 1:3], ACT.Tanh, scale=0.5).then_inc(
                        sem("lora_act"), 1)
            for g in range(GROUPS):
                marks = list(MARKS[g])

                def m():
                    if marks:
                        tile(marks.pop(0))

                m()
                act.wait_ge(sem("w65_ready"), g + 1)
                wait_full(act, "zw", g)
                for c in range(2):
                    ins = nc.scalar.activation(aT[:, c], bank("zw", g)[:, c * SEQ:(c + 1) * SEQ],
                                               ACT.Tanh, scale=0.5, bias=hw0[:, 2 * g + c:2 * g + c + 1])
                ins.then_inc(freed("zw", g), 1)
                wait_read(act, "zw", g)
                mark(nc.scalar.activation(
                    w65[:, :, 1:65], aT[:, :, :].rearrange("p c (k t) -> p (c k) t", t=CHUNK),
                    ACT.Exp, scale=-0.5 * EXPM, bias=mc2), "w_done", g + 1)
                wait_full(act, "za", g)
                for c in range(2):
                    ins = nc.scalar.activation(aT[:, c], bank("za", g)[:, c * SEQ:(c + 1) * SEQ],
                                               ACT.Tanh, scale=0.5, bias=ha0[:, 2 * g + c:2 * g + c + 1])
                ins.then_inc(freed("za", g), 1)
                wait_full(act, "gate", g)
                nc.scalar.activation(gT[:, :, :].rearrange("p c t -> p (c t)"), bank("gate", g),
                                     ACT.Copy).then_inc(freed("gate", g), 1)
                m()
                wait_full(act, "ss", g)
                nc.scalar.activation(sq[:, :, :].rearrange("p c t -> p (c t)"), bank("ss", g),
                                     ACT.Sqrt).then_inc(freed("ss", g), 1)
                m()
                for name, dst in (("vt", Vt), ("bt", Bt), ("kt", Kt)):
                    wait_full(act, name, g)
                    nc.scalar.activation(dst[:, :, :, :].rearrange("p c k t -> p (c k t)"),
                                         bank(name, g), ACT.Copy).then_inc(freed(name, g), 1)
                m()
                for lv in range(1, 6):
                    for half in range(2):
                        for name, dst in (("t", Tm), ("tt", TT)):
                            job = f"{name}{lv}_{half}"
                            if (job, g) not in PLAN:
                                continue
                            wait_full(act, job, g)
                            nc.scalar.activation(
                                dst[:, 4 * half:4 * half + 4].rearrange("p a b -> p (a b)"),
                                bank(job, g), ACT.Copy).then_inc(freed(job, g), 1)
                m()
                for c in range(4):
                    rows = slice(64 * (c % 2), 64 * (c % 2) + 64)
                    wait_full(act, f"r{c}", g)
                    act.wait_ge(sem("chain_zero"), g + 1)
                    nc.scalar.activation(Rm[rows, :, :].rearrange("p a b -> p (a b)"),
                                         bank(f"r{c}", g)[rows, 0:256], ACT.Copy).then_inc(
                        freed(f"r{c}", g), 1)
                    wait_full(act, f"yc{c}", g)
                    nc.scalar.activation(y_tm[rows, c // 2].rearrange("p a b -> p (a b)"),
                                         bank(f"yc{c}", g)[rows, 0:256], ACT.Copy).then_inc(
                        freed(f"yc{c}", g), 1)
                    m()
                wait_full(act, "var", g)
                nc.scalar.activation(gn_s[:, :, :].rearrange("p c t -> p (c t)"), bank("var", g),
                                     ACT.Sqrt, bias=gneps_c).then_inc(freed("var", g), 1)
                act.wait_ge(sem("y_f32"), g + 1)
                nc.scalar.activation(yR_hi[:, 2 * g:2 * g + 2, :], yT[:, :, :], ACT.Copy).then_inc(
                    sem("yR_hi"), 1)
                assert not marks
            result(N_IN - 1)

            hi_piece(2 * T_OUT)
            hi_piece(2 * T_OUT + 1)
            act.wait_ge(sem("yR_lo"), GROUPS)
            for c in range(CT):
                wait_full(act, "lr", c)
                nc.scalar.activation(lr[:, c], bank("lr", c)[:, 0:SEQ], ACT.Tanh, scale=0.5,
                                     bias=hba[:, c:c + 1]).then_inc(freed("lr", c), 1)
                wait_full(act, "li", c)
                nc.scalar.activation(li[:, c], bank("li", c)[:, 0:SEQ], ACT.Tanh, scale=0.5,
                                     bias=hbi[:, c:c + 1]).then_inc(freed("li", c), 1)
            act.wait_ge(sem("lr_sig"), 1)
            for c in range(CT):
                nc.scalar.activation(la[:, c], lr[:, c], ACT.Exp, scale=nsp[:, c:c + 1])
                ins = nc.scalar.activation(lt[:, c], lr[:, c], ACT.Tanh, scale=psp[:, c:c + 1])
            ins.then_inc(sem("la_lt_done"), 1)
            hi_piece(2 * T_OUT + 2)
            hi_piece(2 * T_OUT + 3)
            act.wait_ge(sem("om_done"), 1)
            nc.scalar.activation(lt[:, :, :], lt[:, :, :], ACT.Sqrt).then_inc(sem("om_root"), 1)
            hi_piece(2 * T_OUT + 4)
            hi_piece(2 * T_OUT + 5)
            nc.scalar.activation(gate[:, :, :], gate[:, :, :], ACT.Gelu_apprx_tanh).then_inc(
                sem("gelu_done"), 1)
            hi_piece(2 * T_OUT + 6)
            hi_piece(2 * T_OUT + 7)
            act.wait_ge(sem("yL_f32"), 1)
            nc.scalar.activation(yL_hi[:, :, :], lt[:, :, :], ACT.Copy).then_inc(sem("yL_hi"), 1)
            for n in range(2 * T_OUT + 8, 2 * T_Q):
                hi_piece(n)
            norm_root(1)
            turned_hi("h2", h2_tmp)

            def scores_out(t):
                wait_full(act, "sub", t)
                nc.scalar.activation(sub[:, :, t, :], bank("sub", t)[:, 0:2 * P].rearrange(
                    "p (a b) -> p a b", a=2), ACT.Copy).then_inc(freed("sub", t), 1)

            for t in range(N_Q):
                hi_piece(2 * (T_Q + t))
                hi_piece(2 * (T_Q + t) + 1)
                if t >= 2:
                    scores_out(t - 2)
                wait_full(act, "tile", T_Q + t)
                nc.scalar.activation(qT[t % 2][:, :], bank("tile", T_Q + t)[:, 0:SEQ], ACT.Copy).then_inc(
                    freed("tile", T_Q + t), 1)
            scores_out(N_Q - 2)
            scores_out(N_Q - 1)
            act.wait_ge(sem("x2_out"), 16)

            def u_hi(it, q):
                n = 2 * T_U + q
                act.wait_ge(raw_in[n % 4], it * 16 + 16 * (n // 4 + 1))
                act.wait_ge(mm_done, it * 4 + (n - 3))
                nc.scalar.activation(hi[n % 4][:, :], raw[n % 4][:, :], ACT.Copy).then_inc(hi_done, 1)

            def u_gelu(it, b):
                t = T_U + b
                act.wait_ge(mm_done, it * 4 + 2 * (t + 1))
                pb = ps[:, t % 2, 0:SEQ]
                nc.scalar.activation(actg[:, bass.ds(it * 2 + b, 1), :].rearrange("p a b -> p (a b)"), pb,
                                     ACT.Gelu_apprx_tanh).then_inc(free[t % 2], 1)

            def u_body(it, first=False):
                u_hi(it, 0)
                u_hi(it, 1)
                if not first:
                    u_gelu(it, -1)
                u_hi(it, 2)
                u_hi(it, 3)
                u_gelu(it, 0)

            u_body(0, True)
            with act.Fori(1, U_EXP // 2) as it:
                u_body(it)
            act.wait_ge(sem("best_sub"), 1)
            nc.scalar.activation(best[:, :, :, :], best[:, :, :, :], ACT.Exp).then_inc(
                sem("best_exp"), 1)
            with act.Fori(U_EXP // 2, U_FIRST // 2) as it:
                u_body(it)
            for i in range(6):
                wait_full(act, "idx", i)
                nc.scalar.activation(idxT[:, i // 2, (i % 2) * P:(i % 2 + 1) * P],
                                     bank("idx", i)[:, 0:P], ACT.Copy).then_inc(freed("idx", i), 1)
            with act.Fori(U_FIRST // 2, N_U // 2) as it:
                u_body(it)
            act.wait_ge(mm_done, 2 * T_V)
            nc.scalar.activation(actg[:, N_U - 1, :], ps[:, (T_V - 1) % 2, 0:SEQ],
                                 ACT.Gelu_apprx_tanh).then_inc(free[(T_V - 1) % 2], 1)

            act.wait_ge(sem("gated"), N_G)

            def v_body(it, first=False):
                for b in range(2):
                    n = 2 * (T_V + b)
                    if not first:
                        act.wait_ge(mm_done, it * 4 + (n - 2))
                    nc.scalar.activation(a_hi[b][:, :], actg[:, bass.ds(it * 2 + b, 1), :].rearrange(
                        "p a b -> p (a b)"), ACT.Copy).then_inc(sem("ahi_done"), 1)
                    for q in range(2):
                        act.wait_ge(raw_in[(n + q) % 4], it * 16 + 16 * ((n + q) // 4 + 1))
                        act.wait_ge(mm_done, it * 4 + (n + q - 3))
                        nc.scalar.activation(hi[(n + q) % 4][:, :], raw[(n + q) % 4][:, :],
                                             ACT.Copy).then_inc(hi_done, 1)

            v_body(0, True)
            with act.Fori(1, N_V // 2) as it:
                v_body(it)
            for t in range(NT2):
                act.wait_ge(sem("ssq_done"), 4 + t + 1)
                nc.scalar.activation(sd[:, t:t + 1], ssq[:, t:t + 1], ACT.Sqrt, scale=1.0 / D,
                                     bias=eps_c).then_inc(sem("sd_done"), 1)

        @block.vector
        def _(dve):
            chain = [0]
            V = nc.vector

            def link(ins):
                chain[0] += 1
                ins.then_inc(sem("dve_chain"), 1)
                dve.wait_ge(sem("dve_chain"), chain[0])

            def mark(ins, name, value):
                ins.then_inc(sem(name), 1)
                dve.wait_ge(sem(name), value)

            def out_of(ins, name, i):
                ins.then_inc(freed(name, i), 1)
                wait_read(dve, name, i)

            def lo_piece(n):
                dve.wait_ge(hi_done, n + 1)
                if n >= 2:
                    dve.wait_ge(mm_done, n - 1)
                V.tensor_tensor(lo[n % 2][:, :], raw[n % 4][:, :], hi[n % 4][:, :].bitcast(F32),
                                ALU.subtract).then_inc(lo_done, 1)

            def ts(o, i, s1, s2, op0, op1=None):
                return V.tensor_scalar(o, i, s1, s2, op0, op1) if op1 is not None else \
                    V.tensor_scalar(o, i, s1, None, op0)

            def stt(o, i0, s, i1, op0, op1):
                return V.scalar_tensor_tensor(out=o, in0=i0, scalar=s, in1=i1, op0=op0, op1=op1)

            def normalise(i, x, h):
                for t in range(NT2):
                    mark(V.tensor_tensor_reduce(out=h[:, t], in0=x[:, t], in1=x[:, t], scale=1.0,
                                                scalar=0.0, op0=ALU.mult, op1=ALU.add,
                                                accum_out=ssq[:, t:t + 1]), "ssq_done", 2 * i + t + 1)
                dve.wait_ge(sem("sd_done"), i + 1)
                link(V.reciprocal(rs, sd))
                for t in range(NT2):
                    link(ts(h[:, t], x[:, t], rs[:, t:t + 1], None, ALU.mult))
                dve.sem_inc(sem("rows_done"), 1)

            def turned_lo(i, name, job, tmp, gain):
                for j in range(9):
                    if j < 8:
                        wait_full(dve, job, j)
                        g_b = col(gain, 2 * j, 2).unsqueeze(2).broadcast_to([P, 2, SEQ])
                        V.tensor_tensor(tmp[:, j % 2].rearrange("p (c t) -> p c t", c=2),
                                        bank(job, j).rearrange("p (c t) -> p c t", c=2), g_b,
                                        ALU.mult).then_inc(sem(f"{name}_tmp"), 1)
                    if j:
                        q = j - 1
                        dve.wait_ge(sem(f"{name}_tmp"), q + 1)
                        dve.wait_ge(sem(f"{name}_hi"), q + 1)
                        V.tensor_tensor(hT_lo[:, 2 * q:2 * q + 2, :].rearrange("p c t -> p (c t)"),
                                        tmp[:, q % 2], hT_hi[:, 2 * q:2 * q + 2, :].bitcast(F32).rearrange(
                                            "p c t -> p (c t)"), ALU.subtract).then_inc(freed(job, q), 1)
                        wait_read(dve, job, q)
                dve.sem_inc(sem("hT_done"), 1)

            V.memset(eps_c, EPS)
            V.memset(gneps_c, GN_EPS)
            for i in range(2):
                V.memset(mshift[i][:, 0:1], 0.0)
            V.memset(xpad[:, 0:3], 0.0)
            mark(V.memset(mc2, -0.5 * EXPM), "consts_done", 1)
            dve.wait_ge(sem("x_in"), 16)
            normalise(0, x_sb, h0)
            dve.wait_ge(sem("cols_in"), 16)
            for dst, name in ((hw0, "w0"), (ha0, "a0"), (hba, "ba"), (hbi, "bi")):
                ts(dst, colr(name), 0.5, None, ALU.mult)
            ts(omu, colr("mu"), -1.0, 1.0, ALU.mult, ALU.add)
            link(ts(oka, colr("k_a"), -1.0, 1.0, ALU.mult, ALU.add))
            link(ts(sp[5], colr("lam"), -1.0, None, ALU.mult))
            mark(V.tensor_tensor(sp[0], colr("lam"), sp[5], ALU.max), "lam_abs", 1)
            dve.wait_ge(sem("lam_exp"), 1)
            mark(ts(sp[2], sp[1], 1.0, None, ALU.add), "lam_u", 1)
            link(ts(sp[4], sp[2], -1.0, None, ALU.add))
            link(V.tensor_tensor(sp[4], sp[1], sp[4], ALU.subtract))
            link(V.reciprocal(sp[6], sp[2]))
            link(V.tensor_tensor(sp[4], sp[4], sp[6], ALU.mult))
            dve.wait_ge(sem("lam_ln"), 1)
            link(V.tensor_tensor(sp[4], sp[4], sp[3], ALU.add))
            link(stt(sp[4], sp[5], 0.0, sp[4], ALU.max, ALU.add))
            link(ts(psp, sp[4], 8.0, None, ALU.mult))
            link(ts(nsp, sp[4], -8.0, None, ALU.mult))
            dve.wait_ge(sem("ident_in"), 16)
            mark(V.tensor_copy(identb[:, :], ident[:, :]), "identb_done", 1)
            turned_lo(0, "h1", "x1", h_tmp, "g1")

            def result(t):
                kind, c = ORDER[t]
                if kind == "xb":
                    wait_read(dve, "tile", t)
                    link(ts(xc[:, c], xpad[:, 3:3 + SEQ], col("conv_w", 3 * CT + c), col("conv_b", c),
                            ALU.mult, ALU.add))
                    link(stt(xc[:, c], xpad[:, 2:2 + SEQ], col("conv_w", 2 * CT + c), xc[:, c],
                             ALU.mult, ALU.add))
                    link(stt(xc[:, c], xpad[:, 1:1 + SEQ], col("conv_w", CT + c), xc[:, c],
                             ALU.mult, ALU.add))
                    mark(stt(xc[:, c], xpad[:, 0:SEQ], col("conv_w", c), xc[:, c],
                             ALU.mult, ALU.add), "conv_done", c + 1)
                elif kind != "gate":
                    q = SHIFTED.index(t)
                    dve.wait_ge(sem("mu_done"), q + 1)
                    out_of(stt(dest(t), bank("tile", t)[:, 0:SEQ], omu[:, MU[t]:MU[t] + 1],
                               mshift[q % 2][:, 0:SEQ], ALU.mult, ALU.add), "tile", t)

            def tile(t):
                lo_piece(2 * t)
                lo_piece(2 * t + 1)
                if t:
                    result(t - 1)

            for t in range(9):
                tile(t)
                if t == 4:
                    dve.wait_ge(sem("lora_act"), 2)
                    mark(ts(lora[:, 1:3], lora[:, 1:3], 0.5, 0.5, ALU.mult, ALU.add), "lora_done", 1)
            dve.wait_ge(sem("masks_in"), 16)
            dve.wait_ge(sem("scan_in"), 16)
            for g in range(GROUPS):
                marks = list(MARKS[g])

                def m():
                    if marks:
                        tile(marks.pop(0))

                def cg(name, c):
                    return col(name, 2 * g + c)

                R, K, Vv = (rkv[g % 2][:, i] for i in range(3))
                m()
                mark(V.memset(w65[:, :, 0:1], 0.0), "w65_ready", g + 1)
                for c in range(2):
                    link(ts(kk[:, c], K[:, c], cg("k_k", c), None, ALU.mult))
                mark(V.tensor_tensor(sq[:, :, :], kk[:, :, :], kk[:, :, :], ALU.mult), "sq_done", g + 1)
                m()
                dve.wait_ge(sem("w_done"), g + 1)
                link(V.tensor_tensor_scan(P65[:, :, :].rearrange("p a b -> p (a b)"),
                                          w65[:, :, :].rearrange("p a b -> p (a b)"), d1scan[:, :],
                                          0.0, ALU.mult, ALU.add))
                link(V.reciprocal(iP[:, :, :].rearrange("p c (k t) -> p (c k) t", t=CHUNK),
                                  P65[:, :, 1:65]))
                wait_read(dve, "za", g)
                link(ts(aT[:, :, :], aT[:, :, :], 0.5, 0.5, ALU.mult, ALU.add))
                for c in range(2):
                    link(ts(k2[:, c], aT[:, c], cg("k_a", c), oka[:, 2 * g + c:2 * g + c + 1],
                            ALU.mult, ALU.add))
                link(V.tensor_tensor(k2[:, :, :], k2[:, :, :], K, ALU.mult))
                V.tensor_tensor(kt[:, :, :], k2[:, :, :], iP[:, :, :], ALU.mult)
                for c in range(2):
                    ins = stt(rk[:, c], R[:, c], cg("r_k", c), k2[:, c], ALU.mult, ALU.mult)
                mark(ins, "rk_done", g + 1)
                wait_read(dve, "ss", g)
                link(ts(sq[:, :, :], sq[:, :, :], 1e-12, None, ALU.max))
                link(V.reciprocal(sq[:, :, :], sq[:, :, :]))
                link(V.tensor_tensor(kk[:, :, :], kk[:, :, :], sq[:, :, :], ALU.mult))
                link(V.tensor_tensor(bb[:, :, :], kk[:, :, :], aT[:, :, :], ALU.mult))
                mark(V.tensor_tensor(bt[:, :, :], bb[:, :, :], iP[:, :, :], ALU.mult), "bk_done", g + 1)
                link(stt(ARt[:, 0].rearrange("p c (k t) -> p (c k) t", t=CHUNK),
                         kk[:, :, :].rearrange("p c (k t) -> p (c k) t", t=CHUNK), -1.0,
                         P65[:, :, 0:64], ALU.mult, ALU.mult))
                mark(V.tensor_tensor(ARt[:, 1].rearrange("p c (k t) -> p (c k) t", t=CHUNK),
                                     R.rearrange("p c (k t) -> p (c k) t", t=CHUNK),
                                     P65[:, :, 1:65], ALU.mult), "ar_done", g + 1)
                V.memset(Rm[:, :, :], 0.0)
                V.memset(SA[:, :, :, :], 0.0)
                mark(V.memset(ST[0][:, :, :], 0.0), "chain_zero", g + 1)
                m()
                wait_full(dve, "bsum", g)
                out_of(V.tensor_tensor(bon[:, :, :].rearrange("p c t -> p (c t)"), bank("bsum", g),
                                       Vv.rearrange("p c t -> p (c t)"), ALU.mult), "bsum", g)

                def mask_b(mask, n):
                    return mask.unsqueeze(1).broadcast_to([P, n, P])

                def masked(job, dst):
                    pb = bank(job, g).rearrange("p (t w q) -> p t w q", t=2, w=2)
                    return V.tensor_tensor(dst, pb, mU.unsqueeze(1).broadcast_to([P, 2, 2, P]), ALU.mult)

                for half in range(2):
                    for hl in (half, half + 2):
                        wait_full(dve, f"m1_{hl}", g)
                        V.tensor_tensor(TT[:, 2 * hl:2 * hl + 2, :], bank(f"m1_{hl}", g).rearrange(
                            "p (t w q) -> p t w q", t=2, w=2)[:, :, 0], mask_b(m0T, 2), ALU.mult)
                        out_of(masked(f"m1_{hl}", L1[:, 2 * hl:2 * hl + 2]), f"m1_{hl}", g)
                        wait_full(dve, f"m2_{hl}", g)
                        out_of(masked(f"m2_{hl}", L2[:, 2 * hl:2 * hl + 2]), f"m2_{hl}", g)
                    wait_full(dve, f"m3_{half}", g)
                    out_of(V.tensor_tensor(
                        Tm[:, :, :].rearrange("p (c h t) q -> p c h (t q)", c=2, h=2)[:, :, half].rearrange(
                            "p c (t q) -> p c t q", t=2),
                        bank(f"m3_{half}", g).rearrange("p (c t q) -> p c t q", c=2, t=2),
                        m0.unsqueeze(1).unsqueeze(1).broadcast_to([P, 2, 2, P]), ALU.mult),
                        f"m3_{half}", g)
                V.tensor_tensor(TT[:, :, :], TT[:, :, :], mask_b(ident[:, :], 8), ALU.add)
                mark(V.tensor_tensor(Tm[:, :, :], Tm[:, :, :], mask_b(ident[:, :], 8), ALU.add),
                     "first_inverse", g + 1)
                m()
                for lv in range(1, 6):
                    for half in range(2):
                        job = f"y{lv}_{half}"
                        wait_full(dve, job, g)
                        out_of(V.tensor_tensor(Ym[:, 4 * half:4 * half + 4],
                                               bank(job, g).rearrange("p (a q) -> p a q", a=4),
                                               mask_b(masks[:, 5 + lv], 4), ALU.mult), job, g)
                m()
                for c in range(4):
                    rows = slice(64 * (c % 2), 64 * (c % 2) + 64)
                    if c < 3:
                        pcm = sq[:, c % 2].rearrange("p (c q) -> p c q", c=2)
                        for ct in range(2):
                            k = 4 * ct + c
                            link(ts(pcm[:, ct], blk, P65[:, k, 64:65], None, ALU.mult))
                    wait_full(dve, f"sa{c}", g)
                    out_of(V.tensor_copy(SA[rows, c // 2].rearrange("p a b -> p (a b)"),
                                         bank(f"sa{c}", g)[rows, 0:256]), f"sa{c}", g)
                    if c < 3:
                        wait_full(dve, f"st{c}", g)
                        out_of(V.tensor_tensor(ST[(c + 1) % 2][:, :, :],
                                               bank(f"st{c}", g)[:, 0:256].rearrange(
                                                   "p (c q) -> p c q", c=2), pcm, ALU.mult),
                               f"st{c}", g)
                    m()
                wait_full(dve, "yt", g)
                out_of(V.tensor_copy(yT[:, :, :].rearrange("p c t -> p (c t)"), bank("yt", g)), "yt", g)
                wait_full(dve, "mean", g)
                out_of(V.tensor_tensor(gn_d[:, :, :].rearrange("p c t -> p (c t)"),
                                       yT[:, :, :].rearrange("p c t -> p (c t)"), bank("mean", g),
                                       ALU.subtract), "mean", g)
                mark(V.tensor_tensor(sq[:, :, :], gn_d[:, :, :], gn_d[:, :, :], ALU.mult),
                     "dsq_done", g + 1)
                wait_read(dve, "var", g)
                link(V.reciprocal(gn_s[:, :, :], gn_s[:, :, :]))
                link(V.tensor_tensor(gn_d[:, :, :], gn_d[:, :, :], gn_s[:, :, :], ALU.mult))
                for c in range(2):
                    link(ts(yT[:, c], gn_d[:, c], cg("lnw", c), cg("lnb", c), ALU.mult, ALU.add))
                link(V.tensor_tensor(yT[:, :, :], yT[:, :, :], bon[:, :, :], ALU.add))
                mark(V.tensor_tensor(yT[:, :, :], yT[:, :, :], gT[:, :, :], ALU.mult), "y_f32", g + 1)
                dve.wait_ge(sem("yR_hi"), g + 1)
                mark(V.tensor_tensor(yR_lo[:, 2 * g:2 * g + 2, :], yT[:, :, :],
                                     yR_hi[:, 2 * g:2 * g + 2, :].bitcast(F32), ALU.subtract),
                     "yR_lo", g + 1)
            result(N_IN - 1)

            lo_piece(2 * T_OUT)
            lo_piece(2 * T_OUT + 1)
            wait_read(dve, "lr", CT - 1)
            mark(ts(lr[:, :, :], lr[:, :, :], 0.5, 0.5, ALU.mult, ALU.add), "lr_sig", 1)
            wait_read(dve, "li", CT - 1)
            link(ts(li[:, :, :], li[:, :, :], 0.5, 0.5, ALU.mult, ALU.add))
            link(V.tensor_tensor(li[:, :, :], li[:, :, :], xc[:, :, :], ALU.mult))
            lo_piece(2 * T_OUT + 2)
            dve.wait_ge(sem("la_lt_done"), 1)
            link(V.tensor_tensor(lr[:, :, :], la[:, :, :], la[:, :, :], ALU.mult))
            mark(stt(lt[:, :, :], lr[:, :, :], 1.0, lt[:, :, :], ALU.add, ALU.mult), "om_done", 1)
            lo_piece(2 * T_OUT + 3)
            dve.wait_ge(sem("om_root"), 1)
            link(V.tensor_tensor(li[:, :, :], li[:, :, :], lt[:, :, :], ALU.mult))
            lo_piece(2 * T_OUT + 4)
            lo_piece(2 * T_OUT + 5)
            for c in range(CT):
                link(V.tensor_tensor_scan(lr[:, c], la[:, c], li[:, c], 0.0, ALU.mult, ALU.add))
            lo_piece(2 * T_OUT + 6)
            lo_piece(2 * T_OUT + 7)
            dve.wait_ge(sem("gelu_done"), 1)
            mark(V.tensor_tensor(lt[:, :, :], lr[:, :, :], gate[:, :, :], ALU.mult), "yL_f32", 1)
            dve.wait_ge(sem("yL_hi"), 1)
            mark(V.tensor_tensor(yL_lo[:, :, :], lt[:, :, :], yL_hi[:, :, :].bitcast(F32),
                                 ALU.subtract), "yL_lo", 1)
            for n in range(2 * T_OUT + 8, 2 * T_Q):
                lo_piece(n)
            dve.wait_ge(sem("x2_in"), 16)
            dve.wait_ge(mm_done, 2 * T_Q)
            for i in range(8):
                xs = x2[:, i // 4, (i % 4) * 512:(i % 4 + 1) * 512]
                V.tensor_tensor(xs, xs, bank("out", i), ALU.add).then_inc(freed("out", i), 1)
                wait_read(dve, "out", i)
                dve.sem_inc(sem("x2_done"), 1)
            normalise(1, x2, h2)
            turned_lo(1, "h2", "x2", h2_tmp, "g2")
            for n in range(2 * T_Q, 2 * T_U):
                lo_piece(n)

            def top16(vals, idx, src, tmp):
                return [lambda: (link(V.max(vals[:, 0:8], src)),
                                 link(V.max_index(idx[:, 0:8], vals[:, 0:8], src))),
                        lambda: (link(V.match_replace(tmp, vals[:, 0:8], src, NEG)),
                                 link(V.max(vals[:, 8:16], tmp)),
                                 link(V.max_index(idx[:, 8:16], vals[:, 8:16], tmp)))]

            def head_steps(h, t):
                steps = []
                for p in range(2):
                    steps += top16(tk_sv[:, p], tk_si[:, p], sub[:, t, 2 * h + p, :], tk_s[:, :])

                def sums():
                    link(V.tensor_copy(sif[:, t, :, h, :], tk_si[:, :, :]))
                    link(V.tensor_tensor(
                        tk_cand[:, :, :], tk_sv[:, 0].unsqueeze(2).broadcast_to([P, TOPK, TOPK]),
                        tk_sv[:, 1].unsqueeze(1).broadcast_to([P, TOPK, TOPK]), ALU.add))

                def places():
                    link(ts(tk_ab[:, 0], tk_pos[:, :], 4, None, ALU.logical_shift_right))
                    link(ts(tk_ab[:, 1], tk_pos[:, :], 15, None, ALU.bitwise_and))
                    link(V.tensor_copy(abf[:, t, :, h, :], tk_ab[:, :, :]))

                steps.append(sums)
                steps += top16(best[:, t, h], tk_pos, tk_cand[:, :, :].rearrange("p a b -> p (a b)"),
                               tk_cand2[:, :])
                steps.append(places)
                return steps

            for t in range(NT2):
                for h in range(HEADS):
                    if h == 0 and t == 0:
                        for i in range(4):
                            wait_read(dve, "sub", N_Q - 4 + i)
                    for q, step in enumerate(head_steps(h, t)):
                        lo_piece(2 * T_U + 8 * (t * HEADS + h) + q)
                        step()

            def subtract_max():
                V.tensor_tensor(best[:, :, :, :], best[:, :, :, :],
                                best_max.broadcast_to([P, NT2, HEADS, TOPK]),
                                ALU.subtract).then_inc(sem("best_sub"), 1)

            steps = []
            for t in range(NT2):
                steps.append(lambda t=t: link(V.tensor_copy(sm[:, t], best[:, t, :, 0])))
                steps.append(lambda t=t: link(V.tensor_tensor(
                    best[:, t], best[:, t], sm[:, t].unsqueeze(2).broadcast_to([P, HEADS, TOPK]),
                    ALU.subtract)))
            steps.append(lambda: dve.sem_inc(sem("best_sub"), 1))
            for t in range(NT2):
                for p in range(2):
                    def one_hot(t=t, p=p):
                        link(V.tensor_tensor(
                            oneh[:, :, :],
                            abf[:, t, p].rearrange("p h k -> p (h k)").unsqueeze(2).broadcast_to(
                                [P, HEADS * TOPK, TOPK]),
                            iota[:, 0:TOPK].unsqueeze(1).broadcast_to([P, HEADS * TOPK, TOPK]),
                            ALU.is_equal))

                    def keys(t=t, p=p):
                        o4 = oneh[:, :, :].rearrange("p (h k) a -> p h k a", h=HEADS)
                        link(V.tensor_tensor(
                            o4, o4, sif[:, t, p].unsqueeze(2).broadcast_to([P, HEADS, TOPK, TOPK]),
                            ALU.mult))

                    def total(t=t, p=p):
                        link(V.tensor_reduce(sel[:, t, p], oneh[:, :, :], AX_X, ALU.add))

                    steps += [one_hot, keys, total]

            def softmax():
                dve.wait_ge(sem("best_exp"), 1)
                for t in range(NT2):
                    link(V.tensor_reduce(sm[:, t], best[:, t], AX_X, ALU.add))
                    link(V.reciprocal(sm[:, t], sm[:, t]))
                    link(V.tensor_tensor(
                        sel[:, t, 2].rearrange("p (h k) -> p h k", h=HEADS), best[:, t],
                        sm[:, t].unsqueeze(2).broadcast_to([P, HEADS, TOPK]), ALU.mult))
                dve.sem_inc(sem("sel_done"), 1)

            dve.wait_ge(sem("iota_in"), 16)
            first = 2 * T_U + 128
            last = 2 * (T_U + U_FIRST)
            for q in range(last - first):
                lo_piece(first + q)
                if q % 3 == 0 and q // 3 < len(steps):
                    steps[q // 3]()
                if q == last - first - 6:
                    softmax()
            assert (last - first - 6) // 3 >= len(steps)

            with dve.Fori(U_FIRST // 2, N_U // 2) as it:
                for q in range(4):
                    n = 2 * T_U + q
                    dve.wait_ge(hi_done, it * 4 + (n + 1))
                    dve.wait_ge(mm_done, it * 4 + (n - 1))
                    V.tensor_tensor(lo[n % 2][:, :], raw[n % 4][:, :], hi[n % 4][:, :].bitcast(F32),
                                    ALU.subtract).then_inc(lo_done, 1)

            for i in range(6):
                wait_read(dve, "idx", i)
            dve.wait_ge(free[(T_V - 1) % 2], PLAN["tile", T_V - 1][1] + 1)
            dve.wait_ge(free[(T_V - 2) % 2], PLAN["tile", T_V - 2][1] + 1)

            def one_a(it, q):
                b2, n2 = PLAN["gm", (q - 2) % 4]
                dve.wait_ge(full[b2], it + (FULLS["gm", (q - 2) % 4] - (1 if q < 2 else 0)))
                for k in range(4):
                    tok = it * 16 + (4 * q + k)
                    V.tensor_scalar(oneB[q % 2][:, k], iota[:, :], idxT[:, 1, bass.ds(tok, 1)], None,
                                    ALU.is_equal)
                    ins = V.tensor_scalar(oneA[q % 2][:, k], iota[:, :], idxT[:, 0, bass.ds(tok, 1)],
                                          idxT[:, 2, bass.ds(tok, 1)], ALU.is_equal, ALU.mult)
                ins.then_inc(sem("onehots_made"), 1)

            def gated(it, q):
                b, n = PLAN["gm", q % 4]
                dve.wait_ge(full[b], it + (FULLS["gm", q % 4] - (1 if q < 0 else 0)))
                v = actg[:, :, bass.ds(it * 16 + 4 * q, 4)].rearrange("p i t -> p t i")
                V.tensor_tensor(v, v, ps[:, b].rearrange("p (t i) -> p t i", t=4),
                                ALU.mult).then_inc(free[b], 1)

            def g_body(it, first=False):
                for q in range(4):
                    one_a(it, q)
                    if not (first and q == 0):
                        gated(it, q - 1)

            g_body(0, True)
            with dve.Fori(1, N_G // 4) as it:
                g_body(it)
            gated(N_G // 4, -1)
            for b in range(4):
                wait_read(dve, "gm", N_G - 4 + b)
            dve.sem_inc(sem("gated"), N_G)

            def v_body(it, first=False):
                for b in range(2):
                    n = 2 * (T_V + b)
                    dve.wait_ge(sem("ahi_done"), it * 2 + (b + 1))
                    V.tensor_tensor(a_lo[b][:, :], actg[:, bass.ds(it * 2 + b, 1), :].rearrange(
                        "p a b -> p (a b)"), a_hi[b][:, :].bitcast(F32), ALU.subtract).then_inc(
                        sem("alo_done"), 1)
                    for q in range(2):
                        dve.wait_ge(hi_done, it * 4 + (n + q + 1))
                        dve.wait_ge(mm_done, it * 4 + (n + q - 1))
                        V.tensor_tensor(lo[(n + q) % 2][:, :], raw[(n + q) % 4][:, :],
                                        hi[(n + q) % 4][:, :].bitcast(F32), ALU.subtract).then_inc(
                            lo_done, 1)

            with dve.Fori(0, N_V // 2) as it:
                v_body(it)

            dve.wait_ge(sem("xr_in"), 16)
            dve.wait_ge(sem("gf_in"), 16)
            dve.wait_ge(mm_done, 2 * (T_V + N_V))
            for t in range(NT2):
                for j in range(4):
                    xs = xr[:, t, j * 512:(j + 1) * 512]
                    link(V.tensor_tensor(xs, xs, bank("peer", 4 * t + j), ALU.add))
                V.tensor_tensor_reduce(out=junk[:, :], in0=xr[:, t], in1=xr[:, t], scale=1.0,
                                       scalar=0.0, op0=ALU.mult, op1=ALU.add,
                                       accum_out=ssq[:, t:t + 1]).then_inc(sem("ssq_done"), 1)
                dve.wait_ge(sem("ssq_done"), 4 + t + 1)
            for t in range(NT2):
                dve.wait_ge(sem("sd_done"), 2 + t + 1)
                link(V.reciprocal(rs[:, t:t + 1], sd[:, t:t + 1]))
                stt(xr[:, t], xr[:, t], rs[:, t:t + 1], gf[:, :], ALU.mult, ALU.mult).then_inc(
                    sem("y_done"), 1)

        @block.tensor
        def _(pe):
            def mm(o, lhsT, rhs, start, stop):
                return nc.tensor.matmul(o, lhsT, rhs, start=start, stop=stop, skip_group_check=True)

            def project(n, o):
                half = n % 2
                for k in range(8):
                    kc = 8 * half + k
                    wh, wl = (w[:, k * P:(k + 1) * P] for w in (hi[n % 4], lo[n % 2]))
                    mm(o, wh, hT_hi[:, kc], half == 0 and k == 0, False)
                    mm(o, wh, hT_lo[:, kc], False, False)
                    ins = mm(o, wl, hT_hi[:, kc], False, half == 1 and k == 7)
                ins.then_inc(mm_done, 1)

            def tile(t):
                wait_free(pe, "tile", t)
                for n in (2 * t, 2 * t + 1):
                    pe.wait_ge(lo_done, n + 1)
                    project(n, bank("tile", t)[:, 0:SEQ])

            def rows_out(n, act_hi, act_lo, banks, start, stop):
                for t in range(NT2):
                    ah, al = (x[:, t * P:(t + 1) * P] for x in (act_hi, act_lo))
                    for w, lhsT, s, e in ((hi[n % 4], ah, start, False), (lo[n % 2], ah, False, False),
                                          (hi[n % 4], al, False, stop)):
                        for j in range(2):
                            ins = mm(banks(4 * t + 2 * (n % 2) + j), lhsT,
                                     w[:, j * 512:(j + 1) * 512], s, e)
                ins.then_inc(mm_done, 1)

            def turn(job, rows):
                for j in range(8):
                    wait_free(pe, job, j)
                    for c in range(2):
                        for t in range(NT2):
                            kc = 2 * j + c
                            ins = nc.tensor.transpose(
                                bank(job, j)[:, c * SEQ + t * P:c * SEQ + (t + 1) * P],
                                rows[:, t, kc * P:(kc + 1) * P], ident[:, :])
                    ins.then_inc(full[PLAN[job, j][0]], 1)

            pe.wait_ge(sem("ident_in"), 16)
            pe.wait_ge(sem("rows_done"), 1)
            turn("x1", h0)
            pe.wait_ge(sem("hT_done"), 1)
            for t in range(9):
                tile(t)
            for name in ("masks_in", "w2_in", "a2_in", "g2_in"):
                pe.wait_ge(sem(name), 16)
            pe.wait_ge(sem("identb_done"), 1)
            pe.wait_ge(sem("lora_done"), 1)
            for g in range(GROUPS):
                marks = list(MARKS[g])

                def m():
                    if marks:
                        tile(marks.pop(0))

                def job(name):
                    wait_free(pe, name, g)
                    return bank(name, g)

                def done(ins, name):
                    ins.then_inc(full[PLAN[name, g][0]], 1)

                def chans(c):
                    return slice((2 * g + c) * P, (2 * g + c + 1) * P)

                vv = rkv[g % 2][:, 2]
                m()
                o = job("zw")
                for c in range(2):
                    ins = mm(o[:, c * SEQ:(c + 1) * SEQ], wa2[0:64, chans(c)], lora[0:64, 0],
                             c == 0, c == 1)
                done(ins, "zw")
                o = job("za")
                for c in range(2):
                    ins = mm(o[:, c * SEQ:(c + 1) * SEQ], wa2[64:128, chans(c)], lora[64:128, 0],
                             c == 0, c == 1)
                done(ins, "za")
                o = job("gate")
                for c in range(2):
                    for k in range(2):
                        ins = mm(o[:, c * SEQ:(c + 1) * SEQ], g2[:, k, chans(c)], lora[:, 1 + k],
                                 c == 0 and k == 0, c == 1 and k == 1)
                done(ins, "gate")
                m()
                o = job("ss")
                pe.wait_ge(sem("sq_done"), g + 1)
                done(mm(o, blk, sq[:, :, :].rearrange("p c t -> p (c t)"), True, True), "ss")
                m()
                o = job("bsum")
                pe.wait_ge(sem("rk_done"), g + 1)
                done(mm(o, blk, rk[:, :, :].rearrange("p c t -> p (c t)"), True, True), "bsum")
                for name, src in (("vt", vv), ("bt", bt), ("kt", kt)):
                    o = job(name)
                    if name == "bt":
                        pe.wait_ge(sem("bk_done"), g + 1)
                    for c in range(2):
                        for t in range(NT2):
                            q = 2 * c + t
                            ins = nc.tensor.transpose(o[:, q * P:(q + 1) * P],
                                                      src[:, c, t * P:(t + 1) * P], ident[:, :])
                    done(ins, name)
                pe.wait_ge(sem("ar_done"), g + 1)

                def add_identity(o4):
                    return mm(o4, identb[:, :], identb[:, :].unsqueeze(1).broadcast_to(
                        [P, o4.shape[1], P]), True, False)

                def scores(name, hl, src):
                    hp, c = slice(64 * (hl % 2), 64 * (hl % 2) + 64), hl // 2
                    o = job(name)
                    for t in range(NT2):
                        tok = slice(t * P, (t + 1) * P)
                        ins = mm(o[:, t * SEQ:(t + 1) * SEQ].rearrange("p (w q) -> p w q", w=2),
                                 src[hp, c, tok], ARt[hp, :, c, tok], t == 0, t == 1)
                    done(ins, name)

                for par in range(2):
                    for hl in (par, par + 2):
                        scores(f"m1_{hl}", hl, bt)
                        scores(f"m2_{hl}", hl, kt)
                    o = job(f"m3_{par}")
                    hp = slice(64 * par, 64 * par + 64)
                    for c in range(2):
                        for t in range(NT2):
                            tok = slice(t * P, (t + 1) * P)
                            q = 2 * c + t
                            ins = mm(o[:, q * P:(q + 1) * P], ARt[hp, 0, c, tok], bt[hp, c, tok],
                                     q == 0, q == 3)
                    done(ins, f"m3_{par}")
                m()
                pe.wait_ge(sem("first_inverse"), g + 1)
                for lv in range(1, 6):
                    for half in range(2):
                        o = job(f"y{lv}_{half}")
                        if lv > 1:
                            wait_read(pe, f"t{lv - 1}_{half}", g)
                        add_identity(o.rearrange("p (a q) -> p a q", a=4))
                        for q in range(4):
                            p = 4 * half + q
                            ins = mm(o[:, q * P:(q + 1) * P], L1[:, p, 0], Tm[:, p], False, q == 3)
                        done(ins, f"y{lv}_{half}")
                    for half in range(2):
                        wait_read(pe, f"y{lv}_{half}", g)
                        if lv > 1:
                            wait_read(pe, f"tt{lv - 1}_{half}", g)
                        if lv < 5:
                            o = job(f"t{lv}_{half}")
                            for q in range(4):
                                p = 4 * half + q
                                ins = mm(o[:, q * P:(q + 1) * P], TT[:, p], Ym[:, p], q == 0, q == 3)
                            done(ins, f"t{lv}_{half}")
                        o = job(f"tt{lv}_{half}")
                        for q in range(4):
                            p = 4 * half + q
                            ins = mm(o[:, q * P:(q + 1) * P], Ym[:, p], TT[:, p], q == 0, q == 3)
                        done(ins, f"tt{lv}_{half}")
                m()
                pe.wait_ge(sem("chain_zero"), g + 1)
                for name in ("vt", "bt", "kt", "tt5_0", "tt5_1"):
                    wait_read(pe, name, g)
                for c in range(4):
                    rows, t = slice(64 * (c % 2), 64 * (c % 2) + 64), c // 2
                    tok = slice(t * P, (t + 1) * P)
                    o = job(f"r{c}")
                    if c:
                        wait_read(pe, f"st{c - 1}", g)
                    for ct in range(2):
                        mm(o[:, ct * P:(ct + 1) * P], ARt[:, 0, ct, tok], ST[c % 2][:, ct], ct == 0, False)
                    for hl in range(4):
                        ins = mm(o[:, 64 * hl:64 * hl + 64], L2[:, 2 * hl + t, 0],
                                 Vt[:, hl // 2, t, 64 * (hl % 2):64 * (hl % 2) + 64], False, hl == 3)
                    done(ins, f"r{c}")
                    o = job(f"sa{c}")
                    wait_read(pe, f"r{c}", g)
                    for hl in range(4):
                        ins = mm(o[:, 64 * hl:64 * hl + 64], TT[:, 2 * hl + t], Rm[:, hl],
                                 hl == 0, hl == 3)
                    done(ins, f"sa{c}")
                    if c < 3:
                        o = job(f"st{c}")
                        mm(o[:, 0:256], ident[:, :], ST[c % 2][:, :, :].rearrange("p c q -> p (c q)"),
                           True, False)
                        wait_read(pe, f"sa{c}", g)
                        for ct in range(2):
                            mm(o[:, ct * P:(ct + 1) * P], Kt[rows, ct, t], Vt[rows, ct, t], False, False)
                            ins = mm(o[:, ct * P:(ct + 1) * P], Bt[rows, ct, t],
                                     SA[rows, t, 2 * ct:2 * ct + 2].rearrange("p a b -> p (a b)"),
                                     False, ct == 1)
                        done(ins, f"st{c}")
                    o = job(f"yc{c}")
                    if c == 3:
                        wait_read(pe, f"sa{c}", g)
                    for ct in range(2):
                        mm(o[:, ct * P:(ct + 1) * P], ARt[:, 1, ct, tok], ST[c % 2][:, ct], ct == 0, False)
                    for hl in range(4):
                        cols_h = slice(64 * hl, 64 * hl + 64)
                        mm(o[:, cols_h], L2[:, 2 * hl + t, 1],
                           Vt[:, hl // 2, t, 64 * (hl % 2):64 * (hl % 2) + 64], False, False)
                        ins = mm(o[:, cols_h], L1[:, 2 * hl + t, 1], SA[:, t, hl], False, hl == 3)
                    done(ins, f"yc{c}")
                    m()
                o = job("yt")
                for c in range(4):
                    wait_read(pe, f"yc{c}", g)
                for c in range(2):
                    for t in range(NT2):
                        q = 2 * c + t
                        ins = nc.tensor.transpose(o[:, q * P:(q + 1) * P], y_tm[:, t, c], ident[:, :])
                done(ins, "yt")
                o = job("mean")
                wait_read(pe, "yt", g)
                done(mm(o, blk64, yT[:, :, :].rearrange("p c t -> p (c t)"), True, True), "mean")
                o = job("var")
                pe.wait_ge(sem("dsq_done"), g + 1)
                done(mm(o, blk64, sq[:, :, :].rearrange("p c t -> p (c t)"), True, True), "var")

            pe.wait_ge(sem("wa_in"), 16)
            pe.wait_ge(sem("wi_in"), 16)
            pe.wait_ge(sem("conv_done"), CT)
            for c in range(CT):
                for q, name in enumerate(("lr", "li")):
                    wait_free(pe, name, c)
                    mm(bank(name, c)[:, 0:SEQ], wai[:, q, c], xc[:, c], True, True).then_inc(
                        full[PLAN[name, c][0]], 1)

            for i in range(8):
                wait_free(pe, "out", i)
            pe.wait_ge(sem("yR_lo"), GROUPS)
            for c in range(N_OUT):
                yh, yl = (yR_hi, yR_lo) if c < CT else (yL_hi, yL_lo)
                if c == CT:
                    pe.wait_ge(sem("yL_lo"), 1)
                for half in range(2):
                    n = 2 * (T_OUT + c) + half
                    pe.wait_ge(lo_done, n + 1)
                    rows_out(n, yh[:, c % CT], yl[:, c % CT], lambda i: bank("out", i),
                             c == 0, c == N_OUT - 1)
            pe.wait_ge(sem("rows_done"), 2)
            turn("x2", h2)
            pe.wait_ge(sem("hT_done"), 2)

            pe.wait_ge(sem("keys_in"), 16)

            def key_scores(t):
                wait_free(pe, "sub", t)
                wait_read(pe, "tile", T_Q + t)
                for tt in range(NT2):
                    ins = mm(bank("sub", t)[:, tt * P:(tt + 1) * P], qT[t % 2][:, tt * P:(tt + 1) * P],
                             keysT[:, t], tt == 0, tt == 1)
                ins.then_inc(full[PLAN["sub", t][0]], 1)

            for t in range(N_Q):
                tile(T_Q + t)
                if t:
                    key_scores(t - 1)
            key_scores(N_Q - 1)

            def u_body(it):
                for b in range(2):
                    t = T_U + b
                    pe.wait_ge(free[t % 2], it + PLAN["tile", t][1])
                    for q in range(2):
                        n = 2 * t + q
                        pe.wait_ge(lo_done, it * 4 + (n + 1))
                        project(n, ps[:, t % 2, 0:SEQ])

            with pe.Fori(0, U_FIRST // 2) as it:
                u_body(it)
            pe.wait_ge(sem("sel_done"), 1)
            for i in range(6):
                wait_free(pe, "idx", i)
                nc.tensor.transpose(bank("idx", i)[:, 0:P], sel[:, i % 2, i // 2], ident[:, :]).then_inc(
                    full[PLAN["idx", i][0]], 1)
            with pe.Fori(U_FIRST // 2, N_U // 2) as it:
                u_body(it)

            with pe.Fori(0, N_G // 4) as it:
                for q in range(4):
                    b, n = PLAN["gm", q]
                    pe.wait_ge(free[b], it + n)
                    pe.wait_ge(sem("onehots_made"), it * 4 + (q + 1))
                    for k in range(4):
                        ins = mm(ps[:, b, k * P:(k + 1) * P], oneB[q % 2][:, k], oneA[q % 2][:, k],
                                 k == 0, k == 3)
                    ins.then_inc(full[b], 1)

            for b in range(8):
                wait_free(pe, "peer", b)

            def v_body(it, start=False, stop=False):
                for b in range(2):
                    pe.wait_ge(sem("alo_done"), it * 2 + (b + 1))
                    for q in range(2):
                        n = 2 * (T_V + b) + q
                        pe.wait_ge(lo_done, it * 4 + (n + 1))
                        rows_out(n, a_hi[b], a_lo[b], lambda i: ps[:, i], start and b == 0,
                                 stop and b == 1)

            v_body(0, start=True)
            with pe.Fori(1, N_V // 2 - 1) as it:
                v_body(it)
            v_body(N_V // 2 - 1, stop=True)


def _consts():
    t, s = np.arange(P)[:, None], np.arange(P)[None, :]
    eye = np.eye(P)
    same = (t // CHUNK) == (s // CHUNK)

    def pairs(lv):
        return ((t >> (lv + 1)) == (s >> (lv + 1))) & ((t >> lv) % 2 == 1) & ((s >> lv) % 2 == 0)

    blk = ((t // 64) == (s // 64)).astype(np.float32)
    masks = [blk, blk / 64, same & (t < s), same & (t <= s), pairs(0), pairs(0).T]
    masks += [pairs(lv) + eye for lv in range(1, 6)]
    assert len(masks) == N_MASK
    reset = np.zeros((P, 8, 65))
    reset[:, :, 0] = 1
    parts = [eye, np.broadcast_to(s, (P, P))] + masks + [reset.reshape(P, -1)]
    return np.ascontiguousarray(np.concatenate([np.asarray(q, np.float32) for q in parts], 1))


def _tiles(w):
    n = w.shape[1] // P
    return np.ascontiguousarray(w.reshape(2, 8, P, n, P).transpose(3, 0, 2, 1, 4)).reshape(
        n, 2, P, PIECE)


def _columns(v):
    v = np.asarray(v).reshape(-1)
    full_v = np.zeros((-(-v.size // P)) * P, v.dtype)
    full_v[:v.size] = v
    return full_v.reshape(-1, P).T


def kernel(**inputs):
    import concourse.bacc as _bacc
    from concourse import mybir as _mybir
    from concourse.bass_utils import run_bass_kernel_spmd as _run

    i = {k: np.asarray(v) for k, v in inputs.items()}
    w_in = i["w_in"][0]
    starts = {"xb": 0, "gate": D_LRU, "r": 2 * D_LRU, "k": 3 * D_LRU, "v": 4 * D_LRU, "lora": 5 * D_LRU}
    padded = np.zeros((D, N_IN * P), w_in.dtype)
    for t, (kind, c) in enumerate(ORDER):
        first = starts[kind] + c * P
        part = w_in[:, first:first + P]
        padded[:, t * P:t * P + part.shape[1]] = part
    g2 = np.zeros((2 * P, D_LRU), w_in.dtype)
    g2[:i["rwkv_g2"].shape[1]] = i["rwkv_g2"][0]
    source = {"g1": "norm1_g", "g2": "norm2_g", "conv_w": "conv_w", "conv_b": "conv_b", "ba": "lru_ba",
              "bi": "lru_bi", "lam": "lru_lambda", "mu": "rwkv_mu", "w0": "rwkv_w0", "a0": "rwkv_a0",
              "k_k": "rwkv_k_k", "k_a": "rwkv_k_a", "r_k": "rwkv_r_k", "lnw": "rwkv_lnx_w",
              "lnb": "rwkv_lnx_b"}
    arrays = {
        "x": i["x"], "w_in": _tiles(padded), "w_out": i["w_out"][0], "wq": _tiles(i["peer_wq"][0]),
        "peer_u": _tiles(i["peer_u"][0].T), "peer_v": i["peer_v"][0].reshape(NKEY, NKEY, D),
        "keys": np.ascontiguousarray(i["peer_keys"][0].transpose(3, 0, 1, 2)).reshape(
            P, 2 * HEADS, NKEY),
        "cols": np.ascontiguousarray(np.concatenate([_columns(i[source[n]]) for n in COLS], 1)),
        "consts": _consts(), "w2": i["rwkv_w2"][0], "a2": i["rwkv_a2"][0], "g2": g2,
        "lru_wa": i["lru_wa"][0], "lru_wi": i["lru_wi"][0], "normf_g": i["normf_g"],
    }
    nc = _bacc.Bacc("TRN2", target_bir_lowering=False, num_devices=1)
    aps, fed = {}, {}
    for name, arr in arrays.items():
        arr = np.ascontiguousarray(arr)
        fed[f"in_{name}"] = arr
        aps[name] = nc.dram_tensor(f"in_{name}", arr.shape, _mybir.dt.from_np(arr.dtype),
                                   kind="ExternalInput").ap()
    out = nc.dram_tensor("out_0", (1, SEQ, D), F32, kind="ExternalOutput").ap()
    hybrid_layer_kernel(nc, aps, out)
    r = _run(nc, [fed], core_ids=[0])
    return r.results[0]["out_0"]
```

```python
from contextlib import ExitStack

import numpy as np

import concourse.bass as bass
from concourse import mybir

F32 = mybir.dt.float32
F32R = mybir.dt.float32r
U32 = mybir.dt.uint32
BF16 = mybir.dt.bfloat16
ALU = mybir.AluOpType
ACT = mybir.ActivationFunctionType
AX_X = mybir.AxisListType.X

P = 128
SEQ = 256
NT2 = SEQ // P
D = 2048
KC = D // P
PIECE = 1024
D_LRU = 1024
CT = D_LRU // P
LORA_TILES = 3
GROUPS = 4
CHUNK = 64
NKEY = 128
HEADS = 8
TOPK = 16
NR = 5
EPS = 1e-6
GN_EPS = 64e-5
NEG = -3.0e38
EXPM = float(np.exp(-0.5))

COLS = {}
_at = 0
for _name, _n in (("g1", KC), ("g2", KC), ("conv_w", 4 * CT), ("conv_b", CT), ("ba", CT), ("bi", CT),
                  ("lam", CT), ("mu", 27), ("w0", CT), ("a0", CT), ("k_k", CT), ("k_a", CT),
                  ("r_k", CT), ("lnw", CT), ("lnb", CT)):
    COLS[_name] = (_at, _n)
    _at += _n
NCOL = _at

def w_in_order():
    def group(g):
        return [(kind, 2 * g + c) for kind in "rkv" for c in range(2)]
    lru = [(kind, c) for c in range(CT) for kind in ("xb", "gate")]
    order = [("lora", i) for i in range(LORA_TILES)] + group(0)
    for g in range(1, GROUPS):
        order += group(g) + lru[3 * (g - 1):3 * g]
    return order + lru[9:]


ORDER = w_in_order()
N_IN = len(ORDER)
N_OUT = KC
N_Q = KC
N_U = NKEY
N_V = NKEY
T_OUT = N_IN
T_Q = T_OUT + N_OUT
T_U = T_Q + N_Q
T_V = T_U + N_U
N_MASK = 11
N_G = SEQ // 4
U_FIRST = 95
U_EXP = 75
SHIFTED = [t for t, (kind, _) in enumerate(ORDER) if kind in ("lora", "r", "k", "v")]
MU = {t: {"r": 0, "k": CT, "v": 2 * CT, "lora": 3 * CT}[ORDER[t][0]] + ORDER[t][1] for t in SHIFTED}
MARKS = [range(9, 18), range(18, 27), range(27, 36), range(36, N_IN)]

RWKV_JOBS = ["zw", "za", "gate", "ss", "kb", "bsum", "vt", "bt", "kt",
             "m1_0", "m2_0", "m1_2", "m2_2", "m3_0", "m1_1", "m2_1", "m1_3", "m2_3", "m3_1"]
for _lv in range(1, 6):
    RWKV_JOBS += [f"y{_lv}_0", f"y{_lv}_1"]
    for _half in range(2):
        RWKV_JOBS += [f"{_kind}{_lv}_{_half}" for _kind in (("t", "tt") if _lv < 5 else ("tt",))]
for _c in range(4):
    RWKV_JOBS += [f"{_kind}{_c}" for _kind in ("r", "sa", "st", "yc") if (_kind, _c) != ("st", 3)]
RWKV_JOBS += ["yt"]


def psum_plan():
    names = [("x1", i, i % 8) for i in range(8)]
    ring = 0
    for t in range(9):
        names.append(("tile", t, t % 2))
    for g in range(GROUPS):
        for t in MARKS[g]:
            names.append(("tile", t, t % 2))
        for job in RWKV_JOBS:
            names.append((job, g, 2 + ring % 6))
            ring += 1
    for c in range(CT):
        for kind in ("lr", "li"):
            names.append((kind, c, 2 + ring % 6))
            ring += 1
    names += [("out", i, i) for i in range(8)]
    names += [("x2", i, i) for i in range(8)]
    for t in range(N_Q):
        names.append(("tile", T_Q + t, (T_Q + t) % 2))
        names.append(("sub", t, 2 + t % 4))
    for t in range(N_U):
        names.append(("tile", T_U + t, t % NR))
    for i in range(3):
        names.append(("idx", i, NR + i))
    for i in range(SEQ // 4):
        names.append(("gm", i, 2 + i % 4))
    names += [("peer", i, i) for i in range(8)]
    uses, plan = [0] * 8, {}
    for name, i, bank in names:
        plan[name, i] = (bank, uses[bank])
        uses[bank] += 1
    return plan


PLAN = psum_plan()


def full_counts():
    counts, out = [0] * 8, {}
    for (name, i), (bank, _) in PLAN.items():
        if name not in ("tile", "out", "peer"):
            counts[bank] += 1
            out[name, i] = counts[bank]
    return out


FULLS = full_counts()


def hybrid_layer_kernel(nc, a, out):
    ctx = ExitStack()
    with ctx:
        sems = {}

        def sem(name):
            if name not in sems:
                sems[name] = ctx.enter_context(nc.semaphore(name))
            return sems[name]

        base = [16512]

        def at(name, shape, dt, offset):
            return nc.alloc_sbuf_tensor_at(name, shape, dt, offset=offset)

        def place(name, shape, dt=F32):
            size = 4 * int(np.prod(shape[1:]))
            t = at(name, shape, dt, base[0])
            base[0] += (size + 31) // 32 * 32
            return t

        raw_at = base[0]
        raw = [place(f"raw{i}", [P, PIECE]) for i in range(NR)]
        lo = [at(f"lo{i}", [P, PIECE], F32R, raw_at + 4 * PIECE * i) for i in range(NR)]
        hi = [place(f"hi{i}", [P, PIECE], F32R) for i in range(NR)]
        hT_at = base[0]
        hT_hi = place("hT_hi", [P, KC, SEQ], F32R)
        hT_lo = place("hT_lo", [P, KC, SEQ], F32R)
        cols = place("cols", [P, NCOL])
        ident = place("ident", [P, P])
        iota = place("iota", [P, P])
        scal = place("scal", [P, 64])
        idx_at = base[0]
        idxT = place("idxT", [P, 3, SEQ])
        xpad = at("xpad", [P, SEQ + 3], F32, idx_at + 1024)
        mshift = [place(f"mshift{i}", [P, 1 + SEQ]) for i in range(2)]
        ARENA = (base[0] + 31) // 32 * 32
        ARENA_F = 32768
        end = ARENA + 4 * ARENA_F
        identb = at("identb", [P, P], BF16, end)
        assert end + 256 <= nc.sbuf_usable_end, (end, nc.sbuf_usable_end)

        def ar(name, first, shape, dt=F32):
            assert first + int(np.prod(shape[1:])) <= ARENA_F, name
            return at(name, shape, dt, ARENA + 4 * first)

        actg = ar("actg", 0, [P, NKEY, SEQ])

        f = [0]

        def nx(name, shape, dt=F32):
            t = ar(name, f[0], shape, dt)
            f[0] += int(np.prod(shape[1:]))
            return t

        masks = nx("masks", [P, N_MASK, P])
        blk, blk64, mU, m0, m0T = masks[:, 0], masks[:, 1], masks[:, 2:4], masks[:, 4], masks[:, 5]
        d0scan = nx("d0scan", [P, 8 * 65])
        wa2 = nx("wa2", [P, D_LRU])
        g2 = nx("g2", [P, 2, D_LRU])
        wai = nx("wai", [P, 2, CT, P])
        xc = nx("xc", [P, CT, SEQ])
        gate = nx("gate", [P, CT, SEQ])
        yR_hi = nx("yR_hi", [P, CT, SEQ], F32R)
        yR_lo = nx("yR_lo", [P, CT, SEQ], F32R)
        rkv = [nx(f"rkv{i}", [P, 3, 2, SEQ]) for i in range(2)]
        lora = nx("lora", [P, 3, SEQ])
        group_at = f[0]
        w65 = nx("w65", [P, 8, 65])
        aT = nx("aT", [P, 2, SEQ])
        inv_at = f[0]
        iP = nx("iP", [P, 2, SEQ])
        kk = nx("kk", [P, 2, SEQ])
        k2 = nx("k2", [P, 2, SEQ])
        bb = nx("bb", [P, 2, SEQ])
        sq = nx("sq", [P, 2, SEQ])
        gT = nx("gT", [P, 2, SEQ])
        P65 = nx("P65", [P, 8, 65])
        ARt = nx("ARt", [P, 2, 2, SEQ])
        ym_at = f[0]
        bt = nx("bt", [P, 2, SEQ])
        kt = nx("kt", [P, 2, SEQ])
        rk = nx("rk", [P, 2, SEQ])
        bon = nx("bon", [P, 2, SEQ])
        Vt = nx("Vt", [P, 2, NT2, P])
        Bt = nx("Bt", [P, 2, NT2, P])
        Kt = nx("Kt", [P, 2, NT2, P])
        L1 = nx("L1", [P, 8, 2, P])
        L2 = nx("L2", [P, 8, 2, P])
        ST1 = nx("ST1", [P, 2, P])
        kn = nx("kn", [P, 8])
        gsum, gvar, gsd = (nx(name, [P, 4, 4]) for name in ("gsum", "gvar", "gsd"))
        Tm = ar("Tm", inv_at, [P, 8, P])
        TT = ar("TT", inv_at + 1024, [P, 8, P])
        Ym = ar("Ym", ym_at, [P, 8, P])
        Rm = ar("Rm", group_at, [P, 4, 64])
        SA = ar("SA", group_at + 256, [P, NT2, 4, 64])
        ST = [ar("ST0", group_at + 768, [P, 2, P]), ST1]
        y_tm = ar("y_tm", inv_at, [P, NT2, 2, P])
        yT = ar("yT", inv_at + 512, [P, 2, SEQ])
        ysq = ar("ysq", ym_at, [P, 4, 64])
        x_sb = ar("x_sb", group_at, [P, NT2, D])
        h0 = ar("h0", group_at + 4096, [P, NT2, D])
        h_tmp = ar("h_tmp", group_at + 8192, [P, 2, 512])
        yL_hi = ar("yL_hi", group_at, [P, CT, SEQ], F32R)
        yL_lo = ar("yL_lo", group_at + 2048, [P, CT, SEQ], F32R)
        lr = ar("lr", group_at + 4096, [P, CT, SEQ])
        li = ar("li", group_at + 6144, [P, CT, SEQ])
        la = ar("la", group_at + 8192, [P, CT, SEQ])
        lt = ar("lt", group_at + 10240, [P, CT, SEQ])
        x2 = ar("x2", 0, [P, NT2, D])
        h2 = ar("h2", 4096, [P, NT2, D])
        h2_tmp = ar("h2_tmp", 8192, [P, 2, 512])
        keysT = ar("keysT", 20480, [P, 2 * HEADS, NKEY])
        TK = U_FIRST * SEQ
        qT = [ar(f"qT{i}", TK + i * SEQ, [P, SEQ]) for i in range(2)]
        tk_s = ar("tk_s", TK + 512, [P, P])
        tk_cand = ar("tk_cand", TK + 640, [P, TOPK, TOPK])
        tk_cand2 = ar("tk_cand2", TK + 896, [P, TOPK * TOPK])
        tk_sv = ar("tk_sv", TK + 1152, [P, 2, TOPK])
        tk_si = ar("tk_si", TK + 1184, [P, 2, TOPK], U32)
        tk_pos = ar("tk_pos", TK + 1216, [P, TOPK], U32)
        tk_ab = ar("tk_ab", TK + 1232, [P, 2, TOPK], U32)
        sif = ar("sif", TK + 1280, [P, NT2, 2, HEADS, TOPK])
        abf = ar("abf", TK + 1792, [P, NT2, 2, HEADS, TOPK])
        best = ar("best", TK + 2304, [P, NT2, HEADS, TOPK])
        sel = ar("sel", TK + 2560, [P, NT2, 3, HEADS * TOPK])
        sm = ar("sm", TK + 3328, [P, NT2, HEADS])
        sub = ar("sub", TK + 4096, [P, NT2, 2 * HEADS, P])
        oneh = ar("oneh", TK + 4096, [P, HEADS * TOPK, TOPK])
        oneB = [at(f"oneB{i}", [P, 4, P], F32, hT_at + 2048 * i) for i in range(2)]
        oneA = [at(f"oneA{i}", [P, 4, P], F32, hT_at + 4096 + 2048 * i) for i in range(2)]
        a_hi = [at(f"a_hi{i}", [P, SEQ], F32R, hT_at + 8192 + 1024 * i) for i in range(NR)]
        a_lo = [at(f"a_lo{i}", [P, SEQ], F32R, hT_at + 13312 + 1024 * i) for i in range(NR)]
        xr = ar("xr", 0, [P, NT2, D])
        gf = ar("gf", 4096, [P, D])
        junk = ar("junk", 6144, [P, D])

        ps = ctx.enter_context(nc.psum_tensor("ps", [P, 8, 512], F32))
        x2_dram = nc.dram_tensor("x2_spill", (P, NT2 * D), F32, kind="Internal").ap()

        full = [sem(f"bank_full{i}") for i in range(8)]
        free = [sem(f"bank_free{i}") for i in range(8)]
        raw_in = [sem(f"raw_in{i}") for i in range(NR)]
        hi_done, lo_done, mm_done = sem("hi_done"), sem("lo_done"), sem("mm_done")
        block = ctx.enter_context(nc.Block())

        def col(name, i=0, n=1):
            first = COLS[name][0] + i
            return cols[:, first:first + n]

        def colr(name):
            return col(name, 0, COLS[name][1])

        rs, ssq, sd = scal[:, 0:2], scal[:, 2:4], scal[:, 4:6]
        hw0, ha0, hba, hbi, nsp = (scal[:, 6 + 8 * i:14 + 8 * i] for i in range(5))
        eps_c, gneps_c, mc2 = scal[:, 46:47], scal[:, 47:48], scal[:, 48:49]
        omu, oka, psp = idxT[:, 0, 0:27], idxT[:, 0, 32:40], idxT[:, 0, 40:48]
        sp = [idxT[:, 0, 48 + 8 * i:56 + 8 * i] for i in range(7)]

        def bank(name, i):
            return ps[:, PLAN[name, i][0]]

        def freed(name, i):
            return free[PLAN[name, i][0]]

        def wait_full(eng, name, i):
            b, n = PLAN[name, i]
            if name == "tile":
                eng.wait_ge(mm_done, 2 * i + 2)
            else:
                eng.wait_ge(full[b], FULLS[name, i])

        def wait_free(eng, name, i):
            b, n = PLAN[name, i]
            if n:
                eng.wait_ge(free[b], n)

        def wait_read(eng, name, i):
            b, n = PLAN[name, i]
            eng.wait_ge(free[b], n + 1)

        def dest(t):
            kind, c = ORDER[t]
            if kind == "lora":
                return lora[:, c]
            return rkv[(c // 2) % 2][:, "rkv".index(kind), c % 2]

        @block.sync
        def _(sync):
            xv = a["x"].rearrange("o (t p) d -> p (o t) d", p=P)
            sync.dma_start(x_sb[:, :, :], xv).then_inc(sem("x_in"), 16)
            sync.dma_start(cols[:, :], a["cols"]).then_inc(sem("cols_in"), 16)
            sync.dma_start(ident[:, :], a["consts"][:, 0:P]).then_inc(sem("ident_in"), 16)
            sync.dma_start(iota[:, :], a["consts"][:, P:2 * P]).then_inc(sem("iota_in"), 16)

            def load(n, src):
                if n >= NR:
                    sync.wait_ge(mm_done, n - NR + 1)
                sync.dma_start(raw[n % NR][:, :], src).then_inc(raw_in[n % NR], 16)

            for n in range(2 * N_IN):
                load(n, a["w_in"][n // 2, n % 2])
                if n == 3:
                    m_end = (2 + N_MASK) * P
                    sync.dma_start(masks[:, :, :], a["consts"][:, 2 * P:m_end].rearrange(
                        "p (m q) -> p m q", q=P)).then_inc(sem("masks_in"), 16)
                    sync.dma_start(d0scan[:, :], a["consts"][:, m_end:m_end + 520]).then_inc(
                        sem("scan_in"), 16)
                    sync.dma_start(wa2[0:64, :], a["w2"]).then_inc(sem("w2_in"), 16)
                    sync.dma_start(wa2[64:128, :], a["a2"]).then_inc(sem("a2_in"), 16)
                    sync.dma_start(g2[:, :, :], a["g2"].rearrange("(k p) c -> p k c", p=P)).then_inc(
                        sem("g2_in"), 16)
                    sync.dma_start(wai[:, 0], a["lru_wa"].rearrange("h i j -> i h j")).then_inc(
                        sem("wa_in"), 16)
                    sync.dma_start(wai[:, 1], a["lru_wi"].rearrange("h i j -> i h j")).then_inc(
                        sem("wi_in"), 16)
            for c in range(N_OUT):
                ch = (c + CT) % KC
                for half in range(2):
                    load(2 * (T_OUT + c) + half,
                         a["w_out"][ch * P:(ch + 1) * P, half * PIECE:(half + 1) * PIECE])
                if c == 0:
                    sync.wait_ge(sem("yR_lo"), GROUPS)
                    sync.dma_start(x2[:, :, :], xv).then_inc(sem("x2_in"), 16)
            for t in range(N_Q):
                for half in range(2):
                    load(2 * (T_Q + t) + half, a["wq"][t, half])
                if t == 0:
                    sync.wait_ge(sem("x2_done"), 8)
                    sync.dma_start(keysT[:, :, :], a["keys"]).then_inc(sem("keys_in"), 16)
                    sync.dma_start(x2_dram, x2[:, :, :].rearrange("p t d -> p (t d)")).then_inc(
                        sem("x2_out"), 16)
            def u_load(it, tiles=NR):
                for q in range(2 * tiles):
                    n = 2 * T_U + q
                    sync.wait_ge(mm_done, it * (2 * NR) + (n - NR + 1))
                    sync.dma_start(raw[n % NR][:, :], a["peer_u"][it * NR + q // 2, q % 2]).then_inc(
                        raw_in[n % NR], 16)

            def v_load(it, tiles=NR):
                for q in range(2 * tiles):
                    n = 2 * T_V + q
                    sync.wait_ge(mm_done, it * (2 * NR) + (n - NR + 1))
                    sync.dma_start(raw[n % NR][:, :], a["peer_v"][
                        it * NR + q // 2, :, (q % 2) * PIECE:(q % 2 + 1) * PIECE]).then_inc(
                        raw_in[n % NR], 16)

            with sync.Fori(0, N_U // NR) as it:
                u_load(it)
            u_load(N_U // NR, N_U % NR)
            with sync.Fori(0, N_V // NR) as it:
                v_load(it)
            v_load(N_V // NR, N_V % NR)
            sync.wait_ge(sem("alo_done"), N_V)
            sync.wait_ge(sem("x2_out"), 16)
            sync.dma_start(xr[:, :, :].rearrange("p t d -> p (t d)"), x2_dram).then_inc(sem("xr_in"), 16)
            sync.dma_start(gf[:, :], a["normf_g"].partition_broadcast(P)).then_inc(sem("gf_in"), 16)
            outv = out.rearrange("o (t p) d -> p (o t) d", p=P)
            for t in range(NT2):
                sync.wait_ge(sem("y_done"), t + 1)
                sync.dma_start(outv[:, t], xr[:, t]).then_inc(sem("out_sent"), 16)
            sync.wait_ge(sem("out_sent"), 16 * NT2)

        @block.scalar
        def _(act):
            def mark(ins, name, value):
                ins.then_inc(sem(name), 1)
                act.wait_ge(sem(name), value)

            def hi_piece(n):
                act.wait_ge(raw_in[n % NR], 16 * (n // NR + 1))
                if n >= NR:
                    act.wait_ge(mm_done, n - NR + 1)
                nc.scalar.activation(hi[n % NR][:, :], raw[n % NR][:, :], ACT.Copy).then_inc(hi_done, 1)

            def norm_root(i):
                act.wait_ge(sem("ssq_done"), 2 * i + 2)
                nc.scalar.activation(sd, ssq, ACT.Sqrt, scale=1.0 / D, bias=eps_c).then_inc(
                    sem("sd_done"), 1)

            def turned_hi(name, tmp):
                for j in range(8):
                    act.wait_ge(sem(f"{name}_tmp"), j + 1)
                    nc.scalar.activation(hT_hi[:, 2 * j:2 * j + 2, :].rearrange("p c t -> p (c t)"),
                                         tmp[:, j % 2], ACT.Copy).then_inc(sem(f"{name}_hi"), 1)

            act.wait_ge(sem("consts_done"), 1)
            norm_root(0)
            act.wait_ge(sem("lam_abs"), 1)
            nc.scalar.activation(sp[1], sp[0], ACT.Exp, scale=-1.0).then_inc(sem("lam_exp"), 1)
            act.wait_ge(sem("lam_u"), 1)
            nc.scalar.activation(sp[3], sp[2], ACT.Ln).then_inc(sem("lam_ln"), 1)
            turned_hi("h1", h_tmp)

            def result(t):
                kind, c = ORDER[t]
                wait_full(act, "tile", t)
                pb = bank("tile", t)[:, 0:SEQ]
                if kind == "xb":
                    if c:
                        act.wait_ge(sem("conv_done"), c)
                    nc.scalar.activation(xpad[:, 3:3 + SEQ], pb, ACT.Copy).then_inc(freed("tile", t), 1)
                elif kind == "gate":
                    nc.scalar.activation(gate[:, c], pb, ACT.Copy).then_inc(freed("tile", t), 1)
                else:
                    q = SHIFTED.index(t)
                    if q >= 2:
                        wait_read(act, "tile", SHIFTED[q - 2])
                    nc.scalar.activation(mshift[q % 2][:, 1:1 + SEQ], pb, ACT.Copy,
                                         scale=col("mu", MU[t])).then_inc(sem("mu_done"), 1)

            def tile(t):
                hi_piece(2 * t + 2)
                hi_piece(2 * t + 3)
                if t:
                    result(t - 1)

            hi_piece(0)
            hi_piece(1)
            for t in range(9):
                tile(t)
                if t == 3:
                    wait_read(act, "tile", 2)
                    nc.scalar.activation(lora[0:64, 0], lora[0:64, 0], ACT.Tanh).then_inc(
                        sem("lora_act"), 1)
                    nc.scalar.activation(lora[:, 1:3], lora[:, 1:3], ACT.Tanh, scale=0.5).then_inc(
                        sem("lora_act"), 1)
            for g in range(GROUPS):
                marks = list(MARKS[g])

                def m():
                    if marks:
                        tile(marks.pop(0))

                m()
                act.wait_ge(sem("w65_ready"), g + 1)
                wait_full(act, "zw", g)
                for c in range(2):
                    ins = nc.scalar.activation(
                        w65[:, 4 * c:4 * c + 4, 1:65],
                        bank("zw", g)[:, c * SEQ:(c + 1) * SEQ].rearrange("p (k t) -> p k t", t=CHUNK),
                        ACT.Tanh, scale=0.5, bias=hw0[:, 2 * g + c:2 * g + c + 1])
                ins.then_inc(freed("zw", g), 1)
                wait_full(act, "za", g)
                for c in range(2):
                    ins = nc.scalar.activation(aT[:, c], bank("za", g)[:, c * SEQ:(c + 1) * SEQ],
                                               ACT.Tanh, scale=0.5, bias=ha0[:, 2 * g + c:2 * g + c + 1])
                ins.then_inc(freed("za", g), 1)
                wait_full(act, "gate", g)
                nc.scalar.activation(gT[:, :, :].rearrange("p c t -> p (c t)"), bank("gate", g),
                                     ACT.Copy).then_inc(freed("gate", g), 1)
                act.wait_ge(sem("scan_done"), g + 1)
                nc.scalar.activation(iP[:, :, :].rearrange("p c (k t) -> p (c k) t", t=CHUNK),
                                     P65[:, :, 1:65], ACT.Exp, scale=0.5 * EXPM).then_inc(
                    sem("ip_done"), 1)
                act.wait_ge(sem("ip_done"), g + 1)
                nc.scalar.activation(P65[:, :, :], P65[:, :, :], ACT.Exp, scale=-0.5 * EXPM).then_inc(
                    sem("p_done"), 1)
                m()
                wait_full(act, "ss", g)
                nc.scalar.activation(kn[:, :], bank("ss", g)[:, 0:8], ACT.Sqrt).then_inc(
                    freed("ss", g), 1)
                m()
                m()
                for name, dst in (("vt", Vt), ("bt", Bt), ("kt", Kt)):
                    wait_full(act, name, g)
                    nc.scalar.activation(dst[:, :, :, :].rearrange("p c k t -> p (c k t)"),
                                         bank(name, g), ACT.Copy).then_inc(freed(name, g), 1)
                m()
                for lv in range(1, 6):
                    for half in range(2):
                        for name, dst in (("t", Tm), ("tt", TT)):
                            job = f"{name}{lv}_{half}"
                            if (job, g) not in PLAN:
                                continue
                            wait_full(act, job, g)
                            nc.scalar.activation(
                                dst[:, 4 * half:4 * half + 4].rearrange("p a b -> p (a b)"),
                                bank(job, g), ACT.Copy).then_inc(freed(job, g), 1)
                m()
                for c in range(4):
                    rows = slice(64 * (c % 2), 64 * (c % 2) + 64)
                    wait_full(act, f"r{c}", g)
                    act.wait_ge(sem("chain_zero"), g + 1)
                    nc.scalar.activation(Rm[rows, :, :].rearrange("p a b -> p (a b)"),
                                         bank(f"r{c}", g)[rows, 0:256], ACT.Copy).then_inc(
                        freed(f"r{c}", g), 1)
                    m()
                    act.wait_ge(sem("gvar_done"), 4 * g + c + 1)
                    nc.scalar.activation(gsd[rows, c], gvar[rows, c], ACT.Sqrt, scale=1.0 / 64,
                                         bias=gneps_c[rows]).then_inc(sem("gsd_done"), 1)
                act.wait_ge(sem("y_f32"), g + 1)
                nc.scalar.activation(yR_hi[:, 2 * g:2 * g + 2, :], yT[:, :, :], ACT.Copy).then_inc(
                    sem("yR_hi"), 1)
                assert not marks
            result(N_IN - 1)

            hi_piece(2 * T_OUT + 2)
            act.wait_ge(sem("yR_lo"), GROUPS)
            for c in range(CT):
                wait_full(act, "lr", c)
                nc.scalar.activation(lr[:, c], bank("lr", c)[:, 0:SEQ], ACT.Tanh, scale=0.5,
                                     bias=hba[:, c:c + 1]).then_inc(freed("lr", c), 1)
                wait_full(act, "li", c)
                nc.scalar.activation(li[:, c], bank("li", c)[:, 0:SEQ], ACT.Tanh, scale=0.5,
                                     bias=hbi[:, c:c + 1]).then_inc(freed("li", c), 1)
            act.wait_ge(sem("lr_sig"), 1)
            for c in range(CT):
                nc.scalar.activation(la[:, c], lr[:, c], ACT.Exp, scale=nsp[:, c:c + 1])
                ins = nc.scalar.activation(lt[:, c], lr[:, c], ACT.Tanh, scale=psp[:, c:c + 1])
            ins.then_inc(sem("la_lt_done"), 1)
            hi_piece(2 * T_OUT + 3)
            act.wait_ge(sem("om_done"), 1)
            nc.scalar.activation(lt[:, :, :], lt[:, :, :], ACT.Sqrt).then_inc(sem("om_root"), 1)
            hi_piece(2 * T_OUT + 4)
            hi_piece(2 * T_OUT + 5)
            nc.scalar.activation(gate[:, :, :], gate[:, :, :], ACT.Gelu_apprx_tanh).then_inc(
                sem("gelu_done"), 1)
            hi_piece(2 * T_OUT + 6)
            hi_piece(2 * T_OUT + 7)
            act.wait_ge(sem("yL_f32"), 1)
            nc.scalar.activation(yL_hi[:, :, :], lt[:, :, :], ACT.Copy).then_inc(sem("yL_hi"), 1)
            for n in range(2 * T_OUT + 8, 2 * T_Q + 2):
                hi_piece(n)
            norm_root(1)
            turned_hi("h2", h2_tmp)

            def scores_out(t):
                wait_full(act, "sub", t)
                nc.scalar.activation(sub[:, :, t, :], bank("sub", t)[:, 0:2 * P].rearrange(
                    "p (a b) -> p a b", a=2), ACT.Copy).then_inc(freed("sub", t), 1)

            for t in range(N_Q):
                hi_piece(2 * (T_Q + t) + 2)
                hi_piece(2 * (T_Q + t) + 3)
                if t >= 2:
                    scores_out(t - 2)
                wait_full(act, "tile", T_Q + t)
                nc.scalar.activation(qT[t % 2][:, :], bank("tile", T_Q + t)[:, 0:SEQ], ACT.Copy).then_inc(
                    freed("tile", T_Q + t), 1)
            scores_out(N_Q - 2)
            scores_out(N_Q - 1)
            act.wait_ge(sem("x2_out"), 16)

            def u_hi(it, q):
                n = 2 * T_U + q
                act.wait_ge(raw_in[n % NR], it * 32 + 16 * (n // NR + 1))
                act.wait_ge(mm_done, it * (2 * NR) + (n - NR + 1))
                nc.scalar.activation(hi[n % NR][:, :], raw[n % NR][:, :], ACT.Copy).then_inc(hi_done, 1)

            def u_gelu(it, b):
                act.wait_ge(mm_done, it * (2 * NR) + 2 * (T_U + b + 1))
                nc.scalar.activation(
                    actg[:, bass.ds(it * NR + b, 1), :].rearrange("p a b -> p (a b)"),
                    ps[:, b % NR, 0:SEQ], ACT.Gelu_apprx_tanh).then_inc(free[b % NR], 1)

            def u_body(it, first=False, tiles=NR):
                for b in range(tiles):
                    if not (first and b == 0):
                        u_hi(it, 2 * b)
                        u_hi(it, 2 * b + 1)
                        u_gelu(it, b - 1)

            u_body(0, True)
            with act.Fori(1, U_EXP // NR) as it:
                u_body(it)
            act.wait_ge(sem("best_sub"), 1)
            nc.scalar.activation(best[:, :, :, :], best[:, :, :, :], ACT.Exp).then_inc(
                sem("best_exp"), 1)
            with act.Fori(U_EXP // NR, U_FIRST // NR) as it:
                u_body(it)
            for i in range(3):
                wait_full(act, "idx", i)
                nc.scalar.activation(idxT[:, i], bank("idx", i)[:, 0:SEQ], ACT.Copy).then_inc(
                    freed("idx", i), 1)
            with act.Fori(U_FIRST // NR, N_U // NR) as it:
                u_body(it)
            u_body(N_U // NR, tiles=N_U % NR)
            u_gelu(N_U // NR, N_U % NR - 1)

            act.wait_ge(sem("gated"), N_G)

            def v_body(it, tiles=NR):
                for b in range(tiles):
                    nc.scalar.activation(a_hi[b][:, :], actg[:, bass.ds(it * NR + b, 1), :].rearrange(
                        "p a b -> p (a b)"), ACT.Copy).then_inc(sem("ahi_done"), 1)
                    for n in (2 * (T_V + b), 2 * (T_V + b) + 1):
                        act.wait_ge(raw_in[n % NR], it * 32 + 16 * (n // NR + 1))
                        act.wait_ge(mm_done, it * (2 * NR) + (n - NR + 1))
                        nc.scalar.activation(hi[n % NR][:, :], raw[n % NR][:, :],
                                             ACT.Copy).then_inc(hi_done, 1)

            with act.Fori(0, N_V // NR) as it:
                v_body(it)
            v_body(N_V // NR, N_V % NR)
            for t in range(NT2):
                act.wait_ge(sem("ssq_done"), 4 + t + 1)
                nc.scalar.activation(sd[:, t:t + 1], ssq[:, t:t + 1], ACT.Sqrt, scale=1.0 / D,
                                     bias=eps_c).then_inc(sem("sd_done"), 1)

        @block.vector
        def _(dve):
            chain = [0]
            V = nc.vector

            def link(ins):
                chain[0] += 1
                ins.then_inc(sem("dve_chain"), 1)
                dve.wait_ge(sem("dve_chain"), chain[0])

            def mark(ins, name, value):
                ins.then_inc(sem(name), 1)
                dve.wait_ge(sem(name), value)

            def out_of(ins, name, i):
                ins.then_inc(freed(name, i), 1)
                wait_read(dve, name, i)

            def lo_piece(n):
                dve.wait_ge(hi_done, n + 1)
                V.tensor_tensor(lo[n % NR][:, :], raw[n % NR][:, :], hi[n % NR][:, :].bitcast(F32),
                                ALU.subtract).then_inc(lo_done, 1)

            def ts(o, i, s1, s2, op0, op1=None):
                return V.tensor_scalar(o, i, s1, s2, op0, op1) if op1 is not None else \
                    V.tensor_scalar(o, i, s1, None, op0)

            def stt(o, i0, s, i1, op0, op1):
                return V.scalar_tensor_tensor(out=o, in0=i0, scalar=s, in1=i1, op0=op0, op1=op1)

            def normalise(i, x, h):
                for t in range(NT2):
                    mark(V.tensor_tensor_reduce(out=h[:, t], in0=x[:, t], in1=x[:, t], scale=1.0,
                                                scalar=0.0, op0=ALU.mult, op1=ALU.add,
                                                accum_out=ssq[:, t:t + 1]), "ssq_done", 2 * i + t + 1)
                dve.wait_ge(sem("sd_done"), i + 1)
                link(V.reciprocal(rs, sd))
                for t in range(NT2):
                    link(ts(h[:, t], x[:, t], rs[:, t:t + 1], None, ALU.mult))
                dve.sem_inc(sem("rows_done"), 1)

            def turned_lo(i, name, job, tmp, gain):
                for j in range(9):
                    if j < 8:
                        wait_full(dve, job, j)
                        g_b = col(gain, 2 * j, 2).unsqueeze(2).broadcast_to([P, 2, SEQ])
                        V.tensor_tensor(tmp[:, j % 2].rearrange("p (c t) -> p c t", c=2),
                                        bank(job, j).rearrange("p (c t) -> p c t", c=2), g_b,
                                        ALU.mult).then_inc(sem(f"{name}_tmp"), 1)
                    if j:
                        q = j - 1
                        dve.wait_ge(sem(f"{name}_tmp"), q + 1)
                        dve.wait_ge(sem(f"{name}_hi"), q + 1)
                        V.tensor_tensor(hT_lo[:, 2 * q:2 * q + 2, :].rearrange("p c t -> p (c t)"),
                                        tmp[:, q % 2], hT_hi[:, 2 * q:2 * q + 2, :].bitcast(F32).rearrange(
                                            "p c t -> p (c t)"), ALU.subtract).then_inc(freed(job, q), 1)
                        wait_read(dve, job, q)
                dve.sem_inc(sem("hT_done"), 1)

            V.memset(eps_c, EPS)
            V.memset(gneps_c, GN_EPS)
            for i in range(2):
                V.memset(mshift[i][:, 0:1], 0.0)
            V.memset(xpad[:, 0:3], 0.0)
            mark(V.memset(mc2, -0.5 * EXPM), "consts_done", 1)
            dve.wait_ge(sem("x_in"), 16)
            normalise(0, x_sb, h0)
            dve.wait_ge(sem("cols_in"), 16)
            for dst, name in ((hw0, "w0"), (ha0, "a0"), (hba, "ba"), (hbi, "bi")):
                ts(dst, colr(name), 0.5, None, ALU.mult)
            ts(omu, colr("mu"), -1.0, 1.0, ALU.mult, ALU.add)
            link(ts(oka, colr("k_a"), -1.0, 1.0, ALU.mult, ALU.add))
            link(ts(sp[5], colr("lam"), -1.0, None, ALU.mult))
            mark(V.tensor_tensor(sp[0], colr("lam"), sp[5], ALU.max), "lam_abs", 1)
            dve.wait_ge(sem("lam_exp"), 1)
            mark(ts(sp[2], sp[1], 1.0, None, ALU.add), "lam_u", 1)
            link(ts(sp[4], sp[2], -1.0, None, ALU.add))
            link(V.tensor_tensor(sp[4], sp[1], sp[4], ALU.subtract))
            link(V.reciprocal(sp[6], sp[2]))
            link(V.tensor_tensor(sp[4], sp[4], sp[6], ALU.mult))
            dve.wait_ge(sem("lam_ln"), 1)
            link(V.tensor_tensor(sp[4], sp[4], sp[3], ALU.add))
            link(stt(sp[4], sp[5], 0.0, sp[4], ALU.max, ALU.add))
            link(ts(psp, sp[4], 8.0, None, ALU.mult))
            link(ts(nsp, sp[4], -8.0, None, ALU.mult))
            dve.wait_ge(sem("ident_in"), 16)
            mark(V.tensor_copy(identb[:, :], ident[:, :]), "identb_done", 1)
            turned_lo(0, "h1", "x1", h_tmp, "g1")

            def result(t):
                kind, c = ORDER[t]
                if kind == "xb":
                    wait_read(dve, "tile", t)
                    link(ts(xc[:, c], xpad[:, 3:3 + SEQ], col("conv_w", 3 * CT + c), col("conv_b", c),
                            ALU.mult, ALU.add))
                    link(stt(xc[:, c], xpad[:, 2:2 + SEQ], col("conv_w", 2 * CT + c), xc[:, c],
                             ALU.mult, ALU.add))
                    link(stt(xc[:, c], xpad[:, 1:1 + SEQ], col("conv_w", CT + c), xc[:, c],
                             ALU.mult, ALU.add))
                    mark(stt(xc[:, c], xpad[:, 0:SEQ], col("conv_w", c), xc[:, c],
                             ALU.mult, ALU.add), "conv_done", c + 1)
                elif kind != "gate":
                    q = SHIFTED.index(t)
                    dve.wait_ge(sem("mu_done"), q + 1)
                    out_of(stt(dest(t), bank("tile", t)[:, 0:SEQ], omu[:, MU[t]:MU[t] + 1],
                               mshift[q % 2][:, 0:SEQ], ALU.mult, ALU.add), "tile", t)

            def tile(t):
                lo_piece(2 * t + 2)
                lo_piece(2 * t + 3)
                if t:
                    result(t - 1)

            lo_piece(0)
            lo_piece(1)
            for t in range(9):
                tile(t)
                if t == 4:
                    dve.wait_ge(sem("lora_act"), 2)
                    mark(ts(lora[:, 1:3], lora[:, 1:3], 0.5, 0.5, ALU.mult, ALU.add), "lora_done", 1)
            def unit_rows(g, c):
                rows = slice(64 * (c % 2), 64 * (c % 2) + 64)
                yd = y_tm[rows, c // 2].rearrange("p c (h i) -> p (c h) i", h=2)
                dve.wait_ge(sem("gsd_done"), 4 * g + c + 1)
                link(V.reciprocal(gsd[rows, c], gsd[rows, c]))
                link(V.tensor_tensor(yd, yd, gsd[rows, c].unsqueeze(2).broadcast_to([64, 4, 64]),
                                     ALU.mult))

            dve.wait_ge(sem("masks_in"), 16)
            dve.wait_ge(sem("scan_in"), 16)
            for g in range(GROUPS):
                marks = list(MARKS[g])

                def m():
                    if marks:
                        tile(marks.pop(0))

                def cg(name, c):
                    return col(name, 2 * g + c)

                R, K, Vv = (rkv[g % 2][:, i] for i in range(3))
                m()
                mark(V.memset(w65[:, :, 0:1], 0.0), "w65_ready", g + 1)
                for c in range(2):
                    link(ts(kk[:, c], K[:, c], cg("k_k", c), None, ALU.mult))
                mark(V.tensor_tensor(sq[:, :, :], kk[:, :, :], kk[:, :, :], ALU.mult), "sq_done", g + 1)
                wait_read(dve, "zw", g)
                link(ts(w65[:, :, 1:65], w65[:, :, 1:65], 1.0, None, ALU.add))
                mark(V.tensor_tensor_scan(P65[:, :, :].rearrange("p a b -> p (a b)"), d0scan[:, :],
                                          w65[:, :, :].rearrange("p a b -> p (a b)"),
                                          0.0, ALU.mult, ALU.add), "scan_done", g + 1)
                m()
                wait_read(dve, "ss", g)
                link(ts(kn[:, :], kn[:, :], 1e-12, None, ALU.max))
                link(V.reciprocal(kn[:, :], kn[:, :]))
                mark(V.tensor_copy(sq[:, :, :].rearrange("p c (k i) -> p (c k) i", i=64),
                                   kn[:, :].unsqueeze(2).broadcast_to([P, 8, 64])), "kn_done", g + 1)
                wait_read(dve, "za", g)
                link(ts(aT[:, :, :], aT[:, :, :], 0.5, 0.5, ALU.mult, ALU.add))
                for c in range(2):
                    link(ts(k2[:, c], aT[:, c], cg("k_a", c), oka[:, 2 * g + c:2 * g + c + 1],
                            ALU.mult, ALU.add))
                link(V.tensor_tensor(k2[:, :, :], k2[:, :, :], K, ALU.mult))
                dve.wait_ge(sem("ip_done"), g + 1)
                V.tensor_tensor(kt[:, :, :], k2[:, :, :], iP[:, :, :], ALU.mult)
                for c in range(2):
                    ins = stt(rk[:, c], R[:, c], cg("r_k", c), k2[:, c], ALU.mult, ALU.mult)
                mark(ins, "rk_done", g + 1)
                m()
                wait_full(dve, "kb", g)
                out_of(V.tensor_tensor(kk[:, :, :].rearrange("p c t -> p (c t)"),
                                       kk[:, :, :].rearrange("p c t -> p (c t)"), bank("kb", g),
                                       ALU.mult), "kb", g)
                link(V.tensor_tensor(bb[:, :, :], kk[:, :, :], aT[:, :, :], ALU.mult))
                mark(V.tensor_tensor(bt[:, :, :], bb[:, :, :], iP[:, :, :], ALU.mult), "bk_done", g + 1)
                dve.wait_ge(sem("p_done"), g + 1)
                link(stt(ARt[:, 0].rearrange("p c (k t) -> p (c k) t", t=CHUNK),
                         kk[:, :, :].rearrange("p c (k t) -> p (c k) t", t=CHUNK), -1.0,
                         P65[:, :, 0:64], ALU.mult, ALU.mult))
                mark(V.tensor_tensor(ARt[:, 1].rearrange("p c (k t) -> p (c k) t", t=CHUNK),
                                     R.rearrange("p c (k t) -> p (c k) t", t=CHUNK),
                                     P65[:, :, 1:65], ALU.mult), "ar_done", g + 1)
                V.memset(Rm[:, :, :], 0.0)
                V.memset(SA[:, :, :, :], 0.0)
                mark(V.memset(ST[0][:, :, :], 0.0), "chain_zero", g + 1)
                m()
                wait_full(dve, "bsum", g)
                out_of(V.tensor_tensor(bon[:, :, :].rearrange("p c t -> p (c t)"), bank("bsum", g),
                                       Vv.rearrange("p c t -> p (c t)"), ALU.mult), "bsum", g)

                def mask_b(mask, n):
                    return mask.unsqueeze(1).broadcast_to([P, n, P])

                def masked(job, dst):
                    pb = bank(job, g).rearrange("p (t w q) -> p t w q", t=2, w=2)
                    return V.tensor_tensor(dst, pb, mU.unsqueeze(1).broadcast_to([P, 2, 2, P]), ALU.mult)

                for half in range(2):
                    for hl in (half, half + 2):
                        wait_full(dve, f"m1_{hl}", g)
                        V.tensor_tensor(TT[:, 2 * hl:2 * hl + 2, :], bank(f"m1_{hl}", g).rearrange(
                            "p (t w q) -> p t w q", t=2, w=2)[:, :, 0], mask_b(m0T, 2), ALU.mult)
                        out_of(masked(f"m1_{hl}", L1[:, 2 * hl:2 * hl + 2]), f"m1_{hl}", g)
                        wait_full(dve, f"m2_{hl}", g)
                        out_of(masked(f"m2_{hl}", L2[:, 2 * hl:2 * hl + 2]), f"m2_{hl}", g)
                    wait_full(dve, f"m3_{half}", g)
                    out_of(V.tensor_tensor(
                        Tm[:, :, :].rearrange("p (c h t) q -> p c h (t q)", c=2, h=2)[:, :, half].rearrange(
                            "p c (t q) -> p c t q", t=2),
                        bank(f"m3_{half}", g).rearrange("p (c t q) -> p c t q", c=2, t=2),
                        m0.unsqueeze(1).unsqueeze(1).broadcast_to([P, 2, 2, P]), ALU.mult),
                        f"m3_{half}", g)
                V.tensor_tensor(TT[:, :, :], TT[:, :, :], mask_b(ident[:, :], 8), ALU.add)
                mark(V.tensor_tensor(Tm[:, :, :], Tm[:, :, :], mask_b(ident[:, :], 8), ALU.add),
                     "first_inverse", g + 1)
                m()
                for lv in range(1, 6):
                    for half in range(2):
                        job = f"y{lv}_{half}"
                        wait_full(dve, job, g)
                        out_of(V.tensor_tensor(Ym[:, 4 * half:4 * half + 4],
                                               bank(job, g).rearrange("p (a q) -> p a q", a=4),
                                               mask_b(masks[:, 5 + lv], 4), ALU.mult), job, g)
                m()
                for c in range(4):
                    rows = slice(64 * (c % 2), 64 * (c % 2) + 64)
                    if c < 3:
                        pcm = sq[:, c % 2].rearrange("p (c q) -> p c q", c=2)
                        for ct in range(2):
                            k = 4 * ct + c
                            link(ts(pcm[:, ct], blk, P65[:, k, 64:65], None, ALU.mult))
                    wait_full(dve, f"sa{c}", g)
                    out_of(V.tensor_copy(SA[rows, c // 2].rearrange("p a b -> p (a b)"),
                                         bank(f"sa{c}", g)[rows, 0:256]), f"sa{c}", g)
                    if c < 3:
                        wait_full(dve, f"st{c}", g)
                        out_of(V.tensor_tensor(ST[(c + 1) % 2][:, :, :],
                                               bank(f"st{c}", g)[:, 0:256].rearrange(
                                                   "p (c q) -> p c q", c=2), pcm, ALU.mult),
                               f"st{c}", g)
                    wait_full(dve, f"yc{c}", g)
                    yp = bank(f"yc{c}", g)[rows, 0:256].rearrange("p (h i) -> p h i", h=4)
                    yd = y_tm[rows, c // 2].rearrange("p c (h i) -> p (c h) i", h=2)
                    link(V.tensor_reduce(gsum[rows, c], yp, AX_X, ALU.add))
                    out_of(stt(yd, gsum[rows, c].unsqueeze(2).broadcast_to([64, 4, 64]), -1.0 / 64, yp,
                               ALU.mult, ALU.add), f"yc{c}", g)
                    link(V.tensor_tensor(ysq[rows, :, :], yd, yd, ALU.mult))
                    mark(V.tensor_reduce(gvar[rows, c], ysq[rows, :, :], AX_X, ALU.add),
                         "gvar_done", 4 * g + c + 1)
                    m()
                    if c:
                        unit_rows(g, c - 1)
                unit_rows(g, 3)
                dve.sem_inc(sem("y_rows_done"), 1)
                wait_full(dve, "yt", g)
                for c in range(2):
                    ins = ts(yT[:, c], bank("yt", g)[:, c * SEQ:(c + 1) * SEQ], cg("lnw", c),
                             cg("lnb", c), ALU.mult, ALU.add)
                out_of(ins, "yt", g)
                link(V.tensor_tensor(yT[:, :, :], yT[:, :, :], bon[:, :, :], ALU.add))
                mark(V.tensor_tensor(yT[:, :, :], yT[:, :, :], gT[:, :, :], ALU.mult), "y_f32", g + 1)
                dve.wait_ge(sem("yR_hi"), g + 1)
                mark(V.tensor_tensor(yR_lo[:, 2 * g:2 * g + 2, :], yT[:, :, :],
                                     yR_hi[:, 2 * g:2 * g + 2, :].bitcast(F32), ALU.subtract),
                     "yR_lo", g + 1)
            result(N_IN - 1)

            lo_piece(2 * T_OUT + 2)
            wait_read(dve, "lr", CT - 1)
            mark(ts(lr[:, :, :], lr[:, :, :], 0.5, 0.5, ALU.mult, ALU.add), "lr_sig", 1)
            wait_read(dve, "li", CT - 1)
            link(ts(li[:, :, :], li[:, :, :], 0.5, 0.5, ALU.mult, ALU.add))
            link(V.tensor_tensor(li[:, :, :], li[:, :, :], xc[:, :, :], ALU.mult))
            dve.wait_ge(sem("la_lt_done"), 1)
            link(V.tensor_tensor(lr[:, :, :], la[:, :, :], la[:, :, :], ALU.mult))
            mark(stt(lt[:, :, :], lr[:, :, :], 1.0, lt[:, :, :], ALU.add, ALU.mult), "om_done", 1)
            lo_piece(2 * T_OUT + 3)
            dve.wait_ge(sem("om_root"), 1)
            link(V.tensor_tensor(li[:, :, :], li[:, :, :], lt[:, :, :], ALU.mult))
            lo_piece(2 * T_OUT + 4)
            lo_piece(2 * T_OUT + 5)
            for c in range(CT):
                link(V.tensor_tensor_scan(lr[:, c], la[:, c], li[:, c], 0.0, ALU.mult, ALU.add))
            lo_piece(2 * T_OUT + 6)
            lo_piece(2 * T_OUT + 7)
            dve.wait_ge(sem("gelu_done"), 1)
            mark(V.tensor_tensor(lt[:, :, :], lr[:, :, :], gate[:, :, :], ALU.mult), "yL_f32", 1)
            dve.wait_ge(sem("yL_hi"), 1)
            mark(V.tensor_tensor(yL_lo[:, :, :], lt[:, :, :], yL_hi[:, :, :].bitcast(F32),
                                 ALU.subtract), "yL_lo", 1)
            for n in range(2 * T_OUT + 8, 2 * T_Q + 2):
                lo_piece(n)
            dve.wait_ge(sem("x2_in"), 16)
            dve.wait_ge(mm_done, 2 * T_Q)
            for i in range(8):
                xs = x2[:, i // 4, (i % 4) * 512:(i % 4 + 1) * 512]
                V.tensor_tensor(xs, xs, bank("out", i), ALU.add).then_inc(freed("out", i), 1)
                wait_read(dve, "out", i)
                dve.sem_inc(sem("x2_done"), 1)
            normalise(1, x2, h2)
            turned_lo(1, "h2", "x2", h2_tmp, "g2")
            for n in range(2 * T_Q + 2, 2 * T_U + 2):
                lo_piece(n)

            def top16(vals, idx, src, tmp):
                return [lambda: (link(V.max(vals[:, 0:8], src)),
                                 link(V.max_index(idx[:, 0:8], vals[:, 0:8], src))),
                        lambda: (link(V.match_replace(tmp, vals[:, 0:8], src, NEG)),
                                 link(V.max(vals[:, 8:16], tmp)),
                                 link(V.max_index(idx[:, 8:16], vals[:, 8:16], tmp)))]

            def head_steps(h, t):
                steps = []
                for p in range(2):
                    steps += top16(tk_sv[:, p], tk_si[:, p], sub[:, t, 2 * h + p, :], tk_s[:, :])

                def sums():
                    link(V.tensor_copy(sif[:, t, :, h, :], tk_si[:, :, :]))
                    link(V.tensor_tensor(
                        tk_cand[:, :, :], tk_sv[:, 0].unsqueeze(2).broadcast_to([P, TOPK, TOPK]),
                        tk_sv[:, 1].unsqueeze(1).broadcast_to([P, TOPK, TOPK]), ALU.add))

                def places():
                    link(ts(tk_ab[:, 0], tk_pos[:, :], 4, None, ALU.logical_shift_right))
                    link(ts(tk_ab[:, 1], tk_pos[:, :], 15, None, ALU.bitwise_and))
                    link(V.tensor_copy(abf[:, t, :, h, :], tk_ab[:, :, :]))

                steps.append(sums)
                steps += top16(best[:, t, h], tk_pos, tk_cand[:, :, :].rearrange("p a b -> p (a b)"),
                               tk_cand2[:, :])
                steps.append(places)
                return steps

            for t in range(NT2):
                for h in range(HEADS):
                    if h == 0 and t == 0:
                        for i in range(4):
                            wait_read(dve, "sub", N_Q - 4 + i)
                    for q, step in enumerate(head_steps(h, t)):
                        lo_piece(2 * T_U + 2 + 8 * (t * HEADS + h) + q)
                        step()

            def subtract_max():
                V.tensor_tensor(best[:, :, :, :], best[:, :, :, :],
                                best_max.broadcast_to([P, NT2, HEADS, TOPK]),
                                ALU.subtract).then_inc(sem("best_sub"), 1)

            steps = []
            for t in range(NT2):
                steps.append(lambda t=t: link(V.tensor_copy(sm[:, t], best[:, t, :, 0])))
                steps.append(lambda t=t: link(V.tensor_tensor(
                    best[:, t], best[:, t], sm[:, t].unsqueeze(2).broadcast_to([P, HEADS, TOPK]),
                    ALU.subtract)))
            steps.append(lambda: dve.sem_inc(sem("best_sub"), 1))
            for t in range(NT2):
                for p in range(2):
                    def one_hot(t=t, p=p):
                        link(V.tensor_tensor(
                            oneh[:, :, :],
                            abf[:, t, p].rearrange("p h k -> p (h k)").unsqueeze(2).broadcast_to(
                                [P, HEADS * TOPK, TOPK]),
                            iota[:, 0:TOPK].unsqueeze(1).broadcast_to([P, HEADS * TOPK, TOPK]),
                            ALU.is_equal))

                    def keys(t=t, p=p):
                        o4 = oneh[:, :, :].rearrange("p (h k) a -> p h k a", h=HEADS)
                        link(V.tensor_tensor(
                            o4, o4, sif[:, t, p].unsqueeze(2).broadcast_to([P, HEADS, TOPK, TOPK]),
                            ALU.mult))

                    def total(t=t, p=p):
                        link(V.tensor_reduce(sel[:, t, p], oneh[:, :, :], AX_X, ALU.add))

                    steps += [one_hot, keys, total]

            def softmax():
                dve.wait_ge(sem("best_exp"), 1)
                for t in range(NT2):
                    link(V.tensor_reduce(sm[:, t], best[:, t], AX_X, ALU.add))
                    link(V.reciprocal(sm[:, t], sm[:, t]))
                    link(V.tensor_tensor(
                        sel[:, t, 2].rearrange("p (h k) -> p h k", h=HEADS), best[:, t],
                        sm[:, t].unsqueeze(2).broadcast_to([P, HEADS, TOPK]), ALU.mult))
                dve.sem_inc(sem("sel_done"), 1)

            dve.wait_ge(sem("iota_in"), 16)
            first = 2 * T_U + 2 + 128
            last = 2 * (T_U + U_FIRST)
            for q in range(last - first):
                lo_piece(first + q)
                if q % 3 == 0 and q // 3 < len(steps):
                    steps[q // 3]()
                if q == last - first - 6:
                    softmax()
            assert (last - first - 6) // 3 >= len(steps)

            def u_body(it, tiles=NR):
                for n in range(2 * T_U, 2 * (T_U + tiles)):
                    dve.wait_ge(hi_done, it * (2 * NR) + (n + 1))
                    V.tensor_tensor(lo[n % NR][:, :], raw[n % NR][:, :], hi[n % NR][:, :].bitcast(F32),
                                    ALU.subtract).then_inc(lo_done, 1)

            with dve.Fori(U_FIRST // NR, N_U // NR) as it:
                u_body(it)
            u_body(N_U // NR, N_U % NR)

            for i in range(3):
                wait_read(dve, "idx", i)
            for t in range(T_V - NR, T_V):
                wait_read(dve, "tile", t)

            def one_a(it, q):
                b2, n2 = PLAN["gm", (q - 2) % 4]
                dve.wait_ge(full[b2], it + (FULLS["gm", (q - 2) % 4] - (1 if q < 2 else 0)))
                for k in range(4):
                    tok = it * 16 + (4 * q + k)
                    V.tensor_scalar(oneB[q % 2][:, k], iota[:, :], idxT[:, 1, bass.ds(tok, 1)], None,
                                    ALU.is_equal)
                    ins = V.tensor_scalar(oneA[q % 2][:, k], iota[:, :], idxT[:, 0, bass.ds(tok, 1)],
                                          idxT[:, 2, bass.ds(tok, 1)], ALU.is_equal, ALU.mult)
                ins.then_inc(sem("onehots_made"), 1)

            def gated(it, q):
                b, n = PLAN["gm", q % 4]
                dve.wait_ge(full[b], it + (FULLS["gm", q % 4] - (1 if q < 0 else 0)))
                v = actg[:, :, bass.ds(it * 16 + 4 * q, 4)].rearrange("p i t -> p t i")
                V.tensor_tensor(v, v, ps[:, b].rearrange("p (t i) -> p t i", t=4),
                                ALU.mult).then_inc(free[b], 1)

            def g_body(it, first=False):
                for q in range(4):
                    one_a(it, q)
                    if not (first and q == 0):
                        gated(it, q - 1)

            g_body(0, True)
            with dve.Fori(1, N_G // 4) as it:
                g_body(it)
            gated(N_G // 4, -1)
            for b in range(4):
                wait_read(dve, "gm", N_G - 4 + b)
            dve.sem_inc(sem("gated"), N_G)

            def v_body(it, tiles=NR):
                for b in range(tiles):
                    dve.wait_ge(sem("ahi_done"), it * NR + (b + 1))
                    V.tensor_tensor(a_lo[b][:, :], actg[:, bass.ds(it * NR + b, 1), :].rearrange(
                        "p a b -> p (a b)"), a_hi[b][:, :].bitcast(F32), ALU.subtract).then_inc(
                        sem("alo_done"), 1)
                    for n in (2 * (T_V + b), 2 * (T_V + b) + 1):
                        dve.wait_ge(hi_done, it * (2 * NR) + (n + 1))
                        V.tensor_tensor(lo[n % NR][:, :], raw[n % NR][:, :],
                                        hi[n % NR][:, :].bitcast(F32), ALU.subtract).then_inc(
                            lo_done, 1)

            with dve.Fori(0, N_V // NR) as it:
                v_body(it)
            v_body(N_V // NR, N_V % NR)

            dve.wait_ge(sem("xr_in"), 16)
            dve.wait_ge(sem("gf_in"), 16)
            dve.wait_ge(mm_done, 2 * (T_V + N_V))
            for t in range(NT2):
                for j in range(4):
                    xs = xr[:, t, j * 512:(j + 1) * 512]
                    link(V.tensor_tensor(xs, xs, bank("peer", 4 * t + j), ALU.add))
                V.tensor_tensor_reduce(out=junk[:, :], in0=xr[:, t], in1=xr[:, t], scale=1.0,
                                       scalar=0.0, op0=ALU.mult, op1=ALU.add,
                                       accum_out=ssq[:, t:t + 1]).then_inc(sem("ssq_done"), 1)
                dve.wait_ge(sem("ssq_done"), 4 + t + 1)
            for t in range(NT2):
                dve.wait_ge(sem("sd_done"), 2 + t + 1)
                link(V.reciprocal(rs[:, t:t + 1], sd[:, t:t + 1]))
                stt(xr[:, t], xr[:, t], rs[:, t:t + 1], gf[:, :], ALU.mult, ALU.mult).then_inc(
                    sem("y_done"), 1)

        @block.tensor
        def _(pe):
            def mm(o, lhsT, rhs, start, stop):
                return nc.tensor.matmul(o, lhsT, rhs, start=start, stop=stop, skip_group_check=True)

            def project(n, o):
                half = n % 2
                for k in range(8):
                    kc = 8 * half + k
                    wh, wl = (w[n % NR][:, k * P:(k + 1) * P] for w in (hi, lo))
                    mm(o, wh, hT_hi[:, kc], half == 0 and k == 0, False)
                    mm(o, wh, hT_lo[:, kc], False, False)
                    ins = mm(o, wl, hT_hi[:, kc], False, half == 1 and k == 7)
                ins.then_inc(mm_done, 1)

            def tile(t):
                wait_free(pe, "tile", t)
                for n in (2 * t, 2 * t + 1):
                    pe.wait_ge(lo_done, n + 1)
                    project(n, bank("tile", t)[:, 0:SEQ])

            def rows_out(n, half, act_hi, act_lo, banks, start, stop):
                for t in range(NT2):
                    ah, al = (x[:, t * P:(t + 1) * P] for x in (act_hi, act_lo))
                    for w, lhsT, s, e in ((hi[n % NR], ah, start, False), (lo[n % NR], ah, False, False),
                                          (hi[n % NR], al, False, stop)):
                        for j in range(2):
                            ins = mm(banks(4 * t + 2 * half + j), lhsT,
                                     w[:, j * 512:(j + 1) * 512], s, e)
                ins.then_inc(mm_done, 1)

            def turn(job, rows):
                for j in range(8):
                    wait_free(pe, job, j)
                    for c in range(2):
                        for t in range(NT2):
                            kc = 2 * j + c
                            ins = nc.tensor.transpose(
                                bank(job, j)[:, c * SEQ + t * P:c * SEQ + (t + 1) * P],
                                rows[:, t, kc * P:(kc + 1) * P], ident[:, :])
                    ins.then_inc(full[PLAN[job, j][0]], 1)

            pe.wait_ge(sem("ident_in"), 16)
            pe.wait_ge(sem("rows_done"), 1)
            turn("x1", h0)
            pe.wait_ge(sem("hT_done"), 1)
            for t in range(9):
                tile(t)
            for name in ("masks_in", "w2_in", "a2_in", "g2_in"):
                pe.wait_ge(sem(name), 16)
            pe.wait_ge(sem("identb_done"), 1)
            pe.wait_ge(sem("lora_done"), 1)
            for g in range(GROUPS):
                marks = list(MARKS[g])

                def m():
                    if marks:
                        tile(marks.pop(0))

                def job(name):
                    wait_free(pe, name, g)
                    return bank(name, g)

                def done(ins, name):
                    ins.then_inc(full[PLAN[name, g][0]], 1)

                def chans(c):
                    return slice((2 * g + c) * P, (2 * g + c + 1) * P)

                vv = rkv[g % 2][:, 2]
                m()
                o = job("zw")
                for c in range(2):
                    ins = mm(o[:, c * SEQ:(c + 1) * SEQ], wa2[0:64, chans(c)], lora[0:64, 0],
                             c == 0, c == 1)
                done(ins, "zw")
                o = job("za")
                for c in range(2):
                    ins = mm(o[:, c * SEQ:(c + 1) * SEQ], wa2[64:128, chans(c)], lora[64:128, 0],
                             c == 0, c == 1)
                done(ins, "za")
                o = job("gate")
                for c in range(2):
                    for k in range(2):
                        ins = mm(o[:, c * SEQ:(c + 1) * SEQ], g2[:, k, chans(c)], lora[:, 1 + k],
                                 c == 0 and k == 0, c == 1 and k == 1)
                done(ins, "gate")
                m()
                o = job("ss")
                pe.wait_ge(sem("sq_done"), g + 1)
                for c in range(2):
                    for t in range(NT2):
                        q = 2 * c + t
                        ins = mm(o[:, 2 * q:2 * q + 2], sq[:, c, t * P:(t + 1) * P], blk[:, 0:P:64],
                                 q == 0, q == 3)
                done(ins, "ss")
                m()
                o = job("kb")
                pe.wait_ge(sem("kn_done"), g + 1)
                for q in range(4):
                    ins = mm(o[:, q * P:(q + 1) * P],
                             sq[:, q // 2, (q % 2) * P:(q % 2 + 1) * P], ident[:, :], q == 0, q == 3)
                done(ins, "kb")
                m()
                o = job("bsum")
                pe.wait_ge(sem("rk_done"), g + 1)
                done(mm(o, blk, rk[:, :, :].rearrange("p c t -> p (c t)"), True, True), "bsum")
                for name, src in (("vt", vv), ("bt", bt), ("kt", kt)):
                    o = job(name)
                    if name == "bt":
                        pe.wait_ge(sem("bk_done"), g + 1)
                    for c in range(2):
                        for t in range(NT2):
                            q = 2 * c + t
                            ins = nc.tensor.transpose(o[:, q * P:(q + 1) * P],
                                                      src[:, c, t * P:(t + 1) * P], ident[:, :])
                    done(ins, name)
                pe.wait_ge(sem("ar_done"), g + 1)

                def add_identity(o4):
                    return mm(o4, identb[:, :], identb[:, :].unsqueeze(1).broadcast_to(
                        [P, o4.shape[1], P]), True, False)

                def scores(name, hl, src):
                    hp, c = slice(64 * (hl % 2), 64 * (hl % 2) + 64), hl // 2
                    o = job(name)
                    for t in range(NT2):
                        tok = slice(t * P, (t + 1) * P)
                        ins = mm(o[:, t * SEQ:(t + 1) * SEQ].rearrange("p (w q) -> p w q", w=2),
                                 src[hp, c, tok], ARt[hp, :, c, tok], t == 0, t == 1)
                    done(ins, name)

                for par in range(2):
                    for hl in (par, par + 2):
                        scores(f"m1_{hl}", hl, bt)
                        scores(f"m2_{hl}", hl, kt)
                    o = job(f"m3_{par}")
                    hp = slice(64 * par, 64 * par + 64)
                    for c in range(2):
                        for t in range(NT2):
                            tok = slice(t * P, (t + 1) * P)
                            q = 2 * c + t
                            ins = mm(o[:, q * P:(q + 1) * P], ARt[hp, 0, c, tok], bt[hp, c, tok],
                                     q == 0, q == 3)
                    done(ins, f"m3_{par}")
                m()
                pe.wait_ge(sem("first_inverse"), g + 1)
                for lv in range(1, 6):
                    for half in range(2):
                        o = job(f"y{lv}_{half}")
                        if lv > 1:
                            wait_read(pe, f"t{lv - 1}_{half}", g)
                        add_identity(o.rearrange("p (a q) -> p a q", a=4))
                        for q in range(4):
                            p = 4 * half + q
                            ins = mm(o[:, q * P:(q + 1) * P], L1[:, p, 0], Tm[:, p], False, q == 3)
                        done(ins, f"y{lv}_{half}")
                    for half in range(2):
                        wait_read(pe, f"y{lv}_{half}", g)
                        if lv > 1:
                            wait_read(pe, f"tt{lv - 1}_{half}", g)
                        if lv < 5:
                            o = job(f"t{lv}_{half}")
                            for q in range(4):
                                p = 4 * half + q
                                ins = mm(o[:, q * P:(q + 1) * P], TT[:, p], Ym[:, p], q == 0, q == 3)
                            done(ins, f"t{lv}_{half}")
                        o = job(f"tt{lv}_{half}")
                        for q in range(4):
                            p = 4 * half + q
                            ins = mm(o[:, q * P:(q + 1) * P], Ym[:, p], TT[:, p], q == 0, q == 3)
                        done(ins, f"tt{lv}_{half}")
                m()
                pe.wait_ge(sem("chain_zero"), g + 1)
                for name in ("vt", "bt", "kt", "tt5_0", "tt5_1"):
                    wait_read(pe, name, g)
                for c in range(4):
                    rows, t = slice(64 * (c % 2), 64 * (c % 2) + 64), c // 2
                    tok = slice(t * P, (t + 1) * P)
                    o = job(f"r{c}")
                    if c:
                        wait_read(pe, f"st{c - 1}", g)
                    for ct in range(2):
                        mm(o[:, ct * P:(ct + 1) * P], ARt[:, 0, ct, tok], ST[c % 2][:, ct], ct == 0, False)
                    for hl in range(4):
                        ins = mm(o[:, 64 * hl:64 * hl + 64], L2[:, 2 * hl + t, 0],
                                 Vt[:, hl // 2, t, 64 * (hl % 2):64 * (hl % 2) + 64], False, hl == 3)
                    done(ins, f"r{c}")
                    o = job(f"sa{c}")
                    wait_read(pe, f"r{c}", g)
                    for hl in range(4):
                        ins = mm(o[:, 64 * hl:64 * hl + 64], TT[:, 2 * hl + t], Rm[:, hl],
                                 hl == 0, hl == 3)
                    done(ins, f"sa{c}")
                    if c < 3:
                        o = job(f"st{c}")
                        mm(o[:, 0:256], ident[:, :], ST[c % 2][:, :, :].rearrange("p c q -> p (c q)"),
                           True, False)
                        wait_read(pe, f"sa{c}", g)
                        for ct in range(2):
                            mm(o[:, ct * P:(ct + 1) * P], Kt[rows, ct, t], Vt[rows, ct, t], False, False)
                            ins = mm(o[:, ct * P:(ct + 1) * P], Bt[rows, ct, t],
                                     SA[rows, t, 2 * ct:2 * ct + 2].rearrange("p a b -> p (a b)"),
                                     False, ct == 1)
                        done(ins, f"st{c}")
                    o = job(f"yc{c}")
                    if c == 3:
                        wait_read(pe, f"sa{c}", g)
                    for ct in range(2):
                        mm(o[:, ct * P:(ct + 1) * P], ARt[:, 1, ct, tok], ST[c % 2][:, ct], ct == 0, False)
                    for hl in range(4):
                        cols_h = slice(64 * hl, 64 * hl + 64)
                        mm(o[:, cols_h], L2[:, 2 * hl + t, 1],
                           Vt[:, hl // 2, t, 64 * (hl % 2):64 * (hl % 2) + 64], False, False)
                        ins = mm(o[:, cols_h], L1[:, 2 * hl + t, 1], SA[:, t, hl], False, hl == 3)
                    done(ins, f"yc{c}")
                    m()
                o = job("yt")
                pe.wait_ge(sem("y_rows_done"), g + 1)
                for c in range(2):
                    for t in range(NT2):
                        q = 2 * c + t
                        ins = nc.tensor.transpose(o[:, q * P:(q + 1) * P], y_tm[:, t, c], ident[:, :])
                done(ins, "yt")

            pe.wait_ge(sem("wa_in"), 16)
            pe.wait_ge(sem("wi_in"), 16)
            pe.wait_ge(sem("conv_done"), CT)
            for c in range(CT):
                for q, name in enumerate(("lr", "li")):
                    wait_free(pe, name, c)
                    mm(bank(name, c)[:, 0:SEQ], wai[:, q, c], xc[:, c], True, True).then_inc(
                        full[PLAN[name, c][0]], 1)

            for i in range(8):
                wait_free(pe, "out", i)
            pe.wait_ge(sem("yR_lo"), GROUPS)
            for c in range(N_OUT):
                yh, yl = (yR_hi, yR_lo) if c < CT else (yL_hi, yL_lo)
                if c == CT:
                    pe.wait_ge(sem("yL_lo"), 1)
                for half in range(2):
                    n = 2 * (T_OUT + c) + half
                    pe.wait_ge(lo_done, n + 1)
                    rows_out(n, half, yh[:, c % CT], yl[:, c % CT], lambda i: bank("out", i),
                             c == 0, c == N_OUT - 1)
            pe.wait_ge(sem("rows_done"), 2)
            turn("x2", h2)
            pe.wait_ge(sem("hT_done"), 2)

            pe.wait_ge(sem("keys_in"), 16)

            def key_scores(t):
                wait_free(pe, "sub", t)
                wait_read(pe, "tile", T_Q + t)
                for tt in range(NT2):
                    ins = mm(bank("sub", t)[:, tt * P:(tt + 1) * P], qT[t % 2][:, tt * P:(tt + 1) * P],
                             keysT[:, t], tt == 0, tt == 1)
                ins.then_inc(full[PLAN["sub", t][0]], 1)

            for t in range(N_Q):
                tile(T_Q + t)
                if t:
                    key_scores(t - 1)
            key_scores(N_Q - 1)

            def u_body(it, tiles=NR):
                for b in range(tiles):
                    pe.wait_ge(free[b], it + PLAN["tile", T_U + b][1])
                    for n in (2 * (T_U + b), 2 * (T_U + b) + 1):
                        pe.wait_ge(lo_done, it * (2 * NR) + (n + 1))
                        project(n, ps[:, b, 0:SEQ])

            with pe.Fori(0, U_FIRST // NR) as it:
                u_body(it)
            pe.wait_ge(sem("sel_done"), 1)
            for i in range(3):
                wait_free(pe, "idx", i)
                for t in range(NT2):
                    ins = nc.tensor.transpose(bank("idx", i)[:, t * P:(t + 1) * P], sel[:, t, i],
                                              ident[:, :])
                ins.then_inc(full[PLAN["idx", i][0]], 1)
            with pe.Fori(U_FIRST // NR, N_U // NR) as it:
                u_body(it)
            u_body(N_U // NR, N_U % NR)

            with pe.Fori(0, N_G // 4) as it:
                for q in range(4):
                    b, n = PLAN["gm", q]
                    pe.wait_ge(free[b], it + n)
                    pe.wait_ge(sem("onehots_made"), it * 4 + (q + 1))
                    for k in range(4):
                        ins = mm(ps[:, b, k * P:(k + 1) * P], oneB[q % 2][:, k], oneA[q % 2][:, k],
                                 k == 0, k == 3)
                    ins.then_inc(full[b], 1)

            for b in range(8):
                wait_free(pe, "peer", b)

            def v_body(it, tiles=NR, start=False, stop=False):
                for b in range(tiles):
                    pe.wait_ge(sem("alo_done"), it * NR + (b + 1))
                    for n in (2 * (T_V + b), 2 * (T_V + b) + 1):
                        pe.wait_ge(lo_done, it * (2 * NR) + (n + 1))
                        rows_out(n, n % 2, a_hi[b], a_lo[b], lambda i: ps[:, i], start and b == 0,
                                 stop and b == tiles - 1)

            v_body(0, start=True)
            with pe.Fori(1, N_V // NR) as it:
                v_body(it)
            v_body(N_V // NR, N_V % NR, stop=True)


def _consts():
    t, s = np.arange(P)[:, None], np.arange(P)[None, :]
    eye = np.eye(P)
    same = (t // CHUNK) == (s // CHUNK)

    def pairs(lv):
        return ((t >> (lv + 1)) == (s >> (lv + 1))) & ((t >> lv) % 2 == 1) & ((s >> lv) % 2 == 0)

    blk = ((t // 64) == (s // 64)).astype(np.float32)
    masks = [blk, blk / 64, same & (t < s), same & (t <= s), pairs(0), pairs(0).T]
    masks += [pairs(lv) + eye for lv in range(1, 6)]
    assert len(masks) == N_MASK
    reset = np.ones((P, 8, 65))
    reset[:, :, 0] = 0
    parts = [eye, np.broadcast_to(s, (P, P))] + masks + [reset.reshape(P, -1)]
    return np.ascontiguousarray(np.concatenate([np.asarray(q, np.float32) for q in parts], 1))


def _tiles(w):
    n = w.shape[1] // P
    return np.ascontiguousarray(w.reshape(2, 8, P, n, P).transpose(3, 0, 2, 1, 4)).reshape(
        n, 2, P, PIECE)


def _columns(v):
    v = np.asarray(v).reshape(-1)
    full_v = np.zeros((-(-v.size // P)) * P, v.dtype)
    full_v[:v.size] = v
    return full_v.reshape(-1, P).T


def kernel(**inputs):
    import concourse.bacc as _bacc
    from concourse import mybir as _mybir
    from concourse.bass_utils import run_bass_kernel_spmd as _run

    i = {k: np.asarray(v) for k, v in inputs.items()}
    w_in = i["w_in"][0]
    starts = {"xb": 0, "gate": D_LRU, "r": 2 * D_LRU, "k": 3 * D_LRU, "v": 4 * D_LRU, "lora": 5 * D_LRU}
    padded = np.zeros((D, N_IN * P), w_in.dtype)
    for t, (kind, c) in enumerate(ORDER):
        first = starts[kind] + c * P
        part = w_in[:, first:first + P]
        padded[:, t * P:t * P + part.shape[1]] = part
    g2 = np.zeros((2 * P, D_LRU), w_in.dtype)
    g2[:i["rwkv_g2"].shape[1]] = i["rwkv_g2"][0]
    source = {"g1": "norm1_g", "g2": "norm2_g", "conv_w": "conv_w", "conv_b": "conv_b", "ba": "lru_ba",
              "bi": "lru_bi", "lam": "lru_lambda", "mu": "rwkv_mu", "w0": "rwkv_w0", "a0": "rwkv_a0",
              "k_k": "rwkv_k_k", "k_a": "rwkv_k_a", "r_k": "rwkv_r_k", "lnw": "rwkv_lnx_w",
              "lnb": "rwkv_lnx_b"}
    arrays = {
        "x": i["x"], "w_in": _tiles(padded), "w_out": i["w_out"][0], "wq": _tiles(i["peer_wq"][0]),
        "peer_u": _tiles(i["peer_u"][0].T), "peer_v": i["peer_v"][0].reshape(NKEY, NKEY, D),
        "keys": np.ascontiguousarray(i["peer_keys"][0].transpose(3, 0, 1, 2)).reshape(
            P, 2 * HEADS, NKEY),
        "cols": np.ascontiguousarray(np.concatenate([_columns(i[source[n]]) for n in COLS], 1)),
        "consts": _consts(), "w2": i["rwkv_w2"][0], "a2": i["rwkv_a2"][0], "g2": g2,
        "lru_wa": i["lru_wa"][0], "lru_wi": i["lru_wi"][0], "normf_g": i["normf_g"],
    }
    nc = _bacc.Bacc("TRN2", target_bir_lowering=False, num_devices=1)
    aps, fed = {}, {}
    for name, arr in arrays.items():
        arr = np.ascontiguousarray(arr)
        fed[f"in_{name}"] = arr
        aps[name] = nc.dram_tensor(f"in_{name}", arr.shape, _mybir.dt.from_np(arr.dtype),
                                   kind="ExternalInput").ap()
    out = nc.dram_tensor("out_0", (1, SEQ, D), F32, kind="ExternalOutput").ap()
    hybrid_layer_kernel(nc, aps, out)
    r = _run(nc, [fed], core_ids=[0])
    return r.results[0]["out_0"]
```

```python
from contextlib import ExitStack

import numpy as np

import concourse.bass as bass
from concourse import mybir

F32 = mybir.dt.float32
F32R = mybir.dt.float32r
U32 = mybir.dt.uint32
BF16 = mybir.dt.bfloat16
ALU = mybir.AluOpType
ACT = mybir.ActivationFunctionType
AX_X = mybir.AxisListType.X

P = 128
SEQ = 256
NT2 = SEQ // P
D = 2048
KC = D // P
PIECE = 1024
D_LRU = 1024
CT = D_LRU // P
LORA_TILES = 3
GROUPS = 4
CHUNK = 64
NKEY = 128
HEADS = 8
TOPK = 16
NR = 5
EPS = 1e-6
GN_EPS = 64e-5
NEG = -3.0e38
EXPM = float(np.exp(-0.5))

COLS = {}
_at = 0
for _name, _n in (("g1", KC), ("g2", KC), ("conv_w", 4 * CT), ("conv_b", CT), ("ba", CT), ("bi", CT),
                  ("lam", CT), ("mu", 27), ("w0", CT), ("a0", CT), ("k_k", CT), ("k_a", CT),
                  ("r_k", CT), ("lnw", CT), ("lnb", CT)):
    COLS[_name] = (_at, _n)
    _at += _n
NCOL = _at

def w_in_order():
    def group(g):
        return [(kind, 2 * g + c) for kind in "rkv" for c in range(2)]
    lru = [(kind, c) for c in range(CT) for kind in ("xb", "gate")]
    order = [("lora", i) for i in range(LORA_TILES)] + group(0)
    for g in range(1, GROUPS):
        order += group(g) + lru[3 * (g - 1):3 * g]
    return order + lru[9:]


ORDER = w_in_order()
N_IN = len(ORDER)
N_OUT = KC
N_Q = KC
N_U = NKEY
N_V = NKEY
T_OUT = N_IN
T_Q = T_OUT + N_OUT
T_U = T_Q + N_Q
T_V = T_U + N_U
N_MASK = 10
N_POOL = 2 * T_OUT + 11
TOPK_TILE = 95
ROOM = [{0, 1, 2, 3, 4, 6, 7, 8, 9}] * 3 + [{2, 3, 4, 6, 7, 8, 9}]
SUM_ORDER = [(t, 2 * half + j) for half in range(2) for t in range(NT2) for j in range(2)]
U_EXP = 50
U_FIRST = 65

I_EARLY = 64
N_LATE = NKEY - I_EARLY
N_G2 = SEQ // 2
N_G4 = SEQ // 4
LATE_BANK = {-1: 5, 0: 4, 1: 5, 2: 6, 3: 7, 4: 5}
SHIFTED = [t for t, (kind, _) in enumerate(ORDER) if kind in ("lora", "r", "k", "v")]
MU = {t: {"r": 0, "k": CT, "v": 2 * CT, "lora": 3 * CT}[ORDER[t][0]] + ORDER[t][1] for t in SHIFTED}
MARKS = [range(9, 18), range(18, 27), range(27, 36), range(36, N_IN)]

RWKV_JOBS = ["zw", "za", "gate", "ss", "kb", "bsum", "vt", "bt", "kt",
             "m1_0", "m2_0", "m1_2", "m2_2", "m3_0", "m1_1", "m2_1", "m1_3", "m2_3", "m3_1"]
for _lv in range(1, 6):
    RWKV_JOBS += [f"y{_lv}_0", f"y{_lv}_1"]
    for _half in range(2):
        RWKV_JOBS += [f"{_kind}{_lv}_{_half}" for _kind in (("t", "tt") if _lv < 5 else ("tt",))]
RWKV_JOBS += ["r0", "yc0", "st0", "sa0", "r1", "st1", "sa1", "r2", "yc1", "st2", "sa2", "r3", "sa3"]
RWKV_JOBS += ["yt"]


def psum_plan():
    names = [("x1", i, i % 8) for i in range(8)]
    ring = 0
    for t in range(9):
        names.append(("tile", t, t % 2))
    for g in range(GROUPS):
        for t in MARKS[g]:
            names.append(("tile", t, t % 2))
        for job in RWKV_JOBS:
            if job in ("r1", "r3"):
                names.append((job, g, shared))
                continue
            if job in ("r0", "r2"):
                shared = 2 + ring % 6
            names.append((job, g, 2 + ring % 6))
            ring += 1
    for c in range(CT):
        names.append(("lru", c, (2, 3, 6, 7)[c % 4]))
    names += [("out", i, i) for i in range(8)]
    names += [("x2", i, i) for i in range(8)]
    for t in range(N_Q):
        names.append(("tile", T_Q + t, (T_Q + t) % 2))
        names.append(("sub", t, 2 + t % 4))
    for t in range(N_U):
        names.append(("tile", T_U + t, t % NR))
    for i in range(3):
        names.append(("idx", i, NR + i))
    names += [("peer", i, i) for i in range(8)]
    uses, plan = [0] * 8, {}
    for name, i, bank in names:
        plan[name, i] = (bank, uses[bank])
        uses[bank] += 1
    return plan


PLAN = psum_plan()


def full_counts():
    counts, out = [0] * 8, {}
    for (name, i), (bank, _) in PLAN.items():
        if name not in ("tile", "out", "peer"):
            counts[bank] += 1
            out[name, i] = counts[bank]
    return out


FULLS = full_counts()


def hybrid_layer_kernel(nc, a, out):
    ctx = ExitStack()
    with ctx:
        sems = {}

        def sem(name):
            if name not in sems:
                sems[name] = ctx.enter_context(nc.semaphore(name))
            return sems[name]

        base = [16512]

        def at(name, shape, dt, offset):
            return nc.alloc_sbuf_tensor_at(name, shape, dt, offset=offset)

        def place(name, shape, dt=F32):
            size = 4 * int(np.prod(shape[1:]))
            t = at(name, shape, dt, base[0])
            base[0] += (size + 31) // 32 * 32
            return t

        raw_at = base[0]
        raw = [place(f"raw{i}", [P, PIECE]) for i in range(NR)]
        lo = [at(f"lo{i}", [P, PIECE], F32R, raw_at + 4 * PIECE * i) for i in range(NR)]
        hi = [place(f"hi{i}", [P, PIECE], F32R) for i in range(NR)]
        hT_at = base[0]
        hT_hi = place("hT_hi", [P, KC, SEQ], F32R)
        hT_lo = place("hT_lo", [P, KC, SEQ], F32R)
        cols_at = base[0]
        cols = place("cols", [P, NCOL])
        ident = place("ident", [P, P])
        iota = place("iota", [P, P])
        scal = place("scal", [P, 64])
        idx_at = base[0]
        idxT = place("idxT", [P, 3, SEQ])
        xpad = at("xpad", [P, SEQ + 3], F32, idx_at + 1024)
        diag = [at(f"diag{i}", [P, P], F32, idx_at + o) for i, o in enumerate((448, 2080))]
        mshift_at = base[0]
        mshift = [place(f"mshift{i}", [P, 1 + SEQ]) for i in range(2)]
        ARENA = (base[0] + 31) // 32 * 32
        ARENA_F = 32768
        end = ARENA + 4 * ARENA_F
        identb = at("identb", [P, P], BF16, end)
        assert end + 256 <= nc.sbuf_usable_end, (end, nc.sbuf_usable_end)

        def ar(name, first, shape, dt=F32):
            assert first + int(np.prod(shape[1:])) <= ARENA_F, name
            return at(name, shape, dt, ARENA + 4 * first)

        actg = ar("actg", 0, [P, NKEY, SEQ])

        f = [0]

        def nx(name, shape, dt=F32):
            t = ar(name, f[0], shape, dt)
            f[0] += int(np.prod(shape[1:]))
            return t

        masks = nx("masks", [P, N_MASK, P])
        blk, mU, m0, m0T = masks[:, 0], masks[:, 1:3], masks[:, 3], masks[:, 4]
        d0scan = nx("d0scan", [P, 8 * 65])
        wa2 = nx("wa2", [P, D_LRU])
        g2 = nx("g2", [P, 2, D_LRU])
        wai = nx("wai", [P, 2, CT, P])
        xc = nx("xc", [P, CT, SEQ])
        gate = nx("gate", [P, CT, SEQ])
        yR_hi = nx("yR_hi", [P, CT, SEQ], F32R)
        yR_lo = nx("yR_lo", [P, CT, SEQ], F32R)
        rkv = [nx(f"rkv{i}", [P, 3, 2, SEQ]) for i in range(2)]
        lora = nx("lora", [P, 3, SEQ])
        group_at = f[0]
        w65 = nx("w65", [P, 8, 65])
        aT = nx("aT", [P, 2, SEQ])
        inv_at = f[0]
        iP = nx("iP", [P, 2, SEQ])
        kk = nx("kk", [P, 2, SEQ])
        k2 = nx("k2", [P, 2, SEQ])
        bb = nx("bb", [P, 2, SEQ])
        sq = nx("sq", [P, 2, SEQ])
        gT = nx("gT", [P, 2, SEQ])
        P65 = nx("P65", [P, 8, 65])
        ARt = nx("ARt", [P, 2, 2, SEQ])
        ym_at = f[0]
        bt = nx("bt", [P, 2, SEQ])
        kt = nx("kt", [P, 2, SEQ])
        rk = nx("rk", [P, 2, SEQ])
        bon = nx("bon", [P, 2, SEQ])
        Vt = nx("Vt", [P, 2, NT2, P])
        Bt = nx("Bt", [P, 2, NT2, P])
        Kt = nx("Kt", [P, 2, NT2, P])
        L1 = nx("L1", [P, 8, 2, P])
        L2 = nx("L2", [P, 8, 2, P])
        ST1 = nx("ST1", [P, 2, P])
        kn = nx("kn", [P, 8])
        gsum, gvar, gsd = (nx(name, [P, NT2, 4]) for name in ("gsum", "gvar", "gsd"))
        Tm = ar("Tm", inv_at, [P, 8, P])
        TT = ar("TT", inv_at + 1024, [P, 8, P])
        Ym = ar("Ym", ym_at, [P, 8, P])
        Rm = ar("Rm", group_at, [P, 4, 64])
        SA = ar("SA", group_at + 256, [P, NT2, 4, 64])
        ST = [ar("ST0", group_at + 768, [P, 2, P]), ST1]
        y_tm = ar("y_tm", inv_at, [P, NT2, 2, P])
        yT = ar("yT", inv_at + 512, [P, 2, SEQ])
        ysq = ar("ysq", ym_at, [P, 4, 64])
        x_sb = ar("x_sb", group_at, [P, NT2, D])
        x_sq = ar("x_sq", group_at + 4096, [P, NT2, D])
        yL_hi = ar("yL_hi", group_at, [P, CT, SEQ], F32R)
        yL_lo = ar("yL_lo", group_at + 2048, [P, CT, SEQ], F32R)
        lr = ar("lr", group_at + 4096, [P, CT, SEQ])
        li = ar("li", group_at + 6144, [P, CT, SEQ])
        la = ar("la", group_at + 8192, [P, CT, SEQ])
        lt = ar("lt", group_at + 10240, [P, CT, SEQ])
        x2 = ar("x2", 0, [P, NT2, D])
        x2_sq = ar("x2_sq", 4096, [P, 8, 512])
        keysT = ar("keysT", 20480, [P, 2 * HEADS, NKEY])
        TK = TOPK_TILE * SEQ
        qT = [ar(f"qT{i}", TK + i * SEQ, [P, SEQ]) for i in range(2)]
        tk_s = ar("tk_s", TK + 512, [P, P])
        tk_cand = ar("tk_cand", TK + 640, [P, TOPK, TOPK])
        tk_cand2 = ar("tk_cand2", TK + 896, [P, TOPK * TOPK])
        tk_sv = ar("tk_sv", TK + 1152, [P, 2, TOPK])
        tk_si = ar("tk_si", TK + 1184, [P, 2, TOPK], U32)
        tk_pos = ar("tk_pos", TK + 1216, [P, TOPK], U32)
        tk_ab = ar("tk_ab", TK + 1232, [P, 2, TOPK], U32)
        sif = ar("sif", TK + 1280, [P, NT2, 2, HEADS, TOPK])
        abf = ar("abf", TK + 1792, [P, NT2, 2, HEADS, TOPK])
        best = ar("best", TK + 2304, [P, NT2, HEADS, TOPK])
        sel = ar("sel", TK + 2560, [P, NT2, 3, HEADS * TOPK])
        sm = ar("sm", TK + 3328, [P, NT2, HEADS])
        sub = ar("sub", TK + 4096, [P, NT2, 2 * HEADS, P])
        oneh = ar("oneh", TK + 4096, [P, HEADS * TOPK, TOPK])
        assert nc.sbuf_usable_end - end >= 768
        parts = at("parts", [P, 3, SEQ], BF16, mshift_at)
        oneI = [at(f"oneI{i}", [P, 2, I_EARLY], BF16, mshift_at + 1536 + 256 * i) for i in range(2)]
        oneJ = [at(f"oneJ{i}", [P, 2, P], BF16, idx_at + 2048 + 512 * i) for i in range(2)]
        oneG = [at(f"oneG{i}", [P, 2, 3, I_EARLY], BF16, o) for i, o in enumerate((cols_at, end))]
        rest = ar("rest", TK, [P, SEQ])
        oneJ4 = [at(f"oneJ4_{i}", [P, 4, P], BF16, hT_at + 1024 * i) for i in range(3)]
        oneI4 = [at(f"oneI4_{i}", [P, 4, NKEY - I_EARLY], BF16, hT_at + 3072 + 512 * i)
                 for i in range(3)]
        oneG4 = [at(f"oneG4_{i}", [P, 4, 3, NKEY - I_EARLY], BF16, hT_at + 4608 + 1536 * i)
                 for i in range(3)]
        a_hi = [at(f"a_hi{i}", [P, SEQ], F32R, hT_at + 9728 + 1024 * i) for i in range(NR)]
        a_lo = [at(f"a_lo{i}", [P, SEQ], F32R, hT_at + 14848 + 1024 * i) for i in range(NR)]
        xr = ar("xr", 0, [P, NT2, D])
        gf = ar("gf", 4096, [P, D])
        xr_sq = ar("xr_sq", 6144, [P, 8, 512])

        ps = ctx.enter_context(nc.psum_tensor("ps", [P, 8, 512], F32))
        x2_dram = nc.dram_tensor("x2_spill", (P, NT2 * D), F32, kind="Internal").ap()

        full = [sem(f"bank_full{i}") for i in range(8)]
        free = [sem(f"bank_free{i}") for i in range(8)]
        raw_in = [sem(f"raw_in{i}") for i in range(NR)]
        hi_done, lo_done, mm_done = sem("hi_done"), sem("lo_done"), sem("mm_done")
        block = ctx.enter_context(nc.Block())

        def col(name, i=0, n=1):
            first = COLS[name][0] + i
            return cols[:, first:first + n]

        def colr(name):
            return col(name, 0, COLS[name][1])

        rs, ssq, sd = scal[:, 0:2], scal[:, 2:4], scal[:, 4:6]
        hw0, ha0, hba, hbi, nsp = (scal[:, 6 + 8 * i:14 + 8 * i] for i in range(5))
        eps_c, gneps_c, ssq8 = scal[:, 46:47], scal[:, 47:48], scal[:, 48:56]
        omu, oka, psp = idxT[:, 0, 0:27], idxT[:, 0, 32:40], idxT[:, 0, 40:48]
        sp = [idxT[:, 0, 48 + 8 * i:56 + 8 * i] for i in range(7)]

        def bank(name, i):
            return ps[:, PLAN[name, i][0]]

        def freed(name, i):
            return free[PLAN[name, i][0]]

        def wait_full(eng, name, i):
            b, n = PLAN[name, i]
            if name == "tile":
                eng.wait_ge(mm_done, 2 * i + 2)
            else:
                eng.wait_ge(full[b], FULLS[name, i])

        def wait_free(eng, name, i):
            b, n = PLAN[name, i]
            if n:
                eng.wait_ge(free[b], n)

        def wait_read(eng, name, i):
            b, n = PLAN[name, i]
            eng.wait_ge(free[b], n + 1)

        def wait_raw(eng, n, it=0, step=2 * NR):
            eng.wait_ge(raw_in[n % NR], it * (16 * step // NR) + 16 * (n // NR + 1))

        def wait_slot(eng, n, it=0, step=2 * NR):
            eng.wait_ge(mm_done, it * step + (n - NR + 1))

        def dest(t):
            kind, c = ORDER[t]
            if kind == "lora":
                return lora[:, c]
            return rkv[(c // 2) % 2][:, "rkv".index(kind), c % 2]

        @block.sync
        def _(sync):
            xv = a["x"].rearrange("o (t p) d -> p (o t) d", p=P)
            for t in range(NT2):
                sync.dma_start(x_sb[:, t], xv[:, t]).then_inc(sem(f"x_in{t}"), 16)

            def load(n, src):
                if n >= NR:
                    sync.wait_ge(mm_done, n - NR + 1)
                sync.dma_start(raw[n % NR][:, :], src).then_inc(raw_in[n % NR], 16)

            for n in range(2 * N_IN):
                load(n, a["w_in"][n // 2, n % 2])
            for c in range(N_OUT):
                ch = (c + CT) % KC
                for half in range(2):
                    load(2 * (T_OUT + c) + half,
                         a["w_out"][ch * P:(ch + 1) * P, half * PIECE:(half + 1) * PIECE])
            for t in range(N_Q):
                for half in range(2):
                    load(2 * (T_Q + t) + half, a["wq"][t, half])
            def load_in_loop(n, src, it, step):
                wait_slot(sync, n, it, step)
                sync.dma_start(raw[n % NR][:, :], src).then_inc(raw_in[n % NR], 16)

            def u_load(it, tiles=NR):
                for q in range(2 * tiles):
                    load_in_loop(2 * T_U + q, a["peer_u"][it * NR + q // 2, q % 2], it, 2 * NR)

            def v_row(i, half):
                return a["peer_v"][i, :, half * PIECE:(half + 1) * PIECE]

            with sync.Fori(0, N_U // NR) as it:
                u_load(it)
            u_load(N_U // NR, N_U % NR)
            for half in range(2):
                first = 2 * T_V + half * I_EARLY
                with sync.Fori(0, I_EARLY // NR) as it:
                    for b in range(NR):
                        load_in_loop(first + b, v_row(it * NR + b, half), it, NR)
                for i in range(I_EARLY // NR * NR, I_EARLY):
                    load(first + i, v_row(i, half))
            first = 2 * (T_V + I_EARLY)
            with sync.Fori(0, N_LATE // NR) as it:
                for q in range(2 * NR):
                    load_in_loop(first + q, v_row(it * NR + (I_EARLY + q // 2), q % 2), it, 2 * NR)
            for i in range(N_LATE // NR * NR, N_LATE):
                for half in range(2):
                    load(first + 2 * i + half, v_row(I_EARLY + i, half))
            outv = out.rearrange("o (t p) d -> p (o t) d", p=P)
            for q in range(4):
                part = slice((q % 2) * PIECE, (q % 2 + 1) * PIECE)
                sync.wait_ge(sem("y_done"), q + 1)
                sync.dma_start(outv[:, q // 2, part], xr[:, q // 2, part]).then_inc(sem("out_sent"), 16)
            sync.wait_ge(sem("out_sent"), 64)

        @block.gpsimd
        def _(pool):
            pool.dma_start(ident[:, :], a["consts"][:, 0:P]).then_inc(sem("ident_in"), 16)
            pool.dma_start(cols[:, :], a["cols"]).then_inc(sem("cols_in"), 16)
            pool.dma_start(wa2[0:64, :], a["w2"]).then_inc(sem("w2_in"), 16)
            pool.dma_start(wa2[64:128, :], a["a2"]).then_inc(sem("a2_in"), 16)
            pool.dma_start(g2[:, :, :], a["g2"].rearrange("(k p) c -> p k c", p=P)).then_inc(
                sem("g2_in"), 16)
            m_end = (2 + N_MASK) * P
            pool.dma_start(masks[:, :, :], a["consts"][:, 2 * P:m_end].rearrange(
                "p (m q) -> p m q", q=P)).then_inc(sem("masks_in"), 16)
            pool.dma_start(d0scan[:, :], a["consts"][:, m_end:m_end + 520]).then_inc(
                sem("scan_in"), 16)
            pool.dma_start(wai[:, 0], a["lru_wa"].rearrange("h i j -> i h j")).then_inc(
                sem("wa_in"), 16)
            pool.dma_start(wai[:, 1], a["lru_wi"].rearrange("h i j -> i h j")).then_inc(
                sem("wi_in"), 16)
            pool.dma_start(iota[:, :], a["consts"][:, P:2 * P]).then_inc(sem("iota_in"), 16)
            for n in range(N_POOL):
                pool.wait_ge(hi_done, n + 1)
                nc.gpsimd.tensor_tensor(lo[n % NR][:, :], raw[n % NR][:, :],
                                        hi[n % NR][:, :].bitcast(F32), ALU.subtract).then_inc(lo_done, 1)
            pool.wait_ge(sem("yR_lo"), GROUPS)
            pool.dma_start(x2[:, :, :], a["x"].rearrange("o (t p) d -> p (o t) d", p=P)).then_inc(
                sem("x2_in"), 16)
            for i in range(8):
                wait_read(pool, "out", i)
            pool.dma_start(keysT[:, :, :], a["keys"]).then_inc(sem("keys_in"), 16)
            pool.dma_start(x2_dram, x2[:, :, :].rearrange("p t d -> p (t d)")).then_inc(
                sem("x2_out"), 16)
            pool.wait_ge(sem("x2_out"), 16)

            def scaled(made, used, tok, count, one_i, one_g):
                pool.wait_ge(sem("onehots_made"), made)
                if used is not None:
                    pool.wait_ge(sem("gates_made"), used)
                shape = [P, count, 3, I_EARLY]
                nc.gpsimd.tensor_tensor(
                    one_g[:, :, :, :], one_i[:, :, :].unsqueeze(2).broadcast_to(shape),
                    parts[:, :, bass.ds(tok, count)].rearrange("p k t -> p t k").unsqueeze(
                        3).broadcast_to(shape), ALU.mult).then_inc(sem("gates_scaled"), 1)

            def early_scaled(it, r):
                early = isinstance(it, int) and it * (2 * NR) + (r - 2 * U_FIRST) < 2
                scaled(it * (2 * NR) + (r - 2 * U_FIRST + 1),
                       None if early else it * (2 * NR) + (r - 2 * U_FIRST - 1),
                       it * (4 * NR) + (2 * r - 4 * U_FIRST), 2, oneI[r % 2], oneG[r % 2])

            def late_scaled(it, b):
                early = isinstance(it, int) and it * NR + b < 2
                scaled(it * NR + (N_G2 + b + 1), None if early else it * NR + (N_G2 + b - 1),
                       it * (4 * NR) + 4 * b, 4, oneI4[b % 3], oneG4[b % 3])

            for r in range(2 * NR):
                early_scaled(U_FIRST // NR, r)
            with pool.Fori(U_FIRST // NR + 1, N_U // NR) as it:
                for r in range(2 * NR):
                    early_scaled(it, r)
            for r in range(2 * (N_U % NR) + 2):
                early_scaled(N_U // NR, r)
            for b in range(NR):
                late_scaled(0, b)
            with pool.Fori(1, I_EARLY // NR) as it:
                for b in range(NR):
                    late_scaled(it, b)
            for b in range(I_EARLY % NR):
                late_scaled(I_EARLY // NR, b)
            xr_flat = xr[:, :, :].rearrange("p t d -> p (t d)")
            for q in range(8):
                pool.wait_ge(sem("alo_done"), 2 * I_EARLY + 2 + 4 * q)
                pool.dma_start(xr_flat[:, q * 512:(q + 1) * 512],
                               x2_dram[:, q * 512:(q + 1) * 512]).then_inc(sem("xr_in"), 16)
            for q in range(4):
                pool.wait_ge(sem("alo_done"), 2 * I_EARLY + 34 + 4 * q)
                pool.dma_start(gf[:, q * 512:(q + 1) * 512],
                               a["normf_g"][q * 512:(q + 1) * 512].partition_broadcast(P)).then_inc(
                    sem("gf_in"), 16)

        @block.scalar
        def _(act):
            def mark(ins, name, value):
                ins.then_inc(sem(name), 1)
                act.wait_ge(sem(name), value)

            def hi_piece(n, it=0, step=2 * NR):
                wait_raw(act, n, it, step)
                if n >= NR:
                    wait_slot(act, n, it, step)
                nc.scalar.activation(hi[n % NR][:, :], raw[n % NR][:, :], ACT.Copy).then_inc(hi_done, 1)

            def norm_root(i):
                act.wait_ge(sem("ssq_done"), i + 1)
                nc.scalar.activation(sd, ssq, ACT.Sqrt, scale=1.0 / D, bias=eps_c).then_inc(
                    sem("sd_done"), 1)

            def squares(x, sq_out, wait_sum):
                for q, (t, j) in enumerate(SUM_ORDER):
                    wait_sum(q, t, j)
                    nc.scalar.activation(sq_out[:, q], x[:, t, j * 512:(j + 1) * 512], ACT.Square,
                                         accum_out=ssq8[:, 4 * t + j:4 * t + j + 1]).then_inc(
                        sem("squares_done"), 1)

            def turned_hi(job, gain):
                for j in range(8):
                    wait_full(act, job, j)
                    for c in range(2):
                        ins = nc.scalar.activation(hT_hi[:, 2 * j + c], bank(job, j)[
                            :, c * SEQ:(c + 1) * SEQ], ACT.Copy, scale=col(gain, 2 * j + c))
                    ins.then_inc(sem(f"{job}_hi"), 1)

            act.wait_ge(sem("consts_done"), 1)
            nc.scalar.activation(scal[:, 63:64], eps_c, ACT.Sqrt)
            act.wait_ge(sem("x_in1"), 16)
            nc.scalar.activation(x_sq[:, 1], x_sb[:, 1], ACT.Square,
                                 accum_out=ssq[:, 1:2]).then_inc(sem("square1_done"), 1)
            norm_root(0)
            act.wait_ge(sem("lam_abs"), 1)
            nc.scalar.activation(sp[1], sp[0], ACT.Exp, scale=-1.0).then_inc(sem("lam_exp"), 1)
            act.wait_ge(sem("lam_u"), 1)
            nc.scalar.activation(sp[3], sp[2], ACT.Ln).then_inc(sem("lam_ln"), 1)
            hi_piece(0)
            hi_piece(1)
            act.wait_ge(sem("cols_in"), 16)
            turned_hi("x1", "g1")

            def result(t):
                kind, c = ORDER[t]
                wait_full(act, "tile", t)
                pb = bank("tile", t)[:, 0:SEQ]
                if kind == "xb":
                    if c:
                        act.wait_ge(sem("conv_done"), c)
                    nc.scalar.activation(xpad[:, 3:3 + SEQ], pb, ACT.Copy).then_inc(freed("tile", t), 1)
                elif kind == "gate":
                    nc.scalar.activation(gate[:, c], pb, ACT.Gelu_apprx_tanh).then_inc(
                        freed("tile", t), 1)
                else:
                    q = SHIFTED.index(t)
                    if q >= 2:
                        wait_read(act, "tile", SHIFTED[q - 2])
                    nc.scalar.activation(mshift[q % 2][:, 1:1 + SEQ], pb, ACT.Copy,
                                         scale=col("mu", MU[t])).then_inc(sem("mu_done"), 1)

            def tile(t):
                hi_piece(2 * t + 2)
                hi_piece(2 * t + 3)
                if t:
                    result(t - 1)

            for t in range(9):
                tile(t)
                if t == 3:
                    wait_read(act, "tile", 2)
                    nc.scalar.activation(lora[0:64, 0], lora[0:64, 0], ACT.Tanh).then_inc(
                        sem("lora_act"), 1)
                    nc.scalar.activation(lora[:, 1:3], lora[:, 1:3], ACT.Tanh, scale=0.5).then_inc(
                        sem("lora_act"), 1)
            for g in range(GROUPS):
                marks = list(MARKS[g])

                def m(step):
                    if step in ROOM[g]:
                        tile(marks.pop(0))

                m(0)
                act.wait_ge(sem("w65_ready"), g + 1)
                wait_full(act, "zw", g)
                for c in range(2):
                    ins = nc.scalar.activation(
                        w65[:, 4 * c:4 * c + 4, 1:65],
                        bank("zw", g)[:, c * SEQ:(c + 1) * SEQ].rearrange("p (k t) -> p k t", t=CHUNK),
                        ACT.Tanh, scale=0.5, bias=hw0[:, 2 * g + c:2 * g + c + 1])
                ins.then_inc(freed("zw", g), 1)
                wait_full(act, "za", g)
                for c in range(2):
                    ins = nc.scalar.activation(aT[:, c], bank("za", g)[:, c * SEQ:(c + 1) * SEQ],
                                               ACT.Tanh, scale=0.5, bias=ha0[:, 2 * g + c:2 * g + c + 1])
                ins.then_inc(freed("za", g), 1)
                wait_full(act, "gate", g)
                nc.scalar.activation(gT[:, :, :].rearrange("p c t -> p (c t)"), bank("gate", g),
                                     ACT.Copy).then_inc(freed("gate", g), 1)
                act.wait_ge(sem("scan_done"), g + 1)
                nc.scalar.activation(iP[:, :, :].rearrange("p c (k t) -> p (c k) t", t=CHUNK),
                                     P65[:, :, 1:65], ACT.Exp, scale=0.5 * EXPM).then_inc(
                    sem("ip_done"), 1)
                act.wait_ge(sem("ip_done"), g + 1)
                nc.scalar.activation(P65[:, :, :], P65[:, :, :], ACT.Exp, scale=-0.5 * EXPM).then_inc(
                    sem("p_done"), 1)
                m(1)
                wait_full(act, "ss", g)
                nc.scalar.activation(kn[:, :], bank("ss", g)[:, 0:8], ACT.Sqrt).then_inc(
                    freed("ss", g), 1)
                m(2)
                m(3)
                for name, dst in (("vt", Vt), ("bt", Bt), ("kt", Kt)):
                    wait_full(act, name, g)
                    nc.scalar.activation(dst[:, :, :, :].rearrange("p c k t -> p (c k t)"),
                                         bank(name, g), ACT.Copy).then_inc(freed(name, g), 1)
                m(4)
                for lv in range(1, 6):
                    for half in range(2):
                        for name, dst in (("t", Tm), ("tt", TT)):
                            job = f"{name}{lv}_{half}"
                            if (job, g) not in PLAN:
                                continue
                            wait_full(act, job, g)
                            nc.scalar.activation(
                                dst[:, 4 * half:4 * half + 4].rearrange("p a b -> p (a b)"),
                                bank(job, g), ACT.Copy).then_inc(freed(job, g), 1)
                for c in range(4):
                    rows = slice(64 * (c % 2), 64 * (c % 2) + 64)
                    wait_full(act, f"r{c}", g)
                    act.wait_ge(sem("chain_zero"), g + 1)
                    nc.scalar.activation(Rm[rows, :, :].rearrange("p a b -> p (a b)"),
                                         bank(f"r{c}", g)[rows, 0:256], ACT.Copy).then_inc(
                        freed(f"r{c}", g), 1)
                    m(6 + c)
                    if c % 2:
                        act.wait_ge(sem("gvar_done"), 2 * g + c // 2 + 1)
                        nc.scalar.activation(gsd[:, c // 2], gvar[:, c // 2], ACT.Sqrt, scale=1.0 / 64,
                                             bias=gneps_c).then_inc(sem("gsd_done"), 1)
                if g == GROUPS - 1:
                    result(N_IN - 1)
                act.wait_ge(sem("y_f32"), g + 1)
                nc.scalar.activation(yR_hi[:, 2 * g:2 * g + 2, :], yT[:, :, :], ACT.Copy).then_inc(
                    sem("yR_hi"), 1)
                assert not marks

            def hi_out(first, last):
                for n in range(first, last + 1):
                    hi_piece(2 * T_OUT + n)

            hi_out(2, 3)
            act.wait_ge(sem("yR_lo"), GROUPS)
            for c in range(CT):
                wait_full(act, "lru", c)
                nc.scalar.activation(lr[:, c], bank("lru", c)[:, 0:SEQ], ACT.Tanh, scale=0.5,
                                     bias=hba[:, c:c + 1])
                nc.scalar.activation(li[:, c], bank("lru", c)[:, SEQ:2 * SEQ], ACT.Tanh, scale=0.5,
                                     bias=hbi[:, c:c + 1]).then_inc(freed("lru", c), 1)
            hi_out(4, 4)
            for c in range(CT):
                wait_read(act, "lru", c)
                ins = nc.scalar.activation(la[:, c], lr[:, c], ACT.Exp, scale=nsp[:, c:c + 1],
                                           bias=nsp[:, c:c + 1])
            ins.then_inc(sem("la_done"), 1)
            hi_out(5, 5)
            for c in range(CT):
                ins = nc.scalar.activation(lt[:, c], lr[:, c], ACT.Tanh, scale=psp[:, c:c + 1],
                                           bias=psp[:, c:c + 1])
            ins.then_inc(sem("lt_done"), 1)
            hi_out(6, 6)
            act.wait_ge(sem("om_done"), 1)
            nc.scalar.activation(lt[:, :, :], lt[:, :, :], ACT.Sqrt).then_inc(sem("om_root"), 1)
            hi_out(7, 10)
            act.wait_ge(sem("yL_f32"), 1)
            nc.scalar.activation(yL_hi[:, :, :], lt[:, :, :], ACT.Copy).then_inc(sem("yL_hi"), 1)
            hi_out(11, 2 * N_OUT + 1)
            nc.scalar.activation(scal[:, 63:64], eps_c, ACT.Sqrt)
            squares(x2, x2_sq, lambda q, t, j: wait_read(act, "out", 4 * t + j))
            norm_root(1)
            turned_hi("x2", "g2")

            def scores_out(t):
                wait_full(act, "sub", t)
                nc.scalar.activation(sub[:, :, t, :], bank("sub", t)[:, 0:2 * P].rearrange(
                    "p (a b) -> p a b", a=2), ACT.Copy).then_inc(freed("sub", t), 1)

            for t in range(N_Q):
                hi_piece(2 * (T_Q + t) + 2)
                hi_piece(2 * (T_Q + t) + 3)
                if t >= 2:
                    scores_out(t - 2)
                wait_full(act, "tile", T_Q + t)
                nc.scalar.activation(qT[t % 2][:, :], bank("tile", T_Q + t)[:, 0:SEQ], ACT.Copy).then_inc(
                    freed("tile", T_Q + t), 1)
            scores_out(N_Q - 2)
            scores_out(N_Q - 1)
            act.wait_ge(sem("x2_out"), 16)

            def u_gelu(it, b):
                act.wait_ge(mm_done, it * (2 * NR) + 2 * (T_U + b + 1))
                nc.scalar.activation(
                    actg[:, bass.ds(it * NR + b, 1), :].rearrange("p a b -> p (a b)"),
                    ps[:, b % NR, 0:SEQ], ACT.Gelu_apprx_tanh).then_inc(free[b % NR], 1)

            def u_body(it, first=False, tiles=NR):
                for b in range(tiles):
                    hi_piece(2 * (T_U + b) + 2, it)
                    hi_piece(2 * (T_U + b) + 3, it)
                    if not (first and b == 0):
                        u_gelu(it, b - 1)

            u_body(0, True)
            with act.Fori(1, U_EXP // NR) as it:
                u_body(it)
            act.wait_ge(sem("best_sub"), 1)
            nc.scalar.activation(best[:, :, :, :], best[:, :, :, :], ACT.Exp).then_inc(
                sem("best_exp"), 1)
            with act.Fori(U_EXP // NR, U_FIRST // NR) as it:
                u_body(it)
            for i in range(3):
                wait_full(act, "idx", i)
                nc.scalar.activation(idxT[:, i], bank("idx", i)[:, 0:SEQ], ACT.Copy).then_inc(
                    freed("idx", i), 1)
            with act.Fori(U_FIRST // NR, N_U // NR) as it:
                u_body(it)
            u_body(N_U // NR, tiles=N_U % NR)
            u_gelu(N_U // NR, N_U % NR - 1)

            def act_hi(k, i, it=0):
                nc.scalar.activation(a_hi[k % NR][:, :], actg[:, bass.ds(it * NR + i, 1), :].rearrange(
                    "p a b -> p (a b)"), ACT.Copy).then_inc(sem("ahi_done"), 1)

            act.wait_ge(sem("gates_used"), N_G2)
            act_hi(0, 0)
            for half in range(2):
                first, k = 2 * T_V + half * I_EARLY, half * I_EARLY
                with act.Fori(0, I_EARLY // NR) as it:
                    for b in range(NR):
                        hi_piece(first + b + 2, it, NR)
                        act_hi(k + b + 1, b + 1, it)
                for i in range(I_EARLY // NR * NR, I_EARLY):
                    hi_piece(first + i + 2)
                    if half == 1 and i == I_EARLY - 1:
                        act.wait_ge(sem("gates_used"), N_G2 + N_G4)
                    act_hi(k + i + 1, 0 if half == 0 and i == I_EARLY - 1 else i + 1)
            first, k = 2 * (T_V + I_EARLY), 2 * I_EARLY
            with act.Fori(0, N_LATE // NR) as it:
                for b in range(NR):
                    hi_piece(first + 2 * b + 2, it)
                    hi_piece(first + 2 * b + 3, it)
                    act_hi(k + b + 1, I_EARLY + b + 1, it)
            for i in range(N_LATE // NR * NR, N_LATE - 1):
                hi_piece(first + 2 * i + 2)
                hi_piece(first + 2 * i + 3)
                act_hi(k + i + 1, I_EARLY + i + 1)
            nc.scalar.activation(scal[:, 63:64], eps_c, ACT.Sqrt)
            squares(xr, xr_sq, lambda q, t, j: act.wait_ge(sem("xr_done"), q + 1))
            norm_root(2)

        @block.vector
        def _(dve):
            chain = [0]
            V = nc.vector

            def link(ins):
                chain[0] += 1
                ins.then_inc(sem("dve_chain"), 1)
                dve.wait_ge(sem("dve_chain"), chain[0])

            def mark(ins, name, value):
                ins.then_inc(sem(name), 1)
                dve.wait_ge(sem(name), value)

            def out_of(ins, name, i):
                ins.then_inc(freed(name, i), 1)
                wait_read(dve, name, i)

            def lo_piece(n, it=0, step=2 * NR):
                dve.wait_ge(hi_done, it * step + (n + 1))
                V.tensor_tensor(lo[n % NR][:, :], raw[n % NR][:, :], hi[n % NR][:, :].bitcast(F32),
                                ALU.subtract).then_inc(lo_done, 1)

            def ts(o, i, s1, s2, op0, op1=None):
                return V.tensor_scalar(o, i, s1, s2, op0, op1) if op1 is not None else \
                    V.tensor_scalar(o, i, s1, None, op0)

            def stt(o, i0, s, i1, op0, op1):
                return V.scalar_tensor_tensor(out=o, in0=i0, scalar=s, in1=i1, op0=op0, op1=op1)

            def diagonals(i):
                dve.wait_ge(sem("sd_done"), i + 1)
                link(V.reciprocal(rs, sd))
                for t in range(NT2):
                    ts(diag[t][:, :], ident[:, :], rs[:, t:t + 1], None, ALU.mult).then_inc(
                        sem("diag_done"), 1)

            def sum_squares(i):
                dve.wait_ge(sem("squares_done"), 8 * i)
                V.tensor_reduce(ssq, ssq8.rearrange("p (t j) -> p t j", t=NT2), AX_X,
                                ALU.add).then_inc(sem("ssq_done"), 1)

            def turned_lo(job, gain):
                for j in range(8):
                    dve.wait_ge(sem(f"{job}_hi"), j + 1)
                    for c in range(2):
                        ins = stt(hT_lo[:, 2 * j + c], bank(job, j)[:, c * SEQ:(c + 1) * SEQ],
                                  col(gain, 2 * j + c), hT_hi[:, 2 * j + c].bitcast(F32), ALU.mult,
                                  ALU.subtract)
                    ins.then_inc(freed(job, j), 1)

            V.memset(gneps_c, GN_EPS)
            for i in range(2):
                V.memset(mshift[i][:, 0:1], 0.0)
            V.memset(xpad[:, 0:3], 0.0)
            mark(V.memset(eps_c, EPS), "consts_done", 1)
            dve.wait_ge(sem("x_in0"), 16)
            link(V.tensor_tensor_reduce(out=x_sq[:, 0], in0=x_sb[:, 0], in1=x_sb[:, 0], scale=1.0,
                                        scalar=0.0, op0=ALU.mult, op1=ALU.add,
                                        accum_out=ssq[:, 0:1]))
            dve.wait_ge(sem("square1_done"), 1)
            dve.sem_inc(sem("ssq_done"), 1)
            dve.wait_ge(sem("ident_in"), 16)
            diagonals(0)
            dve.wait_ge(sem("cols_in"), 16)
            for dst, name in ((hw0, "w0"), (ha0, "a0"), (hba, "ba"), (hbi, "bi")):
                ts(dst, colr(name), 0.5, None, ALU.mult)
            ts(omu, colr("mu"), -1.0, 1.0, ALU.mult, ALU.add)
            link(ts(oka, colr("k_a"), -1.0, 1.0, ALU.mult, ALU.add))
            link(ts(sp[5], colr("lam"), -1.0, None, ALU.mult))
            mark(V.tensor_tensor(sp[0], colr("lam"), sp[5], ALU.max), "lam_abs", 1)
            dve.wait_ge(sem("lam_exp"), 1)
            mark(ts(sp[2], sp[1], 1.0, None, ALU.add), "lam_u", 1)
            link(ts(sp[4], sp[2], -1.0, None, ALU.add))
            link(V.tensor_tensor(sp[4], sp[1], sp[4], ALU.subtract))
            link(V.reciprocal(sp[6], sp[2]))
            link(V.tensor_tensor(sp[4], sp[4], sp[6], ALU.mult))
            dve.wait_ge(sem("lam_ln"), 1)
            link(V.tensor_tensor(sp[4], sp[4], sp[3], ALU.add))
            link(stt(sp[4], sp[5], 0.0, sp[4], ALU.max, ALU.add))
            link(ts(psp, sp[4], 4.0, None, ALU.mult))
            link(ts(nsp, sp[4], -4.0, None, ALU.mult))
            mark(V.tensor_copy(identb[:, :], ident[:, :]), "identb_done", 1)
            turned_lo("x1", "g1")

            def result(t):
                kind, c = ORDER[t]
                if kind == "xb":
                    wait_read(dve, "tile", t)
                    link(ts(xc[:, c], xpad[:, 3:3 + SEQ], col("conv_w", 3 * CT + c), col("conv_b", c),
                            ALU.mult, ALU.add))
                    link(stt(xc[:, c], xpad[:, 2:2 + SEQ], col("conv_w", 2 * CT + c), xc[:, c],
                             ALU.mult, ALU.add))
                    link(stt(xc[:, c], xpad[:, 1:1 + SEQ], col("conv_w", CT + c), xc[:, c],
                             ALU.mult, ALU.add))
                    mark(stt(xc[:, c], xpad[:, 0:SEQ], col("conv_w", c), xc[:, c],
                             ALU.mult, ALU.add), "conv_done", c + 1)
                elif kind != "gate":
                    q = SHIFTED.index(t)
                    dve.wait_ge(sem("mu_done"), q + 1)
                    out_of(stt(dest(t), bank("tile", t)[:, 0:SEQ], omu[:, MU[t]:MU[t] + 1],
                               mshift[q % 2][:, 0:SEQ], ALU.mult, ALU.add), "tile", t)

            def tile(t):
                if t:
                    result(t - 1)

            for t in range(9):
                tile(t)
                if t == 4:
                    dve.wait_ge(sem("lora_act"), 2)
                    mark(ts(lora[:, 1:3], lora[:, 1:3], 0.5, 0.5, ALU.mult, ALU.add), "lora_done", 1)
            def unit_rows(g, t):
                yd = y_tm[:, t].rearrange("p c (h i) -> p (c h) i", h=2)
                dve.wait_ge(sem("gsd_done"), 2 * g + t + 1)
                link(V.reciprocal(gsd[:, t], gsd[:, t]))
                link(V.tensor_tensor(yd, yd, gsd[:, t].unsqueeze(2).broadcast_to([P, 4, 64]),
                                     ALU.mult))

            dve.wait_ge(sem("masks_in"), 16)
            dve.wait_ge(sem("scan_in"), 16)
            for g in range(GROUPS):
                marks = list(MARKS[g])

                def m(step):
                    if step in ROOM[g]:
                        tile(marks.pop(0))

                def cg(name, c):
                    return col(name, 2 * g + c)

                R, K, Vv = (rkv[g % 2][:, i] for i in range(3))
                m(0)
                mark(V.memset(w65[:, :, 0:1], 0.0), "w65_ready", g + 1)
                for c in range(2):
                    link(ts(kk[:, c], K[:, c], cg("k_k", c), None, ALU.mult))
                mark(V.tensor_tensor(sq[:, :, :], kk[:, :, :], kk[:, :, :], ALU.mult), "sq_done", g + 1)
                wait_read(dve, "zw", g)
                link(ts(w65[:, :, 1:65], w65[:, :, 1:65], 1.0, None, ALU.add))
                mark(V.tensor_tensor_scan(P65[:, :, :].rearrange("p a b -> p (a b)"), d0scan[:, :],
                                          w65[:, :, :].rearrange("p a b -> p (a b)"),
                                          0.0, ALU.mult, ALU.add), "scan_done", g + 1)
                m(1)
                wait_read(dve, "ss", g)
                link(ts(kn[:, :], kn[:, :], 1e-12, None, ALU.max))
                link(V.reciprocal(kn[:, :], kn[:, :]))
                mark(V.tensor_copy(sq[:, :, :].rearrange("p c (k i) -> p (c k) i", i=64),
                                   kn[:, :].unsqueeze(2).broadcast_to([P, 8, 64])), "kn_done", g + 1)
                wait_read(dve, "za", g)
                link(ts(aT[:, :, :], aT[:, :, :], 0.5, 0.5, ALU.mult, ALU.add))
                for c in range(2):
                    link(ts(k2[:, c], aT[:, c], cg("k_a", c), oka[:, 2 * g + c:2 * g + c + 1],
                            ALU.mult, ALU.add))
                link(V.tensor_tensor(k2[:, :, :], k2[:, :, :], K, ALU.mult))
                dve.wait_ge(sem("ip_done"), g + 1)
                V.tensor_tensor(kt[:, :, :], k2[:, :, :], iP[:, :, :], ALU.mult)
                for c in range(2):
                    ins = stt(rk[:, c], R[:, c], cg("r_k", c), k2[:, c], ALU.mult, ALU.mult)
                mark(ins, "rk_done", g + 1)
                m(2)
                wait_full(dve, "kb", g)
                out_of(V.tensor_tensor(kk[:, :, :].rearrange("p c t -> p (c t)"),
                                       kk[:, :, :].rearrange("p c t -> p (c t)"), bank("kb", g),
                                       ALU.mult), "kb", g)
                link(V.tensor_tensor(bb[:, :, :], kk[:, :, :], aT[:, :, :], ALU.mult))
                mark(V.tensor_tensor(bt[:, :, :], bb[:, :, :], iP[:, :, :], ALU.mult), "bk_done", g + 1)
                dve.wait_ge(sem("p_done"), g + 1)
                link(stt(ARt[:, 0].rearrange("p c (k t) -> p (c k) t", t=CHUNK),
                         kk[:, :, :].rearrange("p c (k t) -> p (c k) t", t=CHUNK), -1.0,
                         P65[:, :, 0:64], ALU.mult, ALU.mult))
                mark(V.tensor_tensor(ARt[:, 1].rearrange("p c (k t) -> p (c k) t", t=CHUNK),
                                     R.rearrange("p c (k t) -> p (c k) t", t=CHUNK),
                                     P65[:, :, 1:65], ALU.mult), "ar_done", g + 1)
                V.memset(Rm[:, :, :], 0.0)
                mark(V.memset(SA[:, :, :, :], 0.0), "chain_zero", g + 1)
                m(3)
                wait_full(dve, "bsum", g)
                out_of(V.tensor_tensor(bon[:, :, :].rearrange("p c t -> p (c t)"), bank("bsum", g),
                                       Vv.rearrange("p c t -> p (c t)"), ALU.mult), "bsum", g)

                def mask_b(mask, n):
                    return mask.unsqueeze(1).broadcast_to([P, n, P])

                def masked(job, dst):
                    pb = bank(job, g).rearrange("p (t w q) -> p t w q", t=2, w=2)
                    return V.tensor_tensor(dst, pb, mU.unsqueeze(1).broadcast_to([P, 2, 2, P]), ALU.mult)

                for half in range(2):
                    for hl in (half, half + 2):
                        wait_full(dve, f"m1_{hl}", g)
                        V.tensor_tensor(TT[:, 2 * hl:2 * hl + 2, :], bank(f"m1_{hl}", g).rearrange(
                            "p (t w q) -> p t w q", t=2, w=2)[:, :, 0], mask_b(m0T, 2), ALU.mult)
                        out_of(masked(f"m1_{hl}", L1[:, 2 * hl:2 * hl + 2]), f"m1_{hl}", g)
                        wait_full(dve, f"m2_{hl}", g)
                        out_of(masked(f"m2_{hl}", L2[:, 2 * hl:2 * hl + 2]), f"m2_{hl}", g)
                    wait_full(dve, f"m3_{half}", g)
                    out_of(V.tensor_tensor(
                        Tm[:, :, :].rearrange("p (c h t) q -> p c h (t q)", c=2, h=2)[:, :, half].rearrange(
                            "p c (t q) -> p c t q", t=2),
                        bank(f"m3_{half}", g).rearrange("p (c t q) -> p c t q", c=2, t=2),
                        m0.unsqueeze(1).unsqueeze(1).broadcast_to([P, 2, 2, P]), ALU.mult),
                        f"m3_{half}", g)
                V.tensor_tensor(TT[:, :, :], TT[:, :, :], mask_b(ident[:, :], 8), ALU.add)
                mark(V.tensor_tensor(Tm[:, :, :], Tm[:, :, :], mask_b(ident[:, :], 8), ALU.add),
                     "first_inverse", g + 1)
                m(4)
                for lv in range(1, 6):
                    for half in range(2):
                        job = f"y{lv}_{half}"
                        wait_full(dve, job, g)
                        out_of(V.tensor_tensor(Ym[:, 4 * half:4 * half + 4],
                                               bank(job, g).rearrange("p (a q) -> p a q", a=4),
                                               mask_b(masks[:, 4 + lv], 4), ALU.mult), job, g)
                for c in range(4):
                    rows = slice(64 * (c % 2), 64 * (c % 2) + 64)
                    if c < 3:
                        pcm = sq[:, c % 2].rearrange("p (c q) -> p c q", c=2)
                        for ct in range(2):
                            k = 4 * ct + c
                            link(ts(pcm[:, ct], blk, P65[:, k, 64:65], None, ALU.mult))
                    wait_full(dve, f"sa{c}", g)
                    out_of(V.tensor_copy(SA[rows, c // 2].rearrange("p a b -> p (a b)"),
                                         bank(f"sa{c}", g)[rows, 0:256]), f"sa{c}", g)
                    if c < 3:
                        wait_full(dve, f"st{c}", g)
                        out_of(V.tensor_tensor(ST[(c + 1) % 2][:, :, :],
                                               bank(f"st{c}", g)[:, 0:256].rearrange(
                                                   "p (c q) -> p c q", c=2), pcm, ALU.mult),
                               f"st{c}", g)
                    if c % 2:
                        t = c // 2
                        wait_full(dve, f"yc{t}", g)
                        yp = bank(f"yc{t}", g)[:, 0:256].rearrange("p (h i) -> p h i", h=4)
                        yd = y_tm[:, t].rearrange("p c (h i) -> p (c h) i", h=2)
                        link(V.tensor_reduce(gsum[:, t], yp, AX_X, ALU.add))
                        out_of(stt(yd, gsum[:, t].unsqueeze(2).broadcast_to([P, 4, 64]), -1.0 / 64, yp,
                                   ALU.mult, ALU.add), f"yc{t}", g)
                        link(V.tensor_tensor(ysq[:, :, :], yd, yd, ALU.mult))
                        mark(V.tensor_reduce(gvar[:, t], ysq[:, :, :], AX_X, ALU.add),
                             "gvar_done", 2 * g + t + 1)
                    m(6 + c)
                    if c == 2:
                        unit_rows(g, 0)
                unit_rows(g, 1)
                dve.sem_inc(sem("y_rows_done"), 1)
                wait_full(dve, "yt", g)
                for c in range(2):
                    ins = ts(yT[:, c], bank("yt", g)[:, c * SEQ:(c + 1) * SEQ], cg("lnw", c),
                             cg("lnb", c), ALU.mult, ALU.add)
                out_of(ins, "yt", g)
                link(V.tensor_tensor(yT[:, :, :], yT[:, :, :], bon[:, :, :], ALU.add))
                mark(V.tensor_tensor(yT[:, :, :], yT[:, :, :], gT[:, :, :], ALU.mult), "y_f32", g + 1)
                dve.wait_ge(sem("yR_hi"), g + 1)
                mark(V.tensor_tensor(yR_lo[:, 2 * g:2 * g + 2, :], yT[:, :, :],
                                     yR_hi[:, 2 * g:2 * g + 2, :].bitcast(F32), ALU.subtract),
                     "yR_lo", g + 1)
            result(N_IN - 1)

            def lo_out(first, last):
                for n in range(first, last + 1):
                    lo_piece(2 * T_OUT + n)

            wait_read(dve, "lru", CT - 1)
            link(stt(li[:, :, :], li[:, :, :], 1.0, xc[:, :, :], ALU.add, ALU.mult))
            dve.wait_ge(sem("lt_done"), 1)
            dve.wait_ge(sem("la_done"), 1)
            link(V.tensor_tensor(lr[:, :, :], la[:, :, :], la[:, :, :], ALU.mult))
            mark(stt(lt[:, :, :], lr[:, :, :], 1.0, lt[:, :, :], ALU.add, ALU.mult), "om_done", 1)
            dve.wait_ge(sem("om_root"), 1)
            link(stt(li[:, :, :], li[:, :, :], 0.5, lt[:, :, :], ALU.mult, ALU.mult))
            for c in range(CT):
                link(V.tensor_tensor_scan(lr[:, c], la[:, c], li[:, c], 0.0, ALU.mult, ALU.add))
            for c in range(CT):
                wait_read(dve, "tile", ORDER.index(("gate", c)))
            mark(V.tensor_tensor(lt[:, :, :], lr[:, :, :], gate[:, :, :], ALU.mult), "yL_f32", 1)
            dve.wait_ge(sem("yL_hi"), 1)
            mark(V.tensor_tensor(yL_lo[:, :, :], lt[:, :, :], yL_hi[:, :, :].bitcast(F32),
                                 ALU.subtract), "yL_lo", 1)
            dve.wait_ge(lo_done, N_POOL)
            lo_out(N_POOL - 2 * T_OUT, 2 * N_OUT + 1)
            dve.wait_ge(sem("x2_in"), 16)
            for q, (t, j) in enumerate(SUM_ORDER):
                dve.wait_ge(mm_done, 2 * T_Q - 1 + q // 4)
                xs = x2[:, t, j * 512:(j + 1) * 512]
                V.tensor_tensor(xs, xs, bank("out", 4 * t + j), ALU.add).then_inc(
                    freed("out", 4 * t + j), 1)
            sum_squares(1)
            diagonals(1)
            turned_lo("x2", "g2")
            for n in range(2 * T_Q + 2, 2 * T_U + 2):
                lo_piece(n)

            def top16(vals, idx, src, tmp):
                return [lambda: (link(V.max(vals[:, 0:8], src)),
                                 link(V.max_index(idx[:, 0:8], vals[:, 0:8], src))),
                        lambda: (link(V.match_replace(tmp, vals[:, 0:8], src, NEG)),
                                 link(V.max(vals[:, 8:16], tmp)),
                                 link(V.max_index(idx[:, 8:16], vals[:, 8:16], tmp)))]

            def head_steps(h, t):
                steps = []
                for p in range(2):
                    steps += top16(tk_sv[:, p], tk_si[:, p], sub[:, t, 2 * h + p, :], tk_s[:, :])

                def sums():
                    link(V.tensor_copy(sif[:, t, :, h, :], tk_si[:, :, :]))
                    link(V.tensor_tensor(
                        tk_cand[:, :, :], tk_sv[:, 0].unsqueeze(2).broadcast_to([P, TOPK, TOPK]),
                        tk_sv[:, 1].unsqueeze(1).broadcast_to([P, TOPK, TOPK]), ALU.add))

                def places():
                    link(ts(tk_ab[:, 0], tk_pos[:, :], 4, None, ALU.logical_shift_right))
                    link(ts(tk_ab[:, 1], tk_pos[:, :], 15, None, ALU.bitwise_and))
                    link(V.tensor_copy(abf[:, t, :, h, :], tk_ab[:, :, :]))

                steps.append(sums)
                steps += top16(best[:, t, h], tk_pos, tk_cand[:, :, :].rearrange("p a b -> p (a b)"),
                               tk_cand2[:, :])
                steps.append(places)
                return steps

            for i in range(4):
                wait_read(dve, "sub", N_Q - 4 + i)
            steps = [step for t in range(NT2) for h in range(HEADS) for step in head_steps(h, t)]
            piece = 2 * T_U + 2
            while steps:
                lo_piece(piece)
                for _ in range(1 + piece % 2):
                    if steps:
                        steps.pop(0)()
                piece += 1

            steps = []
            for t in range(NT2):
                steps.append(lambda t=t: link(V.tensor_copy(sm[:, t], best[:, t, :, 0])))
                steps.append(lambda t=t: link(V.tensor_tensor(
                    best[:, t], best[:, t], sm[:, t].unsqueeze(2).broadcast_to([P, HEADS, TOPK]),
                    ALU.subtract)))
            steps.append(lambda: dve.sem_inc(sem("best_sub"), 1))
            for t in range(NT2):
                for p in range(2):
                    def one_hot(t=t, p=p):
                        link(V.tensor_tensor(
                            oneh[:, :, :],
                            abf[:, t, p].rearrange("p h k -> p (h k)").unsqueeze(2).broadcast_to(
                                [P, HEADS * TOPK, TOPK]),
                            iota[:, 0:TOPK].unsqueeze(1).broadcast_to([P, HEADS * TOPK, TOPK]),
                            ALU.is_equal))

                    def keys(t=t, p=p):
                        o4 = oneh[:, :, :].rearrange("p (h k) a -> p h k a", h=HEADS)
                        link(V.tensor_tensor(
                            o4, o4, sif[:, t, p].unsqueeze(2).broadcast_to([P, HEADS, TOPK, TOPK]),
                            ALU.mult))

                    def total(t=t, p=p):
                        link(V.tensor_reduce(sel[:, t, p], oneh[:, :, :], AX_X, ALU.add))

                    steps += [one_hot, keys, total]

            def softmax():
                dve.wait_ge(sem("best_exp"), 1)
                for t in range(NT2):
                    link(V.tensor_reduce(sm[:, t], best[:, t], AX_X, ALU.add))
                    link(V.reciprocal(sm[:, t], sm[:, t]))
                    link(V.tensor_tensor(
                        sel[:, t, 2].rearrange("p (h k) -> p h k", h=HEADS), best[:, t],
                        sm[:, t].unsqueeze(2).broadcast_to([P, HEADS, TOPK]), ALU.mult))
                dve.sem_inc(sem("sel_done"), 1)

            dve.wait_ge(sem("iota_in"), 16)
            last = 2 * (T_U + U_FIRST) + 2
            while steps:
                lo_piece(piece)
                if piece % 2:
                    steps.pop(0)()
                piece += 1
            assert U_EXP <= piece // 2 - T_U + 2 and piece + 4 <= last, (piece // 2 - T_U, last)
            for n in range(piece, last):
                if n == last - 4:
                    softmax()
                lo_piece(n)

            def onehots(tok, count, one_j, one_i, first_i):
                for which, dst, keys in ((1, one_j, iota[:, :]), (0, one_i, iota[:, first_i:first_i + 64])):
                    ins = V.tensor_tensor(
                        dst[:, :, :],
                        idxT[:, which, bass.ds(tok, count)].unsqueeze(2).broadcast_to(dst.shape),
                        keys.unsqueeze(1).broadcast_to(dst.shape), ALU.is_equal)
                ins.then_inc(sem("onehots_made"), 1)

            def gated(m, tok, count, b, first_i):
                dve.wait_ge(sem("gates_made"), m + 1)
                v = actg[:, first_i:first_i + 64, bass.ds(tok, count)].rearrange("p i t -> p t i")
                V.tensor_tensor(v, v, ps[:, b, 0:64 * count].rearrange("p (t i) -> p t i", t=count),
                                ALU.mult).then_inc(sem("gates_used"), 1)

            for i in range(3):
                wait_read(dve, "idx", i)
            link(V.tensor_copy(parts[:, 0], idxT[:, 2]))
            link(V.tensor_tensor(rest[:, :], idxT[:, 2], parts[:, 0], ALU.subtract))
            link(V.tensor_copy(parts[:, 1], rest[:, :]))
            link(V.tensor_tensor(parts[:, 2], rest[:, :], parts[:, 1], ALU.subtract))
            wait_read(dve, "tile", T_U + I_EARLY - 1)

            def early_onehots(it, r):
                m = it * (2 * NR) + (r - 2 * U_FIRST)
                if not (isinstance(it, int) and m < 2):
                    dve.wait_ge(sem("gates_made"), it * (2 * NR) + (r - 2 * U_FIRST - 1))
                onehots(it * (4 * NR) + (2 * r - 4 * U_FIRST), 2, oneJ[r % 2], oneI[r % 2], 0)

            def early_gated(it, r):
                gated(it * (2 * NR) + (r - 2 * U_FIRST), it * (4 * NR) + (2 * r - 4 * U_FIRST), 2,
                      5 + r % 2, 0)

            def u_body(it, first=False, tiles=NR):
                for r in range(2 * tiles):
                    early_onehots(it, r)
                    lo_piece(2 * T_U + r + 2, it)
                    if not (first and r == 0):
                        early_gated(it, r - 1)

            u_body(U_FIRST // NR, True)
            with dve.Fori(U_FIRST // NR + 1, N_U // NR) as it:
                u_body(it)
            u_body(N_U // NR, tiles=N_U % NR)
            for r in range(2 * (N_U % NR), 2 * (N_U % NR) + 2):
                early_onehots(N_U // NR, r)
                early_gated(N_U // NR, r - 1)
            early_gated(N_U // NR, r)
            for t in range(T_V - NR, T_V):
                wait_read(dve, "tile", t)
            dve.wait_ge(sem("gates_used"), N_G2)

            def act_lo(k, i, it=0):
                dve.wait_ge(sem("ahi_done"), it * NR + (k + 1))
                V.tensor_tensor(a_lo[k % NR][:, :], actg[:, bass.ds(it * NR + i, 1), :].rearrange(
                    "p a b -> p (a b)"), a_hi[k % NR][:, :].bitcast(F32), ALU.subtract).then_inc(
                    sem("alo_done"), 1)

            def late_onehots(it, b):
                if not (isinstance(it, int) and it * NR + b < 2):
                    dve.wait_ge(sem("gates_made"), it * NR + (N_G2 + b - 1))
                onehots(it * (4 * NR) + 4 * b, 4, oneJ4[b % 3], oneI4[b % 3], I_EARLY)

            def late_gated(it, b):
                gated(it * NR + (N_G2 + b), it * (4 * NR) + 4 * b, 4, LATE_BANK[b], I_EARLY)

            def early_v(it, b, half, prev=True, next_i=None):
                if half == 0:
                    late_onehots(it, b)
                lo_piece(2 * T_V + half * I_EARLY + b + 2, it, NR)
                if half == 0 and prev:
                    late_gated(it, b - 1)
                act_lo(half * I_EARLY + b + 1, b + 1 if next_i is None else next_i, it)

            act_lo(0, 0)
            for half in range(2):
                for b in range(NR):
                    early_v(0, b, half, prev=b > 0)
                with dve.Fori(1, I_EARLY // NR) as it:
                    for b in range(NR):
                        early_v(it, b, half)
                for b in range(I_EARLY % NR):
                    at_end = half == 0 and b == I_EARLY % NR - 1
                    early_v(I_EARLY // NR, b, half,
                            next_i=-(I_EARLY // NR) * NR if at_end else None)
                if half == 0:
                    late_gated(I_EARLY // NR, I_EARLY % NR - 1)
            first, k = 2 * (T_V + I_EARLY), 2 * I_EARLY
            with dve.Fori(0, N_LATE // NR) as it:
                for b in range(NR):
                    lo_piece(first + 2 * b + 2, it)
                    lo_piece(first + 2 * b + 3, it)
                    act_lo(k + b + 1, I_EARLY + b + 1, it)
            for i in range(N_LATE // NR * NR, N_LATE - 1):
                lo_piece(first + 2 * i + 2)
                lo_piece(first + 2 * i + 3)
                act_lo(k + i + 1, I_EARLY + i + 1)

            dve.wait_ge(sem("xr_in"), 16 * 8)
            dve.wait_ge(sem("gf_in"), 16 * 4)
            for q, (t, j) in enumerate(SUM_ORDER):
                dve.wait_ge(mm_done, 2 * (T_V + N_V) - 1 + q // 4)
                xs = xr[:, t, j * 512:(j + 1) * 512]
                V.tensor_tensor(xs, xs, bank("peer", 4 * (j // 2) + 2 * t + j % 2), ALU.add).then_inc(
                    sem("xr_done"), 1)
            sum_squares(2)
            dve.wait_ge(sem("sd_done"), 3)
            link(V.reciprocal(rs, sd))
            for q in range(4):
                part = slice((q % 2) * PIECE, (q % 2 + 1) * PIECE)
                stt(xr[:, q // 2, part], xr[:, q // 2, part], rs[:, q // 2:q // 2 + 1], gf[:, part],
                    ALU.mult, ALU.mult).then_inc(sem("y_done"), 1)

        @block.tensor
        def _(pe):
            def mm(o, lhsT, rhs, start, stop):
                return nc.tensor.matmul(o, lhsT, rhs, start=start, stop=stop, skip_group_check=True)

            def project(n, o, turning=None):
                half = n % 2
                for k in range(8):
                    kc = 8 * half + k
                    if turning and kc % 2 == 0:
                        wait_read(pe, turning, kc // 2)
                    wh, wl = (w[n % NR][:, k * P:(k + 1) * P] for w in (hi, lo))
                    mm(o, wh, hT_hi[:, kc], half == 0 and k == 0, False)
                    mm(o, wh, hT_lo[:, kc], False, False)
                    ins = mm(o, wl, hT_hi[:, kc], False, half == 1 and k == 7)
                ins.then_inc(mm_done, 1)

            def tile(t, turning=None, pieces=(0, 1)):
                if 0 in pieces:
                    wait_free(pe, "tile", t)
                for n in (2 * t + q for q in pieces):
                    pe.wait_ge(lo_done, n + 1)
                    project(n, bank("tile", t)[:, 0:SEQ], turning)

            def rows_out(n, act_hi, act_lo, banks, start, stop):
                for t in range(NT2):
                    ah, al = (x[:, t * P:(t + 1) * P] for x in (act_hi, act_lo))
                    for w, lhsT, s, e in ((hi[n % NR], ah, start, False), (lo[n % NR], ah, False, False),
                                          (hi[n % NR], al, False, stop)):
                        for j in range(2):
                            ins = mm(banks(t, j), lhsT, w[:, j * 512:(j + 1) * 512], s, e)
                ins.then_inc(mm_done, 1)

            def turn(i, job, rows):
                pe.wait_ge(sem("diag_done"), 2 * i + 2)
                for j in range(8):
                    wait_free(pe, job, j)
                    for c in range(2):
                        for t in range(NT2):
                            kc = 2 * j + c
                            ins = mm(bank(job, j)[:, c * SEQ + t * P:c * SEQ + (t + 1) * P],
                                     rows[:, t, kc * P:(kc + 1) * P], diag[t][:, :],
                                     c == 0 and t == 0, c == 1 and t == 1)
                    ins.then_inc(full[PLAN[job, j][0]], 1)

            turn(0, "x1", x_sb)
            for t in range(9):
                tile(t, turning=None if t else "x1")
            for name in ("masks_in", "w2_in", "a2_in", "g2_in"):
                pe.wait_ge(sem(name), 16)
            pe.wait_ge(sem("identb_done"), 1)
            pe.wait_ge(sem("lora_done"), 1)
            for g in range(GROUPS):
                marks = list(MARKS[g])

                def m(step, pieces=(0, 1)):
                    if step in ROOM[g]:
                        tile(marks[0], pieces=pieces)
                        if 1 in pieces:
                            marks.pop(0)

                def job(name):
                    wait_free(pe, name, g)
                    return bank(name, g)

                def done(ins, name):
                    ins.then_inc(full[PLAN[name, g][0]], 1)

                def chans(c):
                    return slice((2 * g + c) * P, (2 * g + c + 1) * P)

                vv = rkv[g % 2][:, 2]
                m(0)
                o = job("zw")
                for c in range(2):
                    ins = mm(o[:, c * SEQ:(c + 1) * SEQ], wa2[0:64, chans(c)], lora[0:64, 0],
                             c == 0, c == 1)
                done(ins, "zw")
                o = job("za")
                for c in range(2):
                    ins = mm(o[:, c * SEQ:(c + 1) * SEQ], wa2[64:128, chans(c)], lora[64:128, 0],
                             c == 0, c == 1)
                done(ins, "za")
                o = job("gate")
                for c in range(2):
                    for k in range(2):
                        ins = mm(o[:, c * SEQ:(c + 1) * SEQ], g2[:, k, chans(c)], lora[:, 1 + k],
                                 c == 0 and k == 0, c == 1 and k == 1)
                done(ins, "gate")
                m(1)
                o = job("ss")
                pe.wait_ge(sem("sq_done"), g + 1)
                for c in range(2):
                    for t in range(NT2):
                        q = 2 * c + t
                        ins = mm(o[:, 2 * q:2 * q + 2], sq[:, c, t * P:(t + 1) * P], blk[:, 0:P:64],
                                 q == 0, q == 3)
                done(ins, "ss")
                m(2)
                o = job("kb")
                pe.wait_ge(sem("kn_done"), g + 1)
                for q in range(4):
                    ins = mm(o[:, q * P:(q + 1) * P],
                             sq[:, q // 2, (q % 2) * P:(q % 2 + 1) * P], ident[:, :], q == 0, q == 3)
                done(ins, "kb")
                m(3)
                o = job("bsum")
                pe.wait_ge(sem("rk_done"), g + 1)
                done(mm(o, blk, rk[:, :, :].rearrange("p c t -> p (c t)"), True, True), "bsum")
                for name, src in (("vt", vv), ("bt", bt), ("kt", kt)):
                    o = job(name)
                    if name == "bt":
                        pe.wait_ge(sem("bk_done"), g + 1)
                    for c in range(2):
                        for t in range(NT2):
                            q = 2 * c + t
                            ins = nc.tensor.transpose(o[:, q * P:(q + 1) * P],
                                                      src[:, c, t * P:(t + 1) * P], ident[:, :])
                    done(ins, name)
                pe.wait_ge(sem("ar_done"), g + 1)

                def add_identity(o4):
                    return mm(o4, identb[:, :], identb[:, :].unsqueeze(1).broadcast_to(
                        [P, o4.shape[1], P]), True, False)

                def scores(name, hl, src):
                    hp, c = slice(64 * (hl % 2), 64 * (hl % 2) + 64), hl // 2
                    o = job(name)
                    for t in range(NT2):
                        tok = slice(t * P, (t + 1) * P)
                        ins = mm(o[:, t * SEQ:(t + 1) * SEQ].rearrange("p (w q) -> p w q", w=2),
                                 src[hp, c, tok], ARt[hp, :, c, tok], t == 0, t == 1)
                    done(ins, name)

                for par in range(2):
                    for hl in (par, par + 2):
                        scores(f"m1_{hl}", hl, bt)
                        scores(f"m2_{hl}", hl, kt)
                    o = job(f"m3_{par}")
                    hp = slice(64 * par, 64 * par + 64)
                    for c in range(2):
                        for t in range(NT2):
                            tok = slice(t * P, (t + 1) * P)
                            q = 2 * c + t
                            ins = mm(o[:, q * P:(q + 1) * P], ARt[hp, 0, c, tok], bt[hp, c, tok],
                                     q == 0, q == 3)
                    done(ins, f"m3_{par}")
                m(4, (0,))
                pe.wait_ge(sem("first_inverse"), g + 1)
                for lv in range(1, 6):
                    for half in range(2):
                        o = job(f"y{lv}_{half}")
                        if lv > 1:
                            wait_read(pe, f"t{lv - 1}_{half}", g)
                        add_identity(o.rearrange("p (a q) -> p a q", a=4))
                        for q in range(4):
                            p = 4 * half + q
                            ins = mm(o[:, q * P:(q + 1) * P], L1[:, p, 0], Tm[:, p], False, q == 3)
                        done(ins, f"y{lv}_{half}")
                    for half in range(2):
                        wait_read(pe, f"y{lv}_{half}", g)
                        if lv > 1:
                            wait_read(pe, f"tt{lv - 1}_{half}", g)
                        if lv < 5:
                            o = job(f"t{lv}_{half}")
                            for q in range(4):
                                p = 4 * half + q
                                ins = mm(o[:, q * P:(q + 1) * P], TT[:, p], Ym[:, p], q == 0, q == 3)
                            done(ins, f"t{lv}_{half}")
                        o = job(f"tt{lv}_{half}")
                        for q in range(4):
                            p = 4 * half + q
                            ins = mm(o[:, q * P:(q + 1) * P], Ym[:, p], TT[:, p], q == 0, q == 3)
                        done(ins, f"tt{lv}_{half}")
                m(4, (1,))
                pe.wait_ge(sem("chain_zero"), g + 1)
                for name in ("vt", "bt", "kt", "tt5_0", "tt5_1"):
                    wait_read(pe, name, g)
                for c in range(4):
                    rows, t = slice(64 * (c % 2), 64 * (c % 2) + 64), c // 2
                    tok = slice(64 * c, 64 * c + 64)
                    o = job(f"r{c}")
                    if c % 2 == 0:
                        for hl in range(4):
                            ins = mm(o[:, 64 * hl:64 * hl + 64], L2[:, 2 * hl + t, 0],
                                     Vt[:, hl // 2, t, 64 * (hl % 2):64 * (hl % 2) + 64], hl == 0, False)
                    if c:
                        wait_read(pe, f"st{c - 1}", g)
                        for ct in range(2):
                            ins = mm(o[rows, ct * P:(ct + 1) * P], ARt[:, 0, ct, tok],
                                     ST[c % 2][:, ct], False, c % 2 == 1)
                    done(ins, f"r{c}")
                    if c % 2 == 0:
                        oy = job(f"yc{t}")
                        for hl in range(4):
                            mm(oy[:, 64 * hl:64 * hl + 64], L2[:, 2 * hl + t, 1],
                               Vt[:, hl // 2, t, 64 * (hl % 2):64 * (hl % 2) + 64], hl == 0, False)
                    if c:
                        for ct in range(2):
                            mm(oy[rows, ct * P:(ct + 1) * P], ARt[:, 1, ct, tok], ST[c % 2][:, ct],
                               False, False)
                    if c < 3:
                        o = job(f"st{c}")
                        for ct in range(2):
                            mm(o[:, ct * P:(ct + 1) * P], Kt[rows, ct, t], Vt[rows, ct, t], ct == 0, False)
                        if c:
                            mm(o[:, 0:256], ident[:, :], ST[c % 2][:, :, :].rearrange("p c q -> p (c q)"),
                               False, False)
                    osa = job(f"sa{c}")
                    wait_read(pe, f"r{c}", g)
                    for hl in range(4):
                        ins = mm(osa[:, 64 * hl:64 * hl + 64], TT[:, 2 * hl + t], Rm[:, hl],
                                 hl == 0, hl == 3)
                    done(ins, f"sa{c}")
                    if c < 3:
                        m(6 + c, (0,))
                    wait_read(pe, f"sa{c}", g)
                    if c < 3:
                        for ct in range(2):
                            ins = mm(o[:, ct * P:(ct + 1) * P], Bt[rows, ct, t],
                                     SA[rows, t, 2 * ct:2 * ct + 2].rearrange("p a b -> p (a b)"),
                                     False, ct == 1)
                        done(ins, f"st{c}")
                    if c % 2:
                        for hl in range(4):
                            ins = mm(oy[:, 64 * hl:64 * hl + 64], L1[:, 2 * hl + t, 1], SA[:, t, hl],
                                     False, hl == 3)
                        done(ins, f"yc{t}")
                    m(6 + c, (1,) if c < 3 else (0, 1))
                o = job("yt")
                pe.wait_ge(sem("y_rows_done"), g + 1)
                for c in range(2):
                    for t in range(NT2):
                        q = 2 * c + t
                        ins = nc.tensor.transpose(o[:, q * P:(q + 1) * P], y_tm[:, t, c], ident[:, :])
                done(ins, "yt")

            pe.wait_ge(sem("wa_in"), 16)
            pe.wait_ge(sem("wi_in"), 16)
            pe.wait_ge(sem("conv_done"), CT)

            def lru_gates(c):
                wait_free(pe, "lru", c)
                for q in range(2):
                    ins = mm(bank("lru", c)[:, q * SEQ:(q + 1) * SEQ], wai[:, q, c], xc[:, c],
                             q == 0, q == 1)
                ins.then_inc(full[PLAN["lru", c][0]], 1)

            def out_piece(c, half):
                n = 2 * (T_OUT + c) + half
                if c == 0:
                    for t in range(NT2):
                        for j in range(2):
                            wait_free(pe, "out", 4 * t + 2 * half + j)
                yh, yl = (yR_hi, yR_lo) if c < CT else (yL_hi, yL_lo)
                if c < CT:
                    pe.wait_ge(sem("yR_lo"), c // 2 + 1)
                else:
                    pe.wait_ge(sem("yL_lo"), 1)
                pe.wait_ge(lo_done, n + 1)
                rows_out(n, yh[:, c % CT], yl[:, c % CT],
                         lambda t, j: bank("out", 4 * t + 2 * half + j), c == 0, c == N_OUT - 1)

            for c in range(4):
                lru_gates(c)
            out_piece(0, 0)
            for c in range(4, CT):
                lru_gates(c)
            out_piece(0, 1)
            for c in range(1, N_OUT):
                for half in range(2):
                    out_piece(c, half)
            turn(1, "x2", x2)


            def key_scores(t):
                wait_free(pe, "sub", t)
                pe.wait_ge(sem("keys_in"), 16)
                wait_read(pe, "tile", T_Q + t)
                for tt in range(NT2):
                    ins = mm(bank("sub", t)[:, tt * P:(tt + 1) * P], qT[t % 2][:, tt * P:(tt + 1) * P],
                             keysT[:, t], tt == 0, tt == 1)
                ins.then_inc(full[PLAN["sub", t][0]], 1)

            for t in range(N_Q):
                tile(T_Q + t, turning=None if t else "x2")
                if t:
                    key_scores(t - 1)
            key_scores(N_Q - 1)

            def u_body(it, tiles=NR, gates=False, first=False):
                for b in range(tiles):
                    pe.wait_ge(free[b], it + PLAN["tile", T_U + b][1])
                    for half in range(2):
                        n = 2 * (T_U + b) + half
                        pe.wait_ge(lo_done, it * (2 * NR) + (n + 1))
                        project(n, ps[:, b, 0:SEQ])
                        if gates:
                            early_gates(it, 2 * b + half)

            def gate_products(m_made, m_used, one_j, one_g, b):
                pe.wait_ge(sem("gates_scaled"), m_made)
                if m_used is not None:
                    pe.wait_ge(sem("gates_used"), m_used)
                count = one_j.shape[1]
                for k in range(count):
                    for q in range(3):
                        ins = mm(ps[:, b, 64 * k:64 * k + 64], one_j[:, k], one_g[:, k, q],
                                 k == 0 and q == 0, k == count - 1 and q == 2)
                ins.then_inc(sem("gates_made"), 1)

            def early_gates(it, r):
                m = it * (2 * NR) + (r - 2 * U_FIRST)
                early = isinstance(it, int) and m < 2
                gate_products(it * (2 * NR) + (r - 2 * U_FIRST + 1),
                              None if early else it * (2 * NR) + (r - 2 * U_FIRST - 1),
                              oneJ[r % 2], oneG[r % 2], 5 + r % 2)

            def late_gates(it, b):
                early = isinstance(it, int) and it * NR + b < 2
                gate_products(it * NR + (N_G2 + b + 1), None if early else it * NR + (N_G2 + b - 1),
                              oneJ4[b % 3], oneG4[b % 3], LATE_BANK[b])

            with pe.Fori(0, U_FIRST // NR) as it:
                u_body(it)
            pe.wait_ge(sem("sel_done"), 1)
            for i in range(3):
                wait_free(pe, "idx", i)
                for t in range(NT2):
                    ins = nc.tensor.transpose(bank("idx", i)[:, t * P:(t + 1) * P], sel[:, t, i],
                                              ident[:, :])
                ins.then_inc(full[PLAN["idx", i][0]], 1)
            for i in range(3):
                wait_read(pe, "idx", i)
            u_body(U_FIRST // NR, gates=True)
            with pe.Fori(U_FIRST // NR + 1, N_U // NR) as it:
                u_body(it, gates=True)
            u_body(N_U // NR, N_U % NR, gates=True)
            for r in range(2 * (N_U % NR), 2 * (N_U % NR) + 2):
                early_gates(N_U // NR, r)

            for b in range(8):
                wait_free(pe, "peer", b)

            def v_piece(n, k, half, it=0, step=2 * NR, start=False, stop=False):
                pe.wait_ge(sem("alo_done"), it * NR + (k + 1))
                pe.wait_ge(lo_done, it * step + (n + 1))
                rows_out(n, a_hi[k % NR], a_lo[k % NR], lambda t, j: ps[:, 4 * half + 2 * t + j],
                         start, stop)

            def early_v(it, b, half, start=False):
                v_piece(2 * T_V + half * I_EARLY + b, half * I_EARLY + b, half, it, NR, start)
                if half == 0:
                    late_gates(it, b)

            for half in range(2):
                for b in range(NR):
                    early_v(0, b, half, start=b == 0)
                with pe.Fori(1, I_EARLY // NR) as it:
                    for b in range(NR):
                        early_v(it, b, half)
                for b in range(I_EARLY % NR):
                    early_v(I_EARLY // NR, b, half)
                if half == 0:
                    pe.wait_ge(sem("gates_used"), N_G2 + N_G4)
            first, k = 2 * (T_V + I_EARLY), 2 * I_EARLY
            with pe.Fori(0, N_LATE // NR) as it:
                for q in range(2 * NR):
                    v_piece(first + q, k + q // 2, q % 2, it)
            for i in range(N_LATE // NR * NR, N_LATE):
                for half in range(2):
                    v_piece(first + 2 * i + half, k + i, half, stop=i == N_LATE - 1)


def _consts():
    t, s = np.arange(P)[:, None], np.arange(P)[None, :]
    eye = np.eye(P)
    same = (t // CHUNK) == (s // CHUNK)

    def pairs(lv):
        return ((t >> (lv + 1)) == (s >> (lv + 1))) & ((t >> lv) % 2 == 1) & ((s >> lv) % 2 == 0)

    blk = ((t // 64) == (s // 64)).astype(np.float32)
    masks = [blk, same & (t < s), same & (t <= s), pairs(0), pairs(0).T]
    masks += [pairs(lv) + eye for lv in range(1, 6)]
    assert len(masks) == N_MASK
    reset = np.ones((P, 8, 65))
    reset[:, :, 0] = 0
    parts = [eye, np.broadcast_to(s, (P, P))] + masks + [reset.reshape(P, -1)]
    return np.ascontiguousarray(np.concatenate([np.asarray(q, np.float32) for q in parts], 1))


def _tiles(w):
    n = w.shape[1] // P
    return np.ascontiguousarray(w.reshape(2, 8, P, n, P).transpose(3, 0, 2, 1, 4)).reshape(
        n, 2, P, PIECE)


def _columns(v):
    v = np.asarray(v).reshape(-1)
    full_v = np.zeros((-(-v.size // P)) * P, v.dtype)
    full_v[:v.size] = v
    return full_v.reshape(-1, P).T


def kernel(**inputs):
    import concourse.bacc as _bacc
    from concourse import mybir as _mybir
    from concourse.bass_utils import run_bass_kernel_spmd as _run

    i = {k: np.asarray(v) for k, v in inputs.items()}
    w_in = i["w_in"][0]
    starts = {"xb": 0, "gate": D_LRU, "r": 2 * D_LRU, "k": 3 * D_LRU, "v": 4 * D_LRU, "lora": 5 * D_LRU}
    padded = np.zeros((D, N_IN * P), w_in.dtype)
    for t, (kind, c) in enumerate(ORDER):
        first = starts[kind] + c * P
        part = w_in[:, first:first + P]
        padded[:, t * P:t * P + part.shape[1]] = part
    g2 = np.zeros((2 * P, D_LRU), w_in.dtype)
    g2[:i["rwkv_g2"].shape[1]] = i["rwkv_g2"][0]
    source = {"g1": "norm1_g", "g2": "norm2_g", "conv_w": "conv_w", "conv_b": "conv_b", "ba": "lru_ba",
              "bi": "lru_bi", "lam": "lru_lambda", "mu": "rwkv_mu", "w0": "rwkv_w0", "a0": "rwkv_a0",
              "k_k": "rwkv_k_k", "k_a": "rwkv_k_a", "r_k": "rwkv_r_k", "lnw": "rwkv_lnx_w",
              "lnb": "rwkv_lnx_b"}
    arrays = {
        "x": i["x"], "w_in": _tiles(padded), "w_out": i["w_out"][0], "wq": _tiles(i["peer_wq"][0]),
        "peer_u": _tiles(i["peer_u"][0].T), "peer_v": i["peer_v"][0].reshape(NKEY, NKEY, D),
        "keys": np.ascontiguousarray(i["peer_keys"][0].transpose(3, 0, 1, 2)).reshape(
            P, 2 * HEADS, NKEY),
        "cols": np.ascontiguousarray(np.concatenate([_columns(i[source[n]]) for n in COLS], 1)),
        "consts": _consts(), "w2": i["rwkv_w2"][0], "a2": i["rwkv_a2"][0], "g2": g2,
        "lru_wa": i["lru_wa"][0], "lru_wi": i["lru_wi"][0], "normf_g": i["normf_g"],
    }
    nc = _bacc.Bacc("TRN2", target_bir_lowering=False, num_devices=1)
    aps, fed = {}, {}
    for name, arr in arrays.items():
        arr = np.ascontiguousarray(arr)
        fed[f"in_{name}"] = arr
        aps[name] = nc.dram_tensor(f"in_{name}", arr.shape, _mybir.dt.from_np(arr.dtype),
                                   kind="ExternalInput").ap()
    out = nc.dram_tensor("out_0", (1, SEQ, D), F32, kind="ExternalOutput").ap()
    hybrid_layer_kernel(nc, aps, out)
    r = _run(nc, [fed], core_ids=[0])
    return r.results[0]["out_0"]
```
